# Optimizing a Trainium2 kernel written in Bass

```python
import math
import jax, jax.numpy as jnp
from jax import lax
import numpy as np

D_MODEL = 1024
BATCH = 1
SEQ = 128
DEPTH = 2
DEC_BATCH = 1
DEC_SEQ = 512
PAST_LEN = 128

GRID_W = 64
N_HEADS = 8
HEAD_K = 128
HEAD_V = 128
HK = N_HEADS * HEAD_K
HV = N_HEADS * HEAD_V
QKV_W = 2 * HK + HV
N_PROJ = QKV_W + HV + 4 * N_HEADS
CONV_K = 5
CHUNK = 64
POOL_WINDOWS = (2, 4, 8, 16)
N_POOL_GROUPS = 4
GC = D_MODEL // N_POOL_GROUPS
D_FF = 2816
N_EXPERTS = 8
TOP_K = 2
D_FF_E = 1408
N_DN = (DEPTH + 1) // 2
N_POOL = DEPTH // 2
N_DENSE = (DEPTH + 1) // 2
N_MOE = DEPTH // 2
ALPHA = (2.0 * DEPTH) ** 0.25
BETA_INIT = (8.0 * DEPTH) ** -0.25
EPS = 1e-6

kernel_name = 'hybrid_deltanet_pool_dit_step'

def layer_norm(x, g, b):
    xf = x.astype(jnp.float32)
    mu = xf.mean(-1, keepdims=True)
    var = jnp.square(xf - mu).mean(-1, keepdims=True)
    return ((xf - mu) * lax.rsqrt(var + EPS)).astype(x.dtype) * g + b

def l2norm(x):
    xf = x.astype(jnp.float32)
    return xf * lax.rsqrt(jnp.sum(xf * xf, axis=-1, keepdims=True) + EPS)

def short_conv(x, w):
    return lax.conv_general_dilated(
        x, w[:, None, :].astype(x.dtype), window_strides=(1,),
        padding=[(CONV_K // 2, CONV_K // 2)],
        dimension_numbers=('NWC', 'WIO', 'NWC'), feature_group_count=x.shape[-1])

def chunk_gated_delta(q, k, v, g, beta, s0):
    B, L, H, _ = q.shape
    n = L // CHUNK

    def blocks(t):
        t = t.astype(jnp.float32).reshape((B, n, CHUNK, H) + t.shape[3:])
        return jnp.moveaxis(t, 3, 1)

    q, k, v, g, beta = (blocks(t) for t in (q, k, v, g, beta))
    G = jnp.cumsum(g, axis=-1)
    idx = jnp.arange(CHUNK)
    incl = idx[:, None] >= idx[None, :]
    strict = idx[:, None] > idx[None, :]
    diff = G[..., :, None] - G[..., None, :]
    decay = jnp.where(incl, jnp.exp(jnp.where(incl, diff, 0.0)), 0.0)
    kb = k * beta[..., None]
    A = jnp.where(strict, jnp.einsum('bhnid,bhnjd->bhnij', kb, k) * decay, 0.0)
    IA = A + jnp.eye(CHUNK, dtype=jnp.float32)
    u = lax.linalg.triangular_solve(IA, v * beta[..., None], left_side=True, lower=True,
                                    unit_diagonal=True)
    w = lax.linalg.triangular_solve(IA, kb * jnp.exp(G)[..., None], left_side=True, lower=True,
                                    unit_diagonal=True)
    qk = jnp.einsum('bhnid,bhnjd->bhnij', q, k) * decay
    q_dec = q * jnp.exp(G)[..., None]
    k_dec = k * jnp.exp(G[..., -1:] - G)[..., None]
    g_last = jnp.exp(G[..., -1])
    xs = tuple(jnp.moveaxis(t, 2, 0) for t in (q_dec, k_dec, u, w, qk, g_last))

    def step(S, xc):
        qd, kd, uc, wc, qkc, gl = xc
        v_new = uc - jnp.einsum('bhcd,bhde->bhce', wc, S)
        o = jnp.einsum('bhcd,bhde->bhce', qd, S) + jnp.einsum('bhij,bhje->bhie', qkc, v_new)
        S = S * gl[..., None, None] + jnp.einsum('bhcd,bhce->bhde', kd, v_new)
        return S, o

    S, o = lax.scan(step, s0.astype(jnp.float32), xs)
    o = jnp.transpose(o, (1, 0, 3, 2, 4)).reshape(B, L, H, -1)
    return o, S

def deltanet_mixer(h, w_in, conv_w, a_log, dt_bias, norm_g, w_out, s0):
    B, L, _ = h.shape
    proj = h @ w_in
    qkv, z, ab = jnp.split(proj, [QKV_W, QKV_W + HV], axis=-1)
    qkv = jax.nn.silu(short_conv(qkv, conv_w))
    q, k, v = jnp.split(qkv, [HK, 2 * HK], axis=-1)
    q = l2norm(q.reshape(B, L, N_HEADS, HEAD_K)) * HEAD_K ** -0.5
    k = l2norm(k.reshape(B, L, N_HEADS, HEAD_K))
    v = v.reshape(B, L, N_HEADS, HEAD_V)
    ab = ab.astype(jnp.float32).reshape(B, L, 2, 2, N_HEADS)
    g = -jnp.exp(a_log.astype(jnp.float32)) * jax.nn.softplus(ab[:, :, 0] + dt_bias.astype(jnp.float32))
    beta = jax.nn.sigmoid(ab[:, :, 1])
    o_f, s_f = chunk_gated_delta(q, k, v, g[:, :, 0], beta[:, :, 0], s0[:, 0])
    flip = lambda t: jnp.flip(t, axis=1)
    o_b, s_b = chunk_gated_delta(flip(q), flip(k), flip(v), flip(g[:, :, 1]), flip(beta[:, :, 1]),
                                 s0[:, 1])
    o = o_f + flip(o_b)
    o = o * lax.rsqrt(jnp.mean(o * o, axis=-1, keepdims=True) + EPS) * norm_g.astype(jnp.float32)
    o = o * jax.nn.silu(z.astype(jnp.float32).reshape(B, L, N_HEADS, HEAD_V))
    y = o.astype(h.dtype).reshape(B, L, HV) @ w_out
    return y, jnp.stack([s_f, s_b], axis=1)

def pool_mixer(h, w_grp, b_grp, scale, rows):
    B, L, D = h.shape
    xs = h.astype(jnp.float32)
    if rows is not None:
        xs = xs.reshape(B * rows, GRID_W, D)
    Lr = xs.shape[1]
    cs = jnp.concatenate([jnp.zeros_like(xs[:, :1]), jnp.cumsum(xs, axis=1)], axis=1)
    pos = jnp.arange(Lr)
    parts = []
    for gi, win in enumerate(POOL_WINDOWS):
        sl = slice(gi * GC, (gi + 1) * GC)
        lo = jnp.clip(pos - win // 2, 0, Lr)
        hi = jnp.clip(pos - win // 2 + win, 0, Lr)
        cnt = (hi - lo).astype(jnp.float32)[:, None]
        csg = cs[..., sl]
        parts.append((jnp.take(csg, hi, axis=1) - jnp.take(csg, lo, axis=1)) / cnt - xs[..., sl])
    pooled = jnp.stack(parts, axis=-2).reshape(B, L, N_POOL_GROUPS, GC).astype(h.dtype)
    y = jnp.einsum('blgc,gce->blge', pooled, w_grp).reshape(B, L, D) + b_grp
    return y * scale

def swiglu(h, w_gu, w_down):
    gate, up = jnp.split(h @ w_gu, 2, axis=-1)
    return (jax.nn.silu(gate) * up) @ w_down

def moe_swiglu(h, router_w, w_gu, w_down):
    probs = jax.nn.softmax((h @ router_w).astype(jnp.float32), axis=-1)
    top_p, top_i = lax.top_k(probs, TOP_K)
    top_p = top_p / jnp.sum(top_p, axis=-1, keepdims=True)
    gates = jnp.sum(jax.nn.one_hot(top_i, N_EXPERTS, dtype=jnp.float32) * top_p[..., None],
                    axis=-2).astype(h.dtype)
    y = jnp.zeros_like(h)
    for e in range(N_EXPERTS):
        y = y + gates[..., e:e + 1] * swiglu(h, w_gu[e], w_down[e])
    return y

def run_trunk(x, cond, dn_state0, rows, p):
    states = []
    for i in range(DEPTH):
        j = i // 2
        mod = jax.nn.silu(cond) @ p['ada_w'][i] + p['ada_b'][i]
        sh1, sc1, g1, sh2, sc2, g2 = jnp.split(mod[:, None, :], 6, axis=-1)
        h = x * (1.0 + sc1) + sh1
        if i % 2 == 0:
            y, s = deltanet_mixer(h, p['dn_w_in'][j], p['dn_conv'][j], p['dn_a_log'][j],
                                  p['dn_dt_bias'][j], p['dn_norm_g'][j], p['dn_w_out'][j],
                                  dn_state0[:, j])
            states.append(s)
        else:
            y = pool_mixer(h, p['pool_w'][j], p['pool_b'][j], p['pool_scale'][j], rows)
        x = layer_norm(ALPHA * x + g1 * y, p['ln_g'][i, 0], p['ln_b'][i, 0])
        h = x * (1.0 + sc2) + sh2
        if i % 2 == 0:
            y = swiglu(h, p['ffn_w_gu'][j], p['ffn_w_down'][j])
        else:
            y = moe_swiglu(h, p['moe_router'][j], p['moe_w_gu'][j], p['moe_w_down'][j])
        x = layer_norm(ALPHA * x + g2 * y, p['ln_g'][i, 1], p['ln_b'][i, 1])
    return x, states

def setup_inputs(seed: int = 0) -> dict:
    key = jax.random.key(seed)
    ks = jax.random.split(key, 32)
    f32 = jnp.float32

    def nrm(k, shape, s):
        return jax.random.normal(k, shape, f32) * s

    dt = jnp.exp(jax.random.uniform(ks[12], (N_DN, 2, N_HEADS), f32, math.log(1e-3), math.log(1e-1)))
    return {
        'x_prompt': nrm(ks[0], (BATCH, SEQ, D_MODEL), 1.0),
        'x_sample': nrm(ks[1], (DEC_BATCH, DEC_SEQ, D_MODEL), 1.0),
        'state_dn': nrm(ks[2], (DEC_BATCH, N_DN, 2, N_HEADS, HEAD_K, HEAD_V), 0.1),
        'c': nrm(ks[3], (DEC_BATCH, D_MODEL), 1.0),
        'c_ctx': nrm(ks[4], (D_MODEL,), 1.0),
        'ada_w': nrm(ks[5], (DEPTH, D_MODEL, 6 * D_MODEL), 0.5 * D_MODEL ** -0.5),
        'ada_b': nrm(ks[6], (DEPTH, 6 * D_MODEL), 0.02),
        'ln_g': 1.0 + nrm(ks[7], (DEPTH, 2, D_MODEL), 0.02),
        'ln_b': nrm(ks[8], (DEPTH, 2, D_MODEL), 0.02),
        'dn_w_in': nrm(ks[9], (N_DN, D_MODEL, N_PROJ), D_MODEL ** -0.5),
        'dn_conv': nrm(ks[10], (N_DN, CONV_K, QKV_W), CONV_K ** -0.5),
        'dn_a_log': jnp.log(jax.random.uniform(ks[11], (N_DN, 2, N_HEADS), f32, 1.0, 16.0)),
        'dn_dt_bias': dt + jnp.log(-jnp.expm1(-dt)),
        'dn_norm_g': 1.0 + nrm(ks[13], (N_DN, HEAD_V), 0.02),
        'dn_w_out': nrm(ks[14], (N_DN, HV, D_MODEL), HV ** -0.5 * BETA_INIT),
        'pool_w': nrm(ks[15], (N_POOL, N_POOL_GROUPS, GC, GC), GC ** -0.5 * BETA_INIT),
        'pool_b': nrm(ks[16], (N_POOL, D_MODEL), 0.02),
        'pool_scale': 1.0 + nrm(ks[17], (N_POOL, D_MODEL), 0.02),
        'ffn_w_gu': nrm(ks[18], (N_DENSE, D_MODEL, 2 * D_FF), D_MODEL ** -0.5),
        'ffn_w_down': nrm(ks[19], (N_DENSE, D_FF, D_MODEL), D_FF ** -0.5 * BETA_INIT),
        'moe_router': nrm(ks[20], (N_MOE, D_MODEL, N_EXPERTS), D_MODEL ** -0.5),
        'moe_w_gu': nrm(ks[21], (N_MOE, N_EXPERTS, D_MODEL, 2 * D_FF_E), D_MODEL ** -0.5),
        'moe_w_down': nrm(ks[22], (N_MOE, N_EXPERTS, D_FF_E, D_MODEL), D_FF_E ** -0.5 * BETA_INIT),
    }

def reference(x_prompt, x_sample, state_dn, c, c_ctx, ada_w, ada_b, ln_g, ln_b, dn_w_in, dn_conv,
              dn_a_log, dn_dt_bias, dn_norm_g, dn_w_out, pool_w, pool_b, pool_scale, ffn_w_gu,
              ffn_w_down, moe_router, moe_w_gu, moe_w_down):
    p = dict(ada_w=ada_w, ada_b=ada_b, ln_g=ln_g, ln_b=ln_b, dn_w_in=dn_w_in, dn_conv=dn_conv,
             dn_a_log=dn_a_log, dn_dt_bias=dn_dt_bias, dn_norm_g=dn_norm_g, dn_w_out=dn_w_out,
             pool_w=pool_w, pool_b=pool_b, pool_scale=pool_scale, ffn_w_gu=ffn_w_gu,
             ffn_w_down=ffn_w_down, moe_router=moe_router, moe_w_gu=moe_w_gu,
             moe_w_down=moe_w_down)
    ctx_state0 = jnp.zeros((x_prompt.shape[0], N_DN, 2, N_HEADS, HEAD_K, HEAD_V), jnp.float32)
    y_prompt, ctx_states = run_trunk(x_prompt, c_ctx[None, :], ctx_state0, None, p)
    new_state_dn = jnp.stack(ctx_states, axis=1).astype(x_prompt.dtype)
    rows = x_sample.shape[1] // GRID_W
    y_sample, _ = run_trunk(x_sample, c, state_dn, rows, p)
    return (y_prompt, y_sample, new_state_dn)


_drawn_inputs = setup_inputs


def setup_inputs(seed=0):
    import zlib

    import numpy as np

    out = dict(_drawn_inputs(seed))
    spreads = {}
    factors = {'state_dn': 8.0, 'dn_norm_g': 8.0, 'pool_b': 8.0, 'pool_scale': 8.0}
    for name, (base, spread) in spreads.items():
        noise = np.random.default_rng([zlib.crc32(name.encode()), seed]).standard_normal(out[name].shape)
        drawn = base * np.exp(spread * noise) if base else spread * noise
        out[name] = __import__('jax').numpy.asarray(drawn.astype(out[name].dtype))
    for name, factor in factors.items():
        out[name] = (out[name] * factor).astype(out[name].dtype)
    return out
```

```python
from contextlib import ExitStack

import numpy as np

import concourse.bass as bass
from concourse import mybir

F32 = mybir.dt.float32
ALU = mybir.AluOpType
ACT = mybir.ActivationFunctionType
AX = mybir.AxisListType

P = 128
D = 1024
KD = D // P
T = 5
NT = T * P
H = 8
FE = 1408
KF = FE // P
GRID_W = 64
WINDOWS = (2, 4, 8, 16)
ALPHA = (2.0 * 2) ** 0.25
EPS = 1e-6
RING = 3
LEVELS = 7

IDENT, LE, GE, LT, GT, ONES = range(6)
LEVEL = 6
POOL = LEVEL + 2 * LEVELS
N_CONST = POOL + 2 * len(WINDOWS)


def shape_constants():
    r = np.arange(P)[:, None]
    c = np.arange(P)[None, :]
    m = np.zeros((P, N_CONST, P), np.float32)
    m[:, IDENT] = r == c
    m[:, LE] = r <= c
    m[:, GE] = r >= c
    m[:, LT] = r < c
    m[:, GT] = r > c
    m[:, ONES] = 1.0
    for lv in range(LEVELS):
        s = 1 << lv
        off = (r // (2 * s) == c // (2 * s)) & (r % (2 * s) >= s) & (c % (2 * s) < s)
        m[:, LEVEL + lv] = off
        m[:, LEVEL + LEVELS + lv] = off.T
    for kind, seg in enumerate((P, GRID_W)):
        for g, w in enumerate(WINDOWS):
            for t in range(P):
                base = t // seg * seg
                lo, hi = max(t - w // 2, base), min(t - w // 2 + w, base + seg)
                m[lo:hi, POOL + kind * len(WINDOWS) + g, t] = 1.0 / (hi - lo)
                m[t, POOL + kind * len(WINDOWS) + g, t] -= 1.0
    return m


class Ring:

    def __init__(self):
        self.base = 0

    def slot(self, k):
        return (self.base + k) % RING

    def loaded(self, k, i=0, per=0):
        return 32 * ((self.base + k) // RING + 1) + i * (32 * (per // RING))

    def freed(self, k, i=0, per=0):
        return self.base + k + 1 + i * per


def backbone(nc, A, out_prompt, out_sample, out_state, mod_dram):
    with ExitStack() as ctx:
        def sb(name, shape, dt=F32):
            return ctx.enter_context(nc.sbuf_tensor(name, shape, dt))

        def sem(name):
            return ctx.enter_context(nc.semaphore(name))

        cm = sb("cm", [P, N_CONST, P])
        x = sb("x", [P, T, D])
        xT = sb("xT", [P, KD, NT])
        acc = sb("acc", [P, T, D])
        big = sb("big", [P, KF * NT])
        wring = sb("wring", [P, RING, 4, 512])
        rows = sb("rows", [P, 4, D])
        scratch = sb("scratch", [P, 11556])
        modcol = sb("modcol", [P, 2, 96])
        scp1 = sb("scp1", [P, 2, KD])
        modcol_in = sb("modcol_in", [96, P])
        condr = sb("condr", [16, P])
        cs = sb("cs", [P, 16])
        convr = sb("convr", [120, P])
        convw = sb("convw", [P, 5, 24])
        wab = sb("wab", [P, KD, 32])
        rw = sb("rw", [P, KD, 8])
        dtb = sb("dtb", [P, 16])
        alog = sb("alog", [P, 16])
        ngb = sb("ngb", [P, P])
        gates5 = sb("gates5", [P, 12, T, 16])
        ss = sb("ss", [P, 8, T])
        mhalf = sb("mhalf", [P, T])
        lnst = sb("lnst", [P, T, 2, 6])
        lnmv = sb("lnmv", [P, T, 2])
        rstd = sb("rstd", [P, 2, T])
        gate_e = sb("gate_e", [P, 2, T, 8])
        rt = sb("rt", [P, 10, T, 8])
        state = sb("state", [P, 2, P])
        state_new = sb("state_new", [P, 2, P])
        vnew = sb("vnew", [P, 2, P])

        def carve(buf, off, n, **dims):
            ap = buf[:, off:off + n]
            if not dims:
                return ap
            names = " ".join(dims)
            return ap.rearrange(f"p ({names}) -> p {names}", **dims)

        early = xT[0:2, :, :].rearrange("p k t -> p (k t)")
        brow = early[:, 0:1536].rearrange("p (b n) -> p b n", b=3)
        mrow = early[:, 1536:3072].rearrange("p (b n) -> p b n", b=3)
        oT = carve(big, 0, H * NT, h=H, t=NT)
        hT = carve(big, 0, KF * NT, c=KF, t=NT)
        vn_t = carve(big, H * NT, 3 * NT, c=3, t=NT)
        cbuf = carve(scratch, 0, 3 * 648, c=3, t=648)
        offd = carve(scratch, 0, 2 * NT, d=2, t=NT)
        cv = carve(scratch, 1944, 3 * 644, c=3, t=644)
        vt = carve(scratch, 1944, 2 * NT, d=2, t=NT)
        sq = carve(scratch, 3876, 2 * NT, d=2, t=NT)
        inv = sq
        invT = carve(scratch, 5156, 2 * NT, d=2, t=NT)
        qkT = carve(scratch, 6436, 2 * NT, d=2, t=NT)
        kk = carve(scratch, 7716, NT)
        qk = carve(scratch, 8356, NT)
        oacc, og = kk, qk
        gm = carve(scratch, 8996, 4 * NT, j=4, t=NT)
        R = gm
        hsil = carve(scratch, 0, 3 * 256, b=3, t=256)
        hbuf = carve(scratch, 768, T * 256, b=T, t=256)
        lnt = carve(scratch, 4096, T * D, t=T, d=D)
        rowsf = rows[:, :, :].rearrange("p a b -> p (a b)")
        ex = rowsf[:, 0:4 * NT].rearrange("p (j t) -> p j t", j=4)

        def per_tile(ap):
            return ap.rearrange("p (t c) -> p t c", t=T)

        qTk = rowsf[:, 4 * NT:6 * NT].rearrange("p (j t) -> p j t", j=2)
        modc = [modcol[:, 0, :], modcol[:, 1, :]]

        def u_all(d):
            return vt[:, d, :]

        def wT(d):
            return inv[:, d, :]

        def kdec(d):
            return ex[:, 2 * d, :]

        PP = [ctx.enter_context(nc.psum_tensor(f"pp{i}", [P, 1024], F32)) for i in range(4)]

        def bank(i):
            return PP[i // 2][:, 512 * (i % 2):512 * (i % 2) + 512]

        names = """consts_in x_in small_in cond_ps cond_ready mod_ps mod_row conv_ps conv_cols
            slot_free modcol_ps modcol_ready scp1_ready xt_ps xt_ready z_ps z_ready ab_ps gate_step
            gate_act cum_ps q_k_v_ps conv_in conv_step silu_done tok_ps sq_done v_ready ss_done rn_step
            qkn head_ps qkT_ready gram_ps gram_sb gm_ready decay_ps ex_ready a_step w_step inv_init
            off_ready vt_ps vt_sb upd_x_ps upd_y_ps inv_upd r_ready kdec_ready u_ps wt_ps u_sb wt_sb
            s_read_ps s_add_ps vn_ready o_upd s_upd sp_ready state_in state_out sqo_done sso_done
            rno_step og_step ogT_ps oT_ready res_ps res_step ln_step ln_rstd rows_in poolrows_in
            hp_step poolT_ps poolT_sb pool_ps pool_step logit_ps route_step route_act final_out cbuf_zero
            pool_const gate_arg""".split()
        S = {n: sem(n) for n in names}
        slot_loaded = [sem(f"slot_loaded{i}") for i in range(RING)]
        bias_in = [sem(f"bias_in{i}") for i in range(3)]
        mod_out = [sem(f"mod_out{i}") for i in range(3)]
        modcol_in_s = sem("modcol_rows_in")
        F = [{n: sem(f"{n}{l}") for n in ("gu_ps", "sil_done", "h_done", "hT_ps", "hT_ready", "down_ps",
                                          "acc_done")} for l in range(2)]

        ident = cm[:, IDENT, :]
        block = ctx.enter_context(nc.Block())

        c5 = lambda ap: ap.rearrange("p (a b) -> p a b", b=1) if False else ap

        def col_bc(ap):
            return ap.to_broadcast([P, T, P])

        def mat_bc(m):
            return cm[:, m:m + 1, :].to_broadcast([P, T, P])

        AB0, SPA, SPB, G_, BETA, EG, EK, EL, BG, TMP, NA, T2 = range(12)

        def gcol(which, d, hd):
            return gates5[:, which, :, bass.ds(hd + 8 * d, 1)]

        LN_STEPS = 8

        @block.sync
        def _(sp):
            ring = Ring()
            sp.dma_start(cm[:, :, :], A["consts"]).then_inc(S["consts_in"], 16)
            sp.dma_start(condr[0:8, :], A["c_ctx"].rearrange("(k p) -> k p", p=P)).then_inc(S["small_in"], 16)
            sp.dma_start(condr[8:16, :], A["c"][0].rearrange("(k p) -> k p", p=P)).then_inc(S["small_in"], 16)
            sp.dma_start(convr[:, :], A["dn_conv"][0].rearrange("j (c p) -> (j c) p", p=P)).then_inc(S["small_in"], 16)

            def fill(k, parts, i=0, per=0):
                sp.wait_ge(S["slot_free"], ring.freed(k, i, per))
                for dst, src in parts(ring.slot(k)):
                    sp.dma_start(dst, src).then_inc(slot_loaded[ring.slot(k)], 16)

            def cols512(w, k0, nk, c0):
                wv = w.rearrange("(k p) n -> p k n", p=P)
                a = (nk + 1) // 2

                def parts(s):
                    return [(wring[:, s, 0:a, :], wv[:, k0:k0 + a, bass.ds(c0, 512)]),
                            (wring[:, s, a:nk, :], wv[:, k0 + a:k0 + nk, bass.ds(c0, 512)])]
                return parts

            for layer in range(2):
                with sp.Fori(0, 4) as i:
                    for k in range(6):
                        fill(k, cols512(A["ada_w"][layer], 4 * (k % 2), 4, i * 1536 + 512 * (k // 2)), i, 6)
                ring.base += 24
                if layer == 0:
                    sp.dma_start(x[:, 0, :], A["x_prompt"][0]).then_inc(S["x_in"], 16)
                    sp.dma_start(x[:, 1:T, :], A["x_sample"][0].rearrange("(t p) d -> p t d", p=P)).then_inc(S["x_in"], 16)
                    sp.dma_start(wab[:, :, :], A["dn_w_in"][0].rearrange("(k p) n -> p k n", p=P)[:, :, 4096:4128]).then_inc(S["small_in"], 16)
                    sp.dma_start(rw[:, :, :], A["moe_router"][0].rearrange("(k p) n -> p k n", p=P)).then_inc(S["small_in"], 16)
                    sp.dma_start(dtb[:, :], A["dn_dt_bias"][0].rearrange("d h -> (d h)").partition_broadcast(P)).then_inc(S["small_in"], 16)
                    sp.dma_start(alog[:, :], A["dn_a_log"][0].rearrange("d h -> (d h)").partition_broadcast(P)).then_inc(S["small_in"], 16)
                    sp.dma_start(ngb[:, :], A["dn_norm_g"][0].partition_broadcast(P)).then_inc(S["small_in"], 16)
            for k in range(4):
                fill(k, cols512(A["dn_w_in"][0], 4 * (k % 2), 4, 3072 + 512 * (k // 2)))
            ring.base += 4
            w_in = A["dn_w_in"][0].rearrange("(k p) n -> p k n", p=P)
            with sp.Fori(0, H) as hd:
                for c in range(3):
                    def parts(s, c=c):
                        dst = wring[:, s, 0:2, :].rearrange("p a (b n) -> p (a b) n", n=P)
                        return [(dst[:, 4 * a:4 * a + 4, :], w_in[:, 4 * a:4 * a + 4, bass.ds(hd * P + D * c, P)])
                                for a in range(2)]
                    fill(c, parts, hd, 3)
            ring.base += 3 * H
            for k in range(4):
                fill(k, cols512(A["dn_w_out"][0], 4 * (k % 2), 4, 512 * (k // 2)))
            ring.base += 4

            def expert_fills(e, gate_w, down_w, up_off):
                gv = gate_w.rearrange("(k p) n -> p k n", p=P)
                for j in range(6):
                    w = 256 if j < 5 else 128
                    for a in range(2):
                        def parts(s, j=j, w=w, a=a):
                            return [(wring[:, s, 0:4, w * u:w * u + w],
                                     gv[:, 4 * a:4 * a + 4, bass.ds(up_off[u] + 256 * j, w)]) for u in range(2)]
                        fill(2 * j + a, parts, e, 18)
                for n in range(2):
                    for a in range(3):
                        nk = 4 if a < 2 else 3
                        fill(12 + 3 * n + a, cols512(down_w, 4 * a, nk, 512 * n), e, 18)

            wd = A["ffn_w_down"][0].rearrange("(e f) d -> e f d", f=FE)
            with sp.Fori(0, 2) as e:
                expert_fills(e, A["ffn_w_gu"][0], wd[bass.ds(e, 1)].rearrange("a f d -> (a f) d"),
                             (e * FE, e * FE + 2 * FE))
            ring.base += 36
            wp = A["pool_w"][0].rearrange("g (k p) n -> p (g k) n", p=P)

            def parts(s):
                dst = wring[:, s, :, :].rearrange("p a (b n) -> p (a b) n", n=256)
                return [(dst[:, 4 * a:4 * a + 4, :], wp[:, 4 * a:4 * a + 4, :]) for a in range(2)]
            fill(0, parts)
            ring.base += 1
            with sp.Fori(0, 8) as e:
                expert_fills(e, A["moe_w_gu"][0][bass.ds(e, 1)].rearrange("a k n -> (a k) n"),
                             A["moe_w_down"][0][bass.ds(e, 1)].rearrange("a f d -> (a f) d"), (0, FE))
            sp.wait_ge(S["ln_step"], 4 * T * LN_STEPS)
            sp.dma_start(out_prompt[0], x[:, 0, :]).then_inc(S["final_out"], 16)
            sp.dma_start(out_sample[0].rearrange("(t p) d -> p t d", p=P), x[:, 1:T, :]).then_inc(S["final_out"], 16)
            sp.wait_ge(S["final_out"], 32)

        @block.tensor
        def _(pe):
            ring = Ring()
            pe.sem_inc(S["slot_free"], RING)
            xt_n = [0]

            def slot(k, i=0, per=0):
                pe.wait_ge(slot_loaded[ring.slot(k)], ring.loaded(k, i, per))
                return ring.slot(k)

            def gemm5(k, nk, lhs, c0, first, last, done, i=0, per=0, n=512, free=None):
                s = slot(k, i, per)
                for t in range(T):
                    if first and free is not None:
                        free(t)
                    for kk_ in range(nk):
                        mm = pe.matmul(bank(t)[:, 0:n], lhs(c0 + kk_, t), wring[:, s, kk_, 0:n],
                                       start=(first and kk_ == 0), stop=(last and kk_ == nk - 1))
                    if last:
                        mm.then_inc(done, 1)
                if not last:
                    mm.then_inc(S["slot_free"], 1)

            pe.wait_ge(S["consts_in"], 16)
            pe.wait_ge(S["small_in"], 48)
            pe.transpose(PP[3][:, 0:16], condr[:, :], ident[0:16, 0:16]).then_inc(S["cond_ps"], 1)
            pe.transpose(PP[3][:, 512:632], convr[:, :], ident[0:120, 0:120]).then_inc(S["conv_ps"], 1)
            pe.wait_ge(S["cond_ready"], 1)
            csv = cs[:, :].rearrange("p (r k) -> p k r", r=2)
            for layer in range(2):
                with pe.Fori(0, 4) as i:
                    for b in range(3):
                        pe.wait_ge(S["mod_row"], i * 3 + (12 * layer + b + 1))
                        for a in range(2):
                            s = slot(2 * b + a, i, 6)
                            for k in range(4):
                                mm = pe.matmul(bank(b)[0:2, :], csv[:, 4 * a + k, :], wring[:, s, k, :],
                                               start=(a == 0 and k == 0), stop=(a == 1 and k == 3))
                            mm.then_inc(S["slot_free" if a == 0 else "mod_ps"], 1)
                        pe.wait_ge(S["mod_ps"], i * 3 + (12 * layer + b + 1))
                        pe.sem_inc(S["slot_free"], 1)
                ring.base += 24
            for layer in range(2):
                pe.wait_ge(modcol_in_s, 16 * (layer + 1))
                if layer:
                    pe.wait_ge(S["modcol_ready"], 1)
                else:
                    pe.wait_ge(S["conv_cols"], 1)
                pe.transpose(PP[3][:, 0:96], modcol_in[:, :], ident[0:96, 0:96]).then_inc(S["modcol_ps"], 1)
                if layer == 0:
                    xt_first = None

                def transpose_x(ln_done):
                    for t in range(T):
                        if ln_done is None:
                            pe.wait_ge(S["x_in"], 32)
                        else:
                            pe.wait_ge(S["ln_step"], (ln_done * T + t + 1) * LN_STEPS)
                        if t >= 4:
                            pe.wait_ge(S["xt_ready"], 2 * (xt_n[0] * T + t - 3))
                        for k in range(KD):
                            mm = pe.transpose(PP[t % 4][:, k * P:(k + 1) * P], x[:, t, k * P:(k + 1) * P], ident)
                        mm.then_inc(S["xt_ps"], 1)
                    xt_n[0] += 1
                if layer == 1:
                    break

            pe.wait_ge(S["modcol_ready"], 2)
            transpose_x(None)

            def lhs_x(k, t):
                return xT[:, k, t * P:(t + 1) * P]

            def lhs_o(k, t):
                return oT[:, k, t * P:(t + 1) * P]

            pe.wait_ge(S["xt_ready"], 2 * T)
            pe.wait_ge(S["small_in"], 16 * 8)
            for t in range(T):
                for k in range(KD):
                    mm = pe.matmul(bank(6)[:, 32 * t:32 * t + 32], lhs_x(k, t), wab[:, k, :],
                                   start=(k == 0), stop=(k == KD - 1))
            mm.then_inc(S["ab_ps"], 1)
            for n in range(2):
                for a in range(2):
                    gemm5(2 * n + a, 4, lhs_x, 4 * a, a == 0, a == 1, S["z_ps"],
                          free=(lambda t: pe.wait_ge(S["z_ready"], t + 1)) if n else None)
                pe.wait_ge(S["z_ps"], T * (n + 1))
                pe.sem_inc(S["slot_free"], 1)
            ring.base += 4
            pe.wait_ge(S["gate_step"], 8)
            gf, gb = gates5[:, G_, :, 0:8], gates5[:, G_, :, 8:16]
            cum = bank(7)[:, 0:240].rearrange("p (s t h) -> p s t h", s=3, h=16)
            for kind, (mf, mb) in enumerate(((LE, GE), (GT, LT), (ONES, ONES))):
                pe.matmul(cum[:, kind, :, 0:8], cm[:, mf, :], gf, start=True, stop=True)
                mm = pe.matmul(cum[:, kind, :, 8:16], cm[:, mb, :], gb, start=True, stop=True)
            mm.then_inc(S["cum_ps"], 1)

            def tiles(j):
                return slice(j * P, (j + 1) * P)

            def mm5(dst, lhs, rhs, sig, n):
                for t in range(T):
                    mm = pe.matmul(dst[:, tiles(t)], lhs(t), rhs(t), start=True, stop=True)
                mm.then_inc(S[sig], 1)

            with pe.Fori(0, H) as hd:
                pe.wait_ge(S["oT_ready"], hd)
                for c in range(3):
                    s = slot(c, hd, 3)
                    w = wring[:, s, 0:2, :].rearrange("p a (b n) -> p (a b) n", n=P)
                    for lo, hi in ((0, 512), (512, NT)):
                        for k in range(KD):
                            mm = pe.matmul(PP[c][:, lo:hi], w[:, k, :], xT[:, k, lo:hi],
                                           start=(k == 0), stop=(k == KD - 1))
                    mm.then_inc(S["q_k_v_ps"], 1)
                    pe.wait_ge(S["q_k_v_ps"], hd * 3 + (c + 1))
                    pe.sem_inc(S["slot_free"], 1)
                for c in range(3):
                    pe.wait_ge(S["silu_done"], hd * 3 + (c + 1))
                    for t in range(T):
                        o = 0 if t == 0 else 132 + (t - 1) * P
                        mm = pe.transpose(PP[c][:, tiles(t)], cv[:, c, o:o + P], ident)
                    mm.then_inc(S["tok_ps"], 1)
                for c in range(2):
                    pe.wait_ge(S["qkn"], hd * 2 + (c + 1))
                    for t in range(T):
                        mm = pe.transpose(PP[c][:, tiles(t)], vn_t[:, c, tiles(t)], ident)
                    mm.then_inc(S["head_ps"], 1)
                pe.wait_ge(S["qkT_ready"], hd * 2 + 2)
                pe.wait_ge(S["v_ready"], hd + 1)
                qTv, kTv = ex[:, 0, :], ex[:, 1, :]
                qT, kT = qTk[:, 0, :], qTk[:, 1, :]
                mm5(PP[2], lambda t: kT[:, tiles(t)], lambda t: kT[:, tiles(t)], "gram_ps", 1)
                mm5(PP[3], lambda t: kT[:, tiles(t)], lambda t: qT[:, tiles(t)], "gram_ps", 1)
                for j, m in enumerate((LE, GT, GE, LT)):
                    pe.wait_ge(S["gm_ready"], hd * 4 + (j + 1))
                    if j >= 2:
                        pe.wait_ge(S["gram_sb"], hd * 2 + (j - 1))
                    pe.matmul(PP[j][:, 0:512], cm[:, m, :], gm[:, j, 0:512], start=True, stop=True)
                    pe.matmul(PP[j][:, 512:NT], cm[:, m, :], gm[:, j, 512:NT], start=True, stop=True)\
                        .then_inc(S["decay_ps"], 1)

                def vt_level(n):
                    d = n % 2
                    pe.wait_ge(S["off_ready"], hd * 14 + (n + 1))
                    if n < 2:
                        pe.wait_ge(S["inv_init"], hd * 4 + 4)
                        pe.wait_ge(S["ex_ready"], hd * 4 + 4)
                    else:
                        pe.wait_ge(S["inv_upd"], hd * 28 + 2 * (n - 1))
                    mm5(PP[d], lambda t: offd[:, d, tiles(t)], lambda t: invT[:, d, tiles(t)], "vt_ps", 1)

                def xy_level(n):
                    d = n % 2
                    pe.wait_ge(S["vt_sb"], hd * 14 + (n + 1))
                    mm5(PP[d], lambda t: inv[:, d, tiles(t)], lambda t: vt[:, d, tiles(t)], "upd_x_ps", 1)
                    mm5(PP[2 + d], lambda t: vt[:, d, tiles(t)], lambda t: inv[:, d, tiles(t)], "upd_y_ps", 1)

                for lv in range(LEVELS):
                    for d in range(2):
                        vt_level(2 * lv + d)
                    for d in range(2):
                        xy_level(2 * lv + d)
                for d in range(2):
                    pe.wait_ge(S["inv_upd"], hd * 28 + (26 + 2 * d))
                    pe.wait_ge(S["r_ready"], hd * 4 + 4)
                    mm5(PP[d], lambda t: invT[:, d, tiles(t)], lambda t: R[:, d, tiles(t)], "u_ps", 1)
                    mm5(PP[2 + d], lambda t: R[:, 2 + d, tiles(t)], lambda t: invT[:, d, tiles(t)], "wt_ps", 1)
                pe.wait_ge(S["u_sb"], hd * 2 + 2)
                pe.wait_ge(S["wt_sb"], hd * 2 + 2)
                pe.wait_ge(S["kdec_ready"], hd * 2 + 2)
                for k in range(T):
                    for d in range(2):
                        tt = tiles(k if d == 0 or k == 0 else T - k)
                        if k:
                            if k == 1:
                                pe.wait_ge(S["state_in"], hd * 32 + 32)
                            else:
                                pe.wait_ge(S["s_upd"], hd * 6 + (2 * (k - 2) + d + 1))
                            pe.wait_ge(S["o_upd"], hd * 19 + (1 + 2 + 4 * (k - 1)))
                            pe.matmul(bank(4 * d)[:, 0:P], wT(d)[:, tt], state[:, d, :], start=True, stop=True)
                            pe.matmul(bank(4 * d + 1)[:, 0:P], qT[:, tt], state[:, d, :], start=True, stop=True)\
                                .then_inc(S["s_read_ps"], 1)
                    for d in range(2):
                        tt = tiles(k if d == 0 or k == 0 else T - k)
                        if k:
                            pe.wait_ge(S["vn_ready"], hd * 8 + (2 * (k - 1) + d + 1))
                            if k == 1:
                                pe.wait_ge(S["sp_ready"], hd * 2 + (d + 1))
                        rhs = vnew[:, d, :] if k else u_all(d)[:, tt]
                        pe.matmul(bank(4 * d + 2)[:, 0:P], kdec(d)[:, tt], rhs, start=True, stop=True)
                        pe.matmul(bank(4 * d + 3)[:, 0:P], qkT[:, d, tt], rhs, start=True, stop=True)\
                            .then_inc(S["s_add_ps"], 1)
                pe.wait_ge(S["og_step"], hd * 3 + 3)
                mm5_t = [pe.transpose(PP[0][:, tiles(t)], og[:, tiles(t)], ident) for t in range(T)]
                mm5_t[-1].then_inc(S["ogT_ps"], 1)
            ring.base += 3 * H

            pe.wait_ge(S["oT_ready"], H)
            for n in range(2):
                for a in range(2):
                    gemm5(2 * n + a, 4, lhs_o, 4 * a, a == 0, a == 1, S["res_ps"],
                          free=(lambda t: pe.wait_ge(S["res_step"], 2 * (t + 1))) if n else None)
                pe.wait_ge(S["res_ps"], T * (n + 1))
                pe.sem_inc(S["slot_free"], 1)
            ring.base += 4

            def ffn(l, n_exp):
                f = F[l]
                pe.wait_ge(S["xt_ready"], 2 * T * xt_n[0])

                def lhs_h(c, t):
                    return hT[:, c, t * P:(t + 1) * P]

                with pe.Fori(0, n_exp) as e:
                    def h_transposes(j):
                        w = 256 if j < 5 else 128
                        for t in range(T):
                            n = T * j + t
                            pe.wait_ge(f["h_done"], e * 30 + (n + 1))
                            if n >= 3:
                                pe.wait_ge(f["hT_ready"], e * 30 + (n - 2))
                            else:
                                pe.wait_ge(f["hT_ready"], e * 30)
                            for c in range(w // P):
                                mm = pe.transpose(bank(5 + n % 3)[:, c * P:(c + 1) * P],
                                                  hbuf[:, t, c * P:(c + 1) * P], ident)
                            mm.then_inc(f["hT_ps"], 1)

                    for j in range(6):
                        w2 = 512 if j < 5 else 256
                        for a in range(2):
                            if j == 0:
                                free = lambda t: pe.wait_ge(f["acc_done"], e * 10)
                            else:
                                free = lambda t, j=j: pe.wait_ge(f["h_done"], e * 30 + (T * (j - 1) + t + 1))
                            gemm5(2 * j + a, 4, lhs_x, 4 * a, a == 0, a == 1, f["gu_ps"], e, 18, w2, free)
                            if a == 0 and j:
                                h_transposes(j - 1)
                        pe.wait_ge(f["gu_ps"], e * 30 + T * (j + 1))
                        pe.sem_inc(S["slot_free"], 1)
                    h_transposes(5)
                    pe.wait_ge(f["hT_ready"], e * 30 + 30)
                    for n in range(2):
                        for a in range(3):
                            free = (lambda t: pe.wait_ge(f["acc_done"], e * 10 + (t + 1))) if n else None
                            gemm5(12 + 3 * n + a, 4 if a < 2 else 3, lhs_h, 4 * a, a == 0, a == 2, f["down_ps"],
                                  e, 18, 512, free)
                        pe.wait_ge(f["down_ps"], e * 10 + T * (n + 1))
                        pe.sem_inc(S["slot_free"], 1)
                ring.base += 18 * n_exp

            transpose_x(0)
            ffn(0, 2)
            s = slot(0)
            wpv = wring[:, s, :, :].rearrange("p a (b n) -> p (a b) n", n=256)
            hp = xT[:, :, :].rearrange("p k t -> p (k t)").rearrange("p (t d) -> p t d", t=T)
            pT = carve(big, 0, 2 * D, b=2, d=D)
            for t in range(T):
                kind = POOL + (len(WINDOWS) if t else 0)
                pe.wait_ge(S["hp_step"], 3 * (t + 1))
                if t >= 2:
                    pe.wait_ge(S["poolT_sb"], t - 1)
                for k in range(KD):
                    mm = pe.matmul(PP[t % 2][:, k * P:(k + 1) * P], hp[:, t, k * P:(k + 1) * P],
                                   cm[:, kind + k // 2, :], start=True, stop=True)
                mm.then_inc(S["poolT_ps"], 1)
                pe.wait_ge(S["poolT_sb"], t + 1)
                if t >= 2:
                    pe.wait_ge(S["pool_step"], 5 * (t - 1))
                for g in range(4):
                    for k in range(2):
                        mm = pe.matmul(PP[2 + t % 2][:, g * 256:(g + 1) * 256],
                                       pT[:, t % 2, (2 * g + k) * P:(2 * g + k + 1) * P],
                                       wpv[:, 2 * g + k, :], start=(k == 0), stop=(k == 1))
                mm.then_inc(S["pool_ps"], 1)
            pe.wait_ge(S["pool_ps"], T)
            pe.sem_inc(S["slot_free"], 1)
            ring.base += 1
            transpose_x(2)
            pe.wait_ge(S["xt_ready"], 2 * T * xt_n[0])
            for t in range(T):
                for k in range(KD):
                    mm = pe.matmul(bank(7)[:, 8 * t:8 * t + 8], lhs_x(k, t), rw[:, k, :],
                                   start=(k == 0), stop=(k == KD - 1))
            mm.then_inc(S["logit_ps"], 1)
            ffn(1, 8)

        @block.gpsimd
        def _(pool):
            pool.memset(mhalf[:, :], -0.5).then_inc(S["pool_const"], 1)
            pool.memset(cbuf, 0.0).then_inc(S["cbuf_zero"], 1)
            pool.wait_ge(S["pool_const"], 1)

            def load_rows(n, layer, which, ln):
                if n:
                    pool.wait_ge(S["ln_step"], n * T * LN_STEPS)
                for r in range(2):
                    pool.dma_start(rows[:, r, :], mod_dram[layer, r, which * D:(which + 1) * D].partition_broadcast(P))\
                        .then_inc(S["rows_in"], 16)
                pool.dma_start(rows[:, 2, :], A["ln_g"][layer, ln].partition_broadcast(P)).then_inc(S["rows_in"], 16)
                pool.dma_start(rows[:, 3, :], A["ln_b"][layer, ln].partition_broadcast(P)).then_inc(S["rows_in"], 16)

            def rstds(n):
                for t in range(T):
                    m = n * T + t
                    pool.wait_ge(S["ln_step"], (m * LN_STEPS) + 3)
                    pool.tensor_scalar(rstd[:, 0, t:t + 1], lnmv[:, t, 1:2], EPS, None, ALU.add).then_inc(S["ln_rstd"], 1)
                    pool.wait_ge(S["ln_rstd"], 2 * m + 1)
                    pool.tensor_tensor(rstd[:, 1, t:t + 1], rstd[:, 0, t:t + 1], mhalf[:, 0:1], ALU.pow).then_inc(S["ln_rstd"], 1)

            for b in range(3):
                pool.wait_ge(mod_out[b], 16 * 8)
            pool.dma_start(modcol_in[:, :], mod_dram[0].rearrange("r (a p) -> (r a) p", p=P)).then_inc(modcol_in_s, 16)
            pool.wait_ge(S["modcol_ready"], 1)
            pool.dma_start(modcol_in[:, :], mod_dram[1].rearrange("r (a p) -> (r a) p", p=P)).then_inc(modcol_in_s, 16)

            with pool.Fori(0, H) as hd:
                pool.wait_ge(S["oT_ready"], hd)
                pool.wait_ge(S["gate_step"], 8)
                for j, (m, d) in enumerate(((GT, 0), (LE, 0), (LT, 1), (GE, 1))):
                    pool.tensor_tensor(per_tile(gm[:, j, :]), mat_bc(m), col_bc(gcol(G_, d, hd)), ALU.mult)\
                        .then_inc(S["gm_ready"], 1)
                for c in range(2):
                    pool.wait_ge(S["ss_done"], hd * 4 + 2 * (c + 1))
                    pool.tensor_tensor(ss[:, 4 + c, :], ss[:, 2 + c, :], mhalf[:, :], ALU.pow).then_inc(S["rn_step"], 1)
                for d in range(2):
                    for dst in (inv, invT):
                        pool.tensor_tensor(per_tile(dst[:, d, :]), mat_bc(IDENT), mat_bc(ONES), ALU.mult)\
                            .then_inc(S["inv_init"], 1)
                for n in range(2 * LEVELS):
                    lv, d = n // 2, n % 2
                    pool.wait_ge(S["a_step"], hd * 4 + (2 * d + 2))
                    if n < 2:
                        pool.wait_ge(S["conv_step"], hd * 15 + 15)
                    else:
                        pool.wait_ge(S["vt_ps"], hd * 14 + (n - 1))
                    pool.tensor_tensor(per_tile(offd[:, d, :]), per_tile(ex[:, 2 * d, :]),
                                       mat_bc(LEVEL + LEVELS * d + lv), ALU.mult).then_inc(S["off_ready"], 1)
                pool.wait_ge(S["decay_ps"], hd * 4 + 4)
                pool.wait_ge(S["v_ready"], hd + 1)
                for d in range(2):
                    pool.tensor_tensor(per_tile(R[:, d, :]), per_tile(vn_t[:, 2, :]), col_bc(gcol(BETA, d, hd)), ALU.mult)\
                        .then_inc(S["r_ready"], 1)
                for d in range(2):
                    pool.tensor_tensor(per_tile(R[:, 2 + d, :]), per_tile(vn_t[:, 1, :]), col_bc(gcol(BG, d, hd)), ALU.mult)\
                        .then_inc(S["r_ready"], 1)
                for d in range(2):
                    pool.wait_ge(S["off_ready"], hd * 14 + 14)
                    pool.tensor_tensor(per_tile(kdec(d)), per_tile(vn_t[:, 1, :]), col_bc(gcol(EK, d, hd)), ALU.mult)\
                        .then_inc(S["kdec_ready"], 1)
                pool.wait_ge(S["sso_done"], hd * 2 + 2)
                pool.tensor_tensor(ss[:, 7, :], ss[:, 6, :], mhalf[:, :], ALU.pow).then_inc(S["rno_step"], 1)

            pool.wait_ge(S["oT_ready"], H)
            load_rows(0, 0, 2, 0)
            rstds(0)
            load_rows(1, 0, 5, 1)
            rstds(1)
            load_rows(2, 1, 2, 0)
            for r in range(2):
                pool.dma_start(acc[:, r, :], mod_dram[1, r, D:2 * D].partition_broadcast(P)).then_inc(S["poolrows_in"], 16)
                pool.dma_start(acc[:, 2 + r, :], mod_dram[1, r, 0:D].partition_broadcast(P)).then_inc(S["poolrows_in"], 16)
            pool.dma_start(big[:, 2 * D:3 * D], A["pool_b"][0].partition_broadcast(P)).then_inc(S["poolrows_in"], 16)
            pool.dma_start(big[:, 3 * D:4 * D], A["pool_scale"][0].partition_broadcast(P)).then_inc(S["poolrows_in"], 16)
            rstds(2)
            load_rows(3, 1, 5, 1)
            rstds(3)

        @block.scalar
        def _(act):
            act.wait_ge(S["cond_ps"], 1)
            act.activation(cs[:, :], PP[3][:, 0:16], ACT.Silu).then_inc(S["cond_ready"], 1)
            for layer in range(2):
                bv = A["ada_b"][layer]
                with act.Fori(0, 4) as i:
                    for b in range(3):
                        act.wait_ge(S["mod_row"], i * 3 + (12 * layer + b + 1))
                        act.dma_start(brow[:, b, :], bv[bass.ds(i * 1536 + 512 * b, 512)].partition_broadcast(2))\
                            .then_inc(bias_in[b], 16)
                    for b in range(3):
                        act.wait_ge(S["mod_row"], i * 3 + (12 * layer + b + 4))
                        act.dma_start(mod_dram[layer, :, bass.ds(i * 1536 + 512 * b, 512)], mrow[:, b, :])\
                            .then_inc(mod_out[b], 16)
            for n in range(2):
                for t in range(T):
                    act.wait_ge(S["z_ps"], T * n + t + 1)
                    act.activation(acc[:, t, 512 * n:512 * n + 512], bank(t), ACT.Silu).then_inc(S["z_ready"], 1)
            act.wait_ge(S["gate_step"], 2)
            act.activation(gates5[:, SPA, :, :], gates5[:, SPA, :, :], ACT.Exp, scale=-1.0).then_inc(S["gate_act"], 1)
            act.activation(gates5[:, TMP, :, :], gates5[:, AB0, :, :], ACT.Exp, scale=-1.0).then_inc(S["gate_act"], 1)
            act.activation(alog[:, :], alog[:, :], ACT.Exp).then_inc(S["gate_act"], 1)
            act.wait_ge(S["gate_act"], 1)
            act.activation(gates5[:, SPB, :, :], gates5[:, SPA, :, :], ACT.Ln, bias=1.0).then_inc(S["gate_act"], 1)
            act.wait_ge(S["cum_ps"], 1)
            cum = bank(7)[:, 0:240].rearrange("p (s q) -> p s q", s=3)
            act.activation(gates5[:, EG:EG + 3, :, :].rearrange("p s t h -> p s (t h)"), cum, ACT.Exp).then_inc(S["gate_act"], 1)

            with act.Fori(0, H) as hd:
                act.wait_ge(S["oT_ready"], hd)
                for d in range(2):
                    act.dma_start(state[:, d, :], A["state_dn"][0, 0, d, bass.ds(hd, 1)].rearrange("a k v -> (a k) v"))\
                        .then_inc(S["state_in"], 16)
                act.wait_ge(S["cbuf_zero"], hd + 1)
                for c in range(3):
                    act.wait_ge(S["q_k_v_ps"], hd * 3 + (c + 1))
                    act.activation(cbuf[:, c, 2:130], PP[c][:, 0:P], ACT.Copy)
                    act.activation(cbuf[:, c, 134:646], PP[c][:, P:NT], ACT.Copy).then_inc(S["conv_in"], 1)
                for c in range(3):
                    act.wait_ge(S["conv_step"], hd * 15 + 5 * (c + 1))
                    act.activation(cv[:, c, :], cv[:, c, :], ACT.Silu).then_inc(S["silu_done"], 1)
                for c in range(2):
                    act.wait_ge(S["tok_ps"], hd * 3 + (c + 1))
                    act.activation(sq[:, c, :], PP[c][:, 0:NT], ACT.Square).then_inc(S["sq_done"], 1)
                act.wait_ge(S["tok_ps"], hd * 3 + 3)
                act.activation(vn_t[:, 2, :], PP[2][:, 0:NT], ACT.Copy).then_inc(S["v_ready"], 1)
                for c in range(2):
                    act.wait_ge(S["head_ps"], hd * 2 + (c + 1))
                    act.activation(qTk[:, c, :], PP[c][:, 0:NT], ACT.Copy).then_inc(S["qkT_ready"], 1)
                for c, dst in enumerate((kk, qk)):
                    act.wait_ge(S["gram_ps"], hd * 2 + (c + 1))
                    act.activation(dst, PP[2 + c][:, 0:NT], ACT.Copy).then_inc(S["gram_sb"], 1)
                for j in range(4):
                    act.wait_ge(S["decay_ps"], hd * 4 + (j + 1))
                    act.activation(ex[:, j, :], PP[j][:, 0:NT], ACT.Exp).then_inc(S["ex_ready"], 1)
                for n in range(2 * LEVELS):
                    d = n % 2
                    act.wait_ge(S["vt_ps"], hd * 14 + (n + 1))
                    act.activation(vt[:, d, :], PP[d][:, 0:NT], ACT.Copy).then_inc(S["vt_sb"], 1)
                for d in range(2):
                    act.wait_ge(S["u_ps"], hd * 2 + (d + 1))
                    act.activation(u_all(d), PP[d][:, 0:NT], ACT.Copy).then_inc(S["u_sb"], 1)
                    act.wait_ge(S["wt_ps"], hd * 2 + (d + 1))
                    act.activation(wT(d), PP[2 + d][:, 0:NT], ACT.Copy).then_inc(S["wt_sb"], 1)
                for d in range(2):
                    act.wait_ge(S["s_add_ps"], hd * 10 + (d + 1))
                    act.wait_ge(S["state_out"], hd * 32)
                    act.activation(state_new[:, d, :], bank(4 * d + 2)[:, 0:P], ACT.Copy).then_inc(S["sp_ready"], 1)
                for d in range(2):
                    act.wait_ge(S["sp_ready"], hd * 2 + (d + 1))
                    act.dma_start(out_state[0, 0, d, bass.ds(hd, 1)].rearrange("a k v -> (a k) v"), state_new[:, d, :])\
                        .then_inc(S["state_out"], 16)
                act.wait_ge(S["o_upd"], hd * 19 + 19)
                act.activation(invT[:, 0, :], oacc, ACT.Square).then_inc(S["sqo_done"], 1)
                act.wait_ge(S["ogT_ps"], hd + 1)
                act.activation(oT[:, bass.ds(hd, 1), :].rearrange("p a t -> p (a t)"), PP[0][:, 0:NT], ACT.Copy)\
                    .then_inc(S["oT_ready"], 1)
            act.wait_ge(S["state_out"], 32 * H)

            def ffn(l, n_exp):
                f = F[l]
                with act.Fori(0, n_exp) as e:
                    for j in range(6):
                        w = 256 if j < 5 else 128
                        if j:
                            for t in range(T):
                                copy_h(f, e, j - 1, t)
                        for t in range(T):
                            n = T * j + t
                            act.wait_ge(f["gu_ps"], e * 30 + (n + 1))
                            if n >= 3:
                                act.wait_ge(f["h_done"], e * 30 + (n - 2))
                            else:
                                act.wait_ge(f["h_done"], e * 30)
                            act.activation(hsil[:, n % 3, 0:w], bank(t)[:, 0:w], ACT.Silu).then_inc(f["sil_done"], 1)
                    for t in range(T):
                        copy_h(f, e, 5, t)

            def copy_h(f, e, j, t):
                nc_ = 2 if j < 5 else 1
                n = T * j + t
                act.wait_ge(f["hT_ps"], e * 30 + (n + 1))
                src = bank(5 + n % 3)[:, 0:nc_ * P].rearrange("p (c t) -> p c t", c=nc_)
                act.activation(hT[:, 2 * j:2 * j + nc_, t * P:(t + 1) * P], src, ACT.Copy).then_inc(f["hT_ready"], 1)

            ffn(0, 2)
            pT = carve(big, 0, 2 * D, b=2, d=D)
            for t in range(T):
                act.wait_ge(S["poolT_ps"], t + 1)
                if t >= 2:
                    act.wait_ge(S["pool_ps"], t - 1)
                act.activation(pT[:, t % 2, :], PP[t % 2][:, :], ACT.Copy).then_inc(S["poolT_sb"], 1)
            act.wait_ge(S["route_step"], 2)
            act.activation(rt[:, 1, :, :], rt[:, 1, :, :], ACT.Exp).then_inc(S["route_act"], 1)
            ffn(1, 8)

        @block.vector
        def _(dve):
            dve.wait_ge(S["conv_ps"], 1)
            dve.tensor_copy(convw[:, :, :].rearrange("p j c -> p (j c)"), PP[3][:, 512:632]).then_inc(S["conv_cols"], 1)
            dve.sem_inc(S["mod_row"], 3)
            for layer in range(2):
                with dve.Fori(0, 4) as i:
                    for b in range(3):
                        dve.wait_ge(S["mod_ps"], i * 3 + (12 * layer + b + 1))
                        dve.wait_ge(bias_in[b], i * 16 + (64 * layer + 16))
                        dve.wait_ge(mod_out[b], i * 16 + 64 * layer)
                        dve.tensor_tensor(mrow[:, b, :], bank(b)[0:2, :], brow[:, b, :], ALU.add).then_inc(S["mod_row"], 1)
            xt_n = [0]
            for layer in range(2):
                dve.wait_ge(S["modcol_ps"], layer + 1)
                dve.tensor_copy(modc[layer], PP[3][:, 0:96]).then_inc(S["modcol_ready"], 1)
            dve.wait_ge(S["modcol_ready"], 2)

            def transposed_mod(layer, sub):
                mc = modc[layer].rearrange("p (r w k) -> p r w k", r=2, w=6)
                n = xt_n[0]
                if n:
                    dve.wait_ge(S["xt_ready"], 2 * T * n)
                dve.tensor_scalar(scp1[:, :, :], mc[:, :, 3 * sub + 1, :], 1.0, None, ALU.add).then_inc(S["scp1_ready"], 1)
                dve.wait_ge(S["scp1_ready"], n + 1)
                for t in range(T):
                    r = 1 if t else 0
                    dve.wait_ge(S["xt_ps"], n * T + t + 1)
                    for k in range(KD):
                        last = dve.tensor_scalar(xT[:, k, t * P:(t + 1) * P], PP[t % 4][:, k * P:(k + 1) * P],
                                                 scp1[:, r, k:k + 1], mc[:, r, 3 * sub, k:k + 1], ALU.mult, ALU.add)
                        if k in (KD // 2 - 1, KD - 1):
                            last.then_inc(S["xt_ready"], 1)
                xt_n[0] += 1

            transposed_mod(0, 0)
            step = [0]

            def gstep(ins):
                step[0] += 1
                ins.then_inc(S["gate_step"], 1)
                dve.wait_ge(S["gate_step"], step[0])

            dve.wait_ge(S["ab_ps"], 1)
            abv = bank(6)[:, 0:160].rearrange("p (t w) -> p t w", t=T)
            gstep(dve.tensor_copy(gates5[:, AB0, :, :], abv[:, :, 16:32]))
            dve.wait_ge(S["small_in"], 16 * 8)
            bc16 = lambda a: a.rearrange("p (o h) -> p o h", o=1).to_broadcast([P, T, 16])
            dve.tensor_tensor(gates5[:, T2, :, :], abv[:, :, 0:16], bc16(dtb[:, :]), ALU.add).then_inc(S["gate_arg"], 1)
            dve.wait_ge(S["gate_arg"], 1)
            gstep(dve.scalar_tensor_tensor(gates5[:, SPA, :, :], gates5[:, T2, :, :], -1.0, gates5[:, T2, :, :], ALU.mult, ALU.max))
            dve.wait_ge(S["gate_act"], 4)
            gstep(dve.scalar_tensor_tensor(gates5[:, SPB, :, :], gates5[:, T2, :, :], 0.0, gates5[:, SPB, :, :], ALU.max, ALU.add))
            gstep(dve.tensor_tensor(gates5[:, SPB, :, :], gates5[:, SPB, :, :], bc16(alog[:, :]), ALU.mult))
            gstep(dve.tensor_scalar(gates5[:, G_, :, :], gates5[:, SPB, :, :], -1.0, None, ALU.mult))
            gstep(dve.tensor_scalar(gates5[:, TMP, :, :], gates5[:, TMP, :, :], 1.0, None, ALU.add))
            gstep(dve.reciprocal(gates5[:, BETA, :, :], gates5[:, TMP, :, :]))
            gstep(dve.memset(gates5[:, NA, :, :], 0.0))
            dve.wait_ge(S["gate_act"], 5)
            gstep(dve.tensor_tensor(gates5[:, BG, :, :], gates5[:, BETA, :, :], gates5[:, EG, :, :], ALU.mult))

            with dve.Fori(0, H) as hd:
                dve.wait_ge(S["oT_ready"], hd)
                for c in range(3):
                    dve.wait_ge(S["conv_in"], hd * 3 + (c + 1))
                    for j in range(5):
                        wcol = convw[:, j, bass.ds(hd + 8 * c, 1)]
                        if j == 0:
                            ins = dve.tensor_scalar(cv[:, c, :], cbuf[:, c, 0:644], wcol, None, ALU.mult)
                        else:
                            dve.wait_ge(S["conv_step"], hd * 15 + (5 * c + j))
                            ins = dve.scalar_tensor_tensor(cv[:, c, :], cbuf[:, c, j:j + 644], wcol, cv[:, c, :],
                                                           ALU.mult, ALU.add)
                        ins.then_inc(S["conv_step"], 1)
                for c in range(2):
                    dve.wait_ge(S["sq_done"], hd * 2 + (c + 1))
                    dve.tensor_reduce(ss[:, c, :], per_tile(sq[:, c, :]), AX.X, ALU.add).then_inc(S["ss_done"], 1)
                    dve.wait_ge(S["ss_done"], hd * 4 + (2 * c + 1))
                    dve.tensor_scalar(ss[:, 2 + c, :], ss[:, c, :], EPS, float(P) if c == 0 else 1.0, ALU.add, ALU.mult)\
                        .then_inc(S["ss_done"], 1)
                for c in range(2):
                    dve.wait_ge(S["rn_step"], hd * 2 + (c + 1))
                    dve.tensor_tensor(per_tile(vn_t[:, c, :]), per_tile(PP[c][:, 0:NT]),
                                      col_bc(ss[:, 4 + c, :].rearrange("p (t o) -> p t o", o=1)), ALU.mult)\
                        .then_inc(S["qkn"], 1)
                dve.wait_ge(S["gram_sb"], hd * 2 + 2)
                for d in range(2):
                    dve.wait_ge(S["ex_ready"], hd * 4 + (2 * d + 1))
                    a = ex[:, 2 * d, :]
                    dve.tensor_tensor(a, a, kk, ALU.mult).then_inc(S["a_step"], 1)
                    dve.wait_ge(S["a_step"], hd * 4 + (2 * d + 1))
                    dve.tensor_tensor(per_tile(a), per_tile(a), col_bc(gcol(BETA, d, hd)), ALU.mult).then_inc(S["a_step"], 1)
                for d in range(2):
                    dve.wait_ge(S["ex_ready"], hd * 4 + (2 * d + 2))
                    w = ex[:, 2 * d + 1, :]
                    dve.tensor_tensor(w, w, qk, ALU.mult).then_inc(S["w_step"], 1)
                    dve.wait_ge(S["w_step"], hd * 4 + (2 * d + 1))
                    dve.tensor_tensor(per_tile(qkT[:, d, :]), per_tile(w), mat_bc(GE if d else LE), ALU.mult)\
                        .then_inc(S["w_step"], 1)
                dve.wait_ge(S["a_step"], hd * 4 + 4)
                dve.memset(oacc, 0.0).then_inc(S["o_upd"], 1)
                for n in range(2 * LEVELS):
                    d = n % 2
                    dve.wait_ge(S["upd_x_ps"], hd * 14 + (n + 1))
                    if n < 2:
                        dve.wait_ge(S["inv_init"], hd * 4 + 4)
                    else:
                        dve.wait_ge(S["inv_upd"], hd * 28 + 2 * (n - 1))
                    dve.tensor_tensor(invT[:, d, :], invT[:, d, :], PP[d][:, 0:NT], ALU.subtract).then_inc(S["inv_upd"], 1)
                    dve.wait_ge(S["upd_y_ps"], hd * 14 + (n + 1))
                    dve.tensor_tensor(inv[:, d, :], inv[:, d, :], PP[2 + d][:, 0:NT], ALU.subtract).then_inc(S["inv_upd"], 1)
                n_o = 1
                for k in range(T):
                    for d in range(2):
                        t = k if d == 0 or k == 0 else T - k
                        tt = slice(t * P, (t + 1) * P)
                        if k:
                            dve.wait_ge(S["s_read_ps"], hd * 8 + (2 * (k - 1) + d + 1))
                            dve.wait_ge(S["u_sb"], hd * 2 + 2)
                            dve.tensor_tensor(vnew[:, d, :], u_all(d)[:, tt], bank(4 * d)[:, 0:P], ALU.subtract)\
                                .then_inc(S["vn_ready"], 1)
                            dve.wait_ge(S["o_upd"], hd * 19 + n_o)
                            dve.scalar_tensor_tensor(oacc[:, tt], bank(4 * d + 1)[:, 0:P],
                                                     gates5[:, EG, t, bass.ds(hd + 8 * d, 1)], oacc[:, tt],
                                                     ALU.mult, ALU.add).then_inc(S["o_upd"], 1)
                            n_o += 1
                    for d in range(2):
                        t = k if d == 0 or k == 0 else T - k
                        tt = slice(t * P, (t + 1) * P)
                        dve.wait_ge(S["s_add_ps"], hd * 10 + (2 * k + d + 1))
                        if 0 < k < T - 1:
                            if k == 1:
                                dve.wait_ge(S["state_in"], hd * 32 + 32)
                            else:
                                dve.wait_ge(S["s_upd"], hd * 6 + (2 * (k - 2) + d + 1))
                            dve.scalar_tensor_tensor(state[:, d, :], state[:, d, :],
                                                     gates5[:, EL, t, bass.ds(hd + 8 * d, 1)],
                                                     bank(4 * d + 2)[:, 0:P], ALU.mult, ALU.add).then_inc(S["s_upd"], 1)
                        dve.wait_ge(S["o_upd"], hd * 19 + n_o)
                        dve.tensor_tensor(oacc[:, tt], oacc[:, tt], bank(4 * d + 3)[:, 0:P], ALU.add).then_inc(S["o_upd"], 1)
                        n_o += 1
                assert n_o == 19
                dve.wait_ge(S["sqo_done"], hd + 1)
                dve.tensor_reduce(ss[:, 6, :], per_tile(invT[:, 0, :]), AX.X, ALU.add).then_inc(S["sso_done"], 1)
                dve.wait_ge(S["sso_done"], hd * 2 + 1)
                dve.tensor_scalar(ss[:, 6, :], ss[:, 6, :], 1.0 / P, EPS, ALU.mult, ALU.add).then_inc(S["sso_done"], 1)
                dve.wait_ge(S["rno_step"], hd + 1)
                dve.tensor_tensor(per_tile(og), per_tile(oacc), col_bc(ss[:, 7, :].rearrange("p (t o) -> p t o", o=1)),
                                  ALU.mult).then_inc(S["og_step"], 1)
                dve.wait_ge(S["og_step"], hd * 3 + 1)
                dve.tensor_tensor(per_tile(og), per_tile(og),
                                  ngb[:, :].rearrange("p (o c) -> p o c", o=1).to_broadcast([P, T, P]), ALU.mult)\
                    .then_inc(S["og_step"], 1)
                dve.wait_ge(S["og_step"], hd * 3 + 2)
                dve.tensor_tensor(per_tile(og), per_tile(og), acc[:, :, bass.ds(hd * P, P)], ALU.mult)\
                    .then_inc(S["og_step"], 1)
                dve.wait_ge(S["off_ready"], hd * 14 + 14)
                dve.wait_ge(S["vt_ps"], hd * 14 + 14)
                dve.memset(cbuf, 0.0).then_inc(S["cbuf_zero"], 1)

            def layer_norm(n):
                for t in range(T):
                    base = (n * T + t) * LN_STEPS
                    xt = x[:, t, :]
                    ready(n, t)
                    for a in range(2):
                        dve.bn_stats(lnst[:, t, a, :], x[:, t, 512 * a:512 * a + 512]).then_inc(S["ln_step"], 1)
                    dve.wait_ge(S["ln_step"], base + 2)
                    dve.bn_aggr(lnmv[:, t, :], lnst[:, t, :, :].rearrange("p a b -> p (a b)")).then_inc(S["ln_step"], 1)
                    dve.wait_ge(S["ln_step"], base + 3)
                    dve.wait_ge(S["ln_rstd"], 2 * (n * T + t) + 2)
                    dve.tensor_scalar(xt, xt, lnmv[:, t, 0:1], rstd[:, 1, t:t + 1], ALU.subtract, ALU.mult)\
                        .then_inc(S["ln_step"], 1)
                    dve.wait_ge(S["ln_step"], base + 4)
                    dve.tensor_tensor(xt, xt, rows[:, 2, :], ALU.mult).then_inc(S["ln_step"], 1)
                    dve.wait_ge(S["ln_step"], base + 5)
                    dve.tensor_tensor(xt, xt, rows[:, 3, :], ALU.add).then_inc(S["ln_step"], LN_STEPS - 5)

            res_n = [0]

            def ready(n, t):
                dve.wait_ge(S["res_step"], res_after[n])

            res_after = {}

            def rstep(ins):
                res_n[0] += 1
                ins.then_inc(S["res_step"], 1)
                return res_n[0]

            dve.wait_ge(S["rows_in"], 64)
            for n in range(2):
                for t in range(T):
                    dve.wait_ge(S["res_ps"], T * n + t + 1)
                    cols = slice(512 * n, 512 * n + 512)
                    tmp = lnt[:, t, cols]
                    v = rstep(dve.tensor_tensor(tmp, bank(t), rows[:, 1 if t else 0, cols], ALU.mult))
                    dve.wait_ge(S["res_step"], v)
                    v = rstep(dve.scalar_tensor_tensor(x[:, t, cols], x[:, t, cols], ALPHA, tmp, ALU.mult, ALU.add))
            res_after[0] = v
            layer_norm(0)

            def ffn(l, n_exp, n_ln):
                f = F[l]
                dve.memset(acc[:, :, :], 0.0).then_inc(f["acc_done"], 0) if False else None
                with dve.Fori(0, n_exp) as e:
                    for j in range(6):
                        w = 256 if j < 5 else 128
                        for t in range(T):
                            n = T * j + t
                            dve.wait_ge(f["sil_done"], e * 30 + (n + 1))
                            dve.wait_ge(f["hT_ps"], e * 30 + max(0, n - T + 1))
                            dve.tensor_tensor(hbuf[:, t, 0:w], hsil[:, n % 3, 0:w], bank(t)[:, w:2 * w], ALU.mult)\
                                .then_inc(f["h_done"], 1)
                    for n in range(2):
                        for t in range(T):
                            cols = slice(512 * n, 512 * n + 512)
                            dve.wait_ge(f["down_ps"], e * 10 + (T * n + t + 1))
                            dve.wait_ge(f["acc_done"], e * 10)
                            dve.scalar_tensor_tensor(acc[:, t, cols], bank(t),
                                                     gate_e[:, l, t, bass.ds(e, 1)], acc[:, t, cols],
                                                     ALU.mult, ALU.add).then_inc(f["acc_done"], 1)
                dve.wait_ge(f["acc_done"], 10 * n_exp)
                dve.wait_ge(S["rows_in"], 64 * (n_ln + 1))
                for t in range(T):
                    v = rstep(dve.tensor_tensor(acc[:, t, :], acc[:, t, :], rows[:, 1 if t else 0, :], ALU.mult))
                    dve.wait_ge(S["res_step"], v)
                    v = rstep(dve.scalar_tensor_tensor(x[:, t, :], x[:, t, :], ALPHA, acc[:, t, :], ALU.mult, ALU.add))
                    dve.wait_ge(S["res_step"], v)
                res_after[n_ln] = v

            def rwait(ins):
                dve.wait_ge(S["res_step"], rstep(ins))

            transposed_mod(0, 1)
            rwait(dve.memset(gate_e[:, 0, :, :], 1.0))
            rwait(dve.memset(acc[:, :, :], 0.0))
            ffn(0, 2, 1)
            layer_norm(1)

            hp = xT[:, :, :].rearrange("p k t -> p (k t)").rearrange("p (t d) -> p t d", t=T)
            dve.wait_ge(S["poolrows_in"], 16 * 6)
            for t in range(T):
                r = 1 if t else 0
                dve.wait_ge(S["ln_step"], (T + t + 1) * LN_STEPS)
                dve.tensor_tensor(hp[:, t, :], x[:, t, :], acc[:, r, :], ALU.mult).then_inc(S["hp_step"], 1)
                dve.wait_ge(S["hp_step"], 3 * t + 1)
                dve.tensor_tensor(hp[:, t, :], hp[:, t, :], x[:, t, :], ALU.add).then_inc(S["hp_step"], 1)
                dve.wait_ge(S["hp_step"], 3 * t + 2)
                dve.tensor_tensor(hp[:, t, :], hp[:, t, :], acc[:, 2 + r, :], ALU.add).then_inc(S["hp_step"], 1)
            dve.wait_ge(S["rows_in"], 64 * 3)
            pb, psc = big[:, 2 * D:3 * D], big[:, 3 * D:4 * D]
            for t in range(T):
                y = lnt[:, t, :]
                dve.wait_ge(S["pool_ps"], t + 1)
                dve.tensor_tensor(y, PP[2 + t % 2][:, :], pb, ALU.add).then_inc(S["pool_step"], 1)
                dve.wait_ge(S["pool_step"], 5 * t + 1)
                dve.tensor_tensor(y, y, psc, ALU.mult).then_inc(S["pool_step"], 1)
                dve.wait_ge(S["pool_step"], 5 * t + 2)
                dve.tensor_tensor(y, y, rows[:, 1 if t else 0, :], ALU.mult).then_inc(S["pool_step"], 1)
                dve.wait_ge(S["pool_step"], 5 * t + 3)
                v = rstep(dve.scalar_tensor_tensor(x[:, t, :], x[:, t, :], ALPHA, y, ALU.mult, ALU.add))
                dve.wait_ge(S["res_step"], v)
                dve.sem_inc(S["pool_step"], 2)
            res_after[2] = v
            layer_norm(2)
            transposed_mod(1, 1)
            step = [0]

            def rts(ins):
                step[0] += 1
                ins.then_inc(S["route_step"], 1)
                dve.wait_ge(S["route_step"], step[0])

            LOG, E_, PR, MX, SUM, GTM, EQ, PRE, TA, TB = range(10)
            c8 = lambda a: a.to_broadcast([P, T, 8])
            dve.wait_ge(S["logit_ps"], 1)
            lg = bank(7)[:, 0:40].rearrange("p (t e) -> p t e", t=T)
            rts(dve.tensor_reduce(rt[:, SUM, :, 0:1], lg, AX.X, ALU.max))
            rts(dve.tensor_tensor(rt[:, E_, :, :], lg, c8(rt[:, SUM, :, 0:1]), ALU.subtract))
            dve.wait_ge(S["route_act"], 1)
            rts(dve.tensor_reduce(rt[:, SUM, :, 1:2], rt[:, E_, :, :], AX.X, ALU.add))
            rts(dve.reciprocal(rt[:, SUM, :, 2:3], rt[:, SUM, :, 1:2]))
            rts(dve.tensor_tensor(rt[:, PR, :, :], rt[:, E_, :, :], c8(rt[:, SUM, :, 2:3]), ALU.mult))
            for t in range(T):
                rts(dve.max(rt[:, MX, t, :], rt[:, PR, t, :]))
            m2 = rt[:, MX, :, 1:2]
            rts(dve.tensor_tensor(rt[:, GTM, :, :], rt[:, PR, :, :], c8(m2), ALU.is_gt))
            rts(dve.tensor_tensor(rt[:, EQ, :, :], rt[:, PR, :, :], c8(m2), ALU.is_equal))
            rts(dve.tensor_reduce(rt[:, PRE, :, 0:1], rt[:, GTM, :, :], AX.X, ALU.add))
            for e in range(7):
                rts(dve.tensor_tensor(rt[:, PRE, :, e + 1:e + 2], rt[:, PRE, :, e:e + 1], rt[:, EQ, :, e:e + 1], ALU.add))
            rts(dve.tensor_scalar(rt[:, TA, :, :], rt[:, PRE, :, :], 1.5, None, ALU.is_lt))
            rts(dve.tensor_tensor(rt[:, TA, :, :], rt[:, TA, :, :], rt[:, EQ, :, :], ALU.mult))
            rts(dve.tensor_tensor(rt[:, TA, :, :], rt[:, TA, :, :], rt[:, GTM, :, :], ALU.add))
            rts(dve.tensor_tensor(rt[:, SUM, :, 3:4], rt[:, MX, :, 0:1], m2, ALU.add))
            rts(dve.reciprocal(rt[:, SUM, :, 4:5], rt[:, SUM, :, 3:4]))
            rts(dve.tensor_tensor(rt[:, TB, :, :], rt[:, PR, :, :], rt[:, TA, :, :], ALU.mult))
            rts(dve.tensor_tensor(gate_e[:, 1, :, :], rt[:, TB, :, :], c8(rt[:, SUM, :, 4:5]), ALU.mult))
            rwait(dve.memset(acc[:, :, :], 0.0))
            ffn(1, 8, 3)
            layer_norm(3)


_INS = ["x_prompt", "x_sample", "state_dn", "c", "c_ctx", "ada_w", "ada_b", "ln_g", "ln_b", "dn_w_in", "dn_conv",
        "dn_a_log", "dn_dt_bias", "dn_norm_g", "dn_w_out", "pool_w", "pool_b", "pool_scale", "ffn_w_gu",
        "ffn_w_down", "moe_router", "moe_w_gu", "moe_w_down"]


def kernel(**inputs):
    import numpy as _np
    import concourse.bacc as _bacc
    from concourse.bass_utils import run_bass_kernel_spmd as _run

    nc = _bacc.Bacc("TRN2", target_bir_lowering=False, num_devices=1)
    arrays, A = {}, {}
    for name in _INS:
        arrays[f"in_{name}"] = _np.ascontiguousarray(inputs[name])
        A[name] = nc.dram_tensor(f"in_{name}", arrays[f"in_{name}"].shape, F32, kind="ExternalInput").ap()
    arrays["in_consts"] = shape_constants()
    A["consts"] = nc.dram_tensor("in_consts", arrays["in_consts"].shape, F32, kind="ExternalInput").ap()
    outs = [nc.dram_tensor(n, s, F32, kind="ExternalOutput").ap()
            for n, s in (("y_prompt", (1, P, D)), ("y_sample", (1, 4 * P, D)), ("new_state", (1, 1, 2, H, P, P)))]
    mod_dram = nc.dram_tensor("mod_rows", (2, 2, 6 * D), F32, kind="Internal").ap()
    backbone(nc, A, *outs, mod_dram)
    r = _run(nc, [arrays], core_ids=[0]).results[0]
    return r["y_prompt"], r["y_sample"], r["new_state"]
```

```python
from contextlib import ExitStack

import numpy as np

import concourse.bass as bass
from concourse import mybir

F32 = mybir.dt.float32
F32R = mybir.dt.float32r
I32 = mybir.dt.int32
U32 = mybir.dt.uint32
ALU = mybir.AluOpType
ACT = mybir.ActivationFunctionType
AX = mybir.AxisListType

P = 128
D = 1024
KD = D // P
T = 5
NT = T * P
H = 8
FE = 1408
KF = FE // P
GRID_W = 64
WINDOWS = (2, 4, 8, 16)
ALPHA = (2.0 * 2) ** 0.25
EPS = 1e-6
RING = 3
LEVELS = 7

SLOTS = 18
HALVES = 4
IDENT, LT, ONES = range(3)
POOL = 3
N_CONST = POOL + 2 * len(WINDOWS)
LE, GE, GT = range(N_CONST, N_CONST + 3)
LEVEL = GT + 1
N_ALL = LEVEL + 2 * LEVELS


def shape_constants():
    r = np.arange(P)[:, None]
    c = np.arange(P)[None, :]
    m = np.zeros((P, N_ALL, P), np.float32)
    m[:, IDENT] = r == c
    m[:, LE] = r <= c
    m[:, GE] = r >= c
    m[:, LT] = r < c
    m[:, GT] = r > c
    m[:, ONES] = 1.0
    for lv in range(LEVELS):
        s = 1 << lv
        off = (r // (2 * s) == c // (2 * s)) & (r % (2 * s) >= s) & (c % (2 * s) < s)
        m[:, LEVEL + lv] = off
        m[:, LEVEL + LEVELS + lv] = off.T
    for kind, seg in enumerate((P, GRID_W)):
        for g, w in enumerate(WINDOWS):
            for t in range(P):
                base = t // seg * seg
                lo, hi = max(t - w // 2, base), min(t - w // 2 + w, base + seg)
                m[lo:hi, POOL + kind * len(WINDOWS) + g, t] = 1.0 / (hi - lo)
                m[t, POOL + kind * len(WINDOWS) + g, t] -= 1.0
    return m


class Ring:

    def __init__(self):
        self.base = 0

    def slot(self, k):
        return (self.base + k) % RING

    def loaded(self, k, i=0, per=0):
        return 32 * ((self.base + k) // RING + 1) + i * (32 * (per // RING))

    def freed(self, k, i=0, per=0):
        return 2 * (self.base + k + 1) + i * (2 * per)


def split_count(k, s, e=0):
    return 2 * k + s + 1 + 2 * RING + e * 36


def half_rows(k, s):
    return 1 if k in (14, 17) and s == 1 else 2


def backbone(nc, A, out_prompt, out_sample, out_state, mod_dram, h_dram, xs_dram, ys_dram, xpark):
    with ExitStack() as ctx:
        def sb(name, shape, dt=F32):
            return ctx.enter_context(nc.sbuf_tensor(name, shape, dt))

        def sem(name):
            return ctx.enter_context(nc.semaphore(name))

        cm = sb("cm", [P, N_CONST, P])
        x = sb("x", [P, T, D])
        wring = sb("wring", [P, RING, 4, 512])
        modcol = sb("modcol", [P, 2, 96])
        scp1 = sb("scp1", [P, 2, KD])
        modcol_in = sb("modcol_in", [96, P])
        condr = sb("condr", [16, P])
        cs = sb("cs", [P, 16])
        convr = sb("convr", [120, P])
        convw = sb("convw", [P, 5, 24])
        wab = sb("wab", [P, KD, 32])
        rw = sb("rw", [P, KD, 8])
        dtb = sb("dtb", [P, 16])
        alog = sb("alog", [P, 16])
        ngb = sb("ngb", [P, P])
        gates5 = sb("gates5", [P, 12, T, 16])
        ss = sb("ss", [P, 8, T])
        mhalf = sb("mhalf", [P, T])
        lnst = sb("lnst", [P, T, 2, 6])
        lnmv = sb("lnmv", [P, T, 2])
        rstd = sb("rstd", [P, 2, T])
        rt = sb("rt", [P, 12, T, 8])
        cnt = sb("cnt", [P, 6, 16])
        tbl = sb("tbl", [P, 2, 16], I32)
        pos = sb("pos", [P, 2, T], I32)
        gates2 = sb("gates2", [P, 2, 2, T])

        ctx_all = ctx
        def stage():
            return ctx_all.enter_context(ExitStack())

        ctx = ExitStack()
        cmd = sb("cmd", [P, N_ALL - N_CONST, P])
        state = sb("state", [P, 2, P])
        state_new = sb("state_new", [P, 2, P])
        vnew = sb("vnew", [P, 2, P])
        zeros = sb("zeros", [P, D])
        xT = sb("xT", [P, KD, NT])
        acc = sb("acc", [P, T, D])
        big = sb("big", [P, KF * NT])
        scratch = sb("scratch", [P, 11556])
        dnrows = sb("dnrows", [P, 6 * NT])
        ctx.close()
        ctx = ExitStack()
        xTh = sb("xTh", [P, KD, NT], F32R)
        xTl = sb("xTl", [P, KD, NT], F32R)
        hTh = sb("hTh", [P, KF, NT], F32R)
        hTl = sb("hTl", [P, KF, NT], F32R)
        whi = sb("whi", [P, HALVES, 2, 512], F32R)
        wlo = sb("wlo", [P, HALVES, 2, 512], F32R)
        hbuf = sb("hbuf", [P, T, 256])
        ybuf = sb("ybuf", [P, T, 512])
        ctx.close()
        ctx = ExitStack()
        rows = sb("rows", [P, 4, D])
        mrows = sb("mrows", [P, 4, D])
        lnt = sb("lnt", [P, T, D])
        hrow = sb("hrow", [P, T, D])
        prow = sb("prow", [P, 2, D])
        pT = sb("pT", [P, 2, D])
        hcol = sb("hcol", [P, KD, NT])
        yA, yB = lnt, hrow
        ctx.close()
        ctx = ctx_all
        xs_stage = x

        def carve(buf, off, n, **dims):
            ap = buf[:, off:off + n]
            if not dims:
                return ap
            names = " ".join(dims)
            return ap.rearrange(f"p ({names}) -> p {names}", **dims)

        early = xT[0:2, :, :].rearrange("p k t -> p (k t)")
        brow = early[:, 0:1536].rearrange("p (b n) -> p b n", b=3)
        mrow = early[:, 1536:3072].rearrange("p (b n) -> p b n", b=3)
        oT = carve(big, 0, H * NT, h=H, t=NT)
        vn_t = carve(big, H * NT, 3 * NT, c=3, t=NT)
        cbuf = carve(scratch, 0, 3 * 648, c=3, t=648)
        offd = carve(scratch, 0, 2 * NT, d=2, t=NT)
        cv = carve(scratch, 1944, 3 * 644, c=3, t=644)
        vt = carve(scratch, 1944, 2 * NT, d=2, t=NT)
        sq = carve(scratch, 3876, 2 * NT, d=2, t=NT)
        inv = sq
        invT = carve(scratch, 5156, 2 * NT, d=2, t=NT)
        qkT = carve(scratch, 6436, 2 * NT, d=2, t=NT)
        kk = carve(scratch, 7716, NT)
        qk = carve(scratch, 8356, NT)
        oacc, og = kk, qk
        gm = carve(scratch, 8996, 4 * NT, j=4, t=NT)
        R = gm
        rowsf = dnrows[:, :]
        ex = rowsf[:, 0:4 * NT].rearrange("p (j t) -> p j t", j=4)

        def per_tile(ap):
            return ap.rearrange("p (t c) -> p t c", t=T)

        qTk = rowsf[:, 4 * NT:6 * NT].rearrange("p (j t) -> p j t", j=2)
        modc = [modcol[:, 0, :], modcol[:, 1, :]]

        def u_all(d):
            return vt[:, d, :]

        def wT(d):
            return inv[:, d, :]

        def kdec(d):
            return ex[:, 2 * d, :]

        PP = [ctx.enter_context(nc.psum_tensor(f"pp{i}", [P, 1024], F32)) for i in range(4)]

        def bank(i):
            return PP[i // 2][:, 512 * (i % 2):512 * (i % 2) + 512]

        names = """consts_in x_in small_in cond_ps cond_ready mod_ps mod_row conv_ps conv_cols
            slot_free modcol_ps modcol_ready scp1_ready xt_ps xt_ready z_ps z_ready ab_ps gate_step
            gate_act cum_ps q_k_v_ps conv_in conv_step silu_done tok_ps sq_done v_ready ss_done rn_step
            qkn head_ps qkT_ready gram_ps gram_sb gm_ready decay_ps ex_ready a_step w_step inv_init
            off_ready vt_ps vt_sb upd_x_ps upd_y_ps inv_upd r_ready kdec_ready u_ps wt_ps u_sb wt_sb
            s_read_ps s_add_ps vn_ready o_upd s_upd sp_ready state_in state_out sqo_done sso_done
            rno_step og_step ogT_ps oT_ready res_ps res_step ln_step ln_rstd rows_in poolrows_in mrows_in
            hp_step poolT_ps poolT_sb pool_ps pool_step logit_ps route_step route_act final_out cbuf_zero
            pool_const gate_arg xs_zero slot_hi rowcount mrow1 hrow_ready h_out xs_scattered x_parked x_back hcol_ps hcol_ready rank_ps tbl_ready y_in comb_step""".split()
        S = {n: sem(n) for n in names}
        slot_loaded = [sem(f"slot_loaded{i}") for i in range(RING)]
        bias_in = [sem(f"bias_in{i}") for i in range(3)]
        mod_out = [sem(f"mod_out{i}") for i in range(3)]
        modcol_in_s = sem("modcol_rows_in")
        F = [{n: sem(f"{n}{l}") for n in ("gu_ps", "sil_done", "h_done", "hT_ps", "hTh_ready", "hTl_ready",
                                          "down_ps", "half_done", "y_copied", "y_out", "xs_in", "xsT_ps",
                                          "xTh_ready", "xTl_ready")} for l in range(2)]
        slot_split = [sem(f"slot_split{l}") for l in range(2)]
        yg_in = [sem(f"yg_in{t}") for t in range(T)]

        def cmat(m, n=0):
            buf, m = (cm, m) if m < N_CONST else (cmd, m - N_CONST)
            return buf[:, m:m + 1, :] if n else buf[:, m, :]

        ring_of = [Ring(), Ring()]
        ring_of[0].base = 48 + 4 + 3 * H + 4
        ring_of[1].base = ring_of[0].base + 36 + 2 + 1

        UNSPLIT = (ring_of[0].base, ring_of[0].base + 1)

        def hi_count(l, m, e=0):
            return (76 if l else 0) + m + 1 + e * 36

        ident = cm[:, IDENT, :]
        block = ctx.enter_context(nc.Block())

        c5 = lambda ap: ap.rearrange("p (a b) -> p a b", b=1) if False else ap

        def col_bc(ap):
            return ap.to_broadcast([P, T, P])

        def mat_bc(m):
            return cmat(m, 1).to_broadcast([P, T, P])

        AB0, SPA, SPB, G_, BETA, EG, EK, EL, BG, TMP, NA, T2 = range(12)

        def gcol(which, d, hd):
            return gates5[:, which, :, bass.ds(hd + 8 * d, 1)]

        LN_STEPS = 8
        ROUTE_SEL = 23

        @block.sync
        def _(sp):
            ring = Ring()
            sp.dma_start(cm[:, :, :], A["consts"][:, 0:N_CONST, :]).then_inc(S["consts_in"], 16)
            sp.dma_start(cmd[:, :, :], A["consts"][:, N_CONST:, :]).then_inc(S["consts_in"], 16)
            sp.dma_start(condr[0:8, :], A["c_ctx"].rearrange("(k p) -> k p", p=P)).then_inc(S["small_in"], 16)
            sp.dma_start(condr[8:16, :], A["c"][0].rearrange("(k p) -> k p", p=P)).then_inc(S["small_in"], 16)
            sp.dma_start(convr[:, :], A["dn_conv"][0].rearrange("j (c p) -> (j c) p", p=P)).then_inc(S["small_in"], 16)

            def fill(k, parts, i=0, per=0, l=None):
                if l is None:
                    sp.wait_ge(S["slot_free"], ring.freed(k, i, per))
                else:
                    sp.wait_ge(slot_split[l], 2 * (k + 1) + i * (2 * per))
                for dst, src in parts(ring.slot(k)):
                    sp.dma_start(dst, src).then_inc(slot_loaded[ring.slot(k)], 16)

            def cols512(w, k0, nk, c0):
                wv = w.rearrange("(k p) n -> p k n", p=P)
                a = (nk + 1) // 2

                def parts(s):
                    return [(wring[:, s, 0:a, :], wv[:, k0:k0 + a, bass.ds(c0, 512)]),
                            (wring[:, s, a:nk, :], wv[:, k0 + a:k0 + nk, bass.ds(c0, 512)])]
                return parts

            for layer in range(2):
                with sp.Fori(0, 4) as i:
                    for k in range(6):
                        fill(k, cols512(A["ada_w"][layer], 4 * (k % 2), 4, i * 1536 + 512 * (k // 2)), i, 6)
                ring.base += 24
                if layer == 0:
                    sp.dma_start(x[:, 0, :], A["x_prompt"][0]).then_inc(S["x_in"], 16)
                    sp.dma_start(x[:, 1:T, :], A["x_sample"][0].rearrange("(t p) d -> p t d", p=P)).then_inc(S["x_in"], 16)
                    sp.dma_start(wab[:, :, :], A["dn_w_in"][0].rearrange("(k p) n -> p k n", p=P)[:, :, 4096:4128]).then_inc(S["small_in"], 16)
                    sp.dma_start(rw[:, :, :], A["moe_router"][0].rearrange("(k p) n -> p k n", p=P)).then_inc(S["small_in"], 16)
                    sp.dma_start(dtb[:, :], A["dn_dt_bias"][0].rearrange("d h -> (d h)").partition_broadcast(P)).then_inc(S["small_in"], 16)
                    sp.dma_start(alog[:, :], A["dn_a_log"][0].rearrange("d h -> (d h)").partition_broadcast(P)).then_inc(S["small_in"], 16)
                    sp.dma_start(ngb[:, :], A["dn_norm_g"][0].partition_broadcast(P)).then_inc(S["small_in"], 16)
            for k in range(4):
                fill(k, cols512(A["dn_w_in"][0], 4 * (k % 2), 4, 3072 + 512 * (k // 2)))
            ring.base += 4
            w_in = A["dn_w_in"][0].rearrange("(k p) n -> p k n", p=P)
            with sp.Fori(0, H) as hd:
                for c in range(3):
                    def parts(s, c=c):
                        dst = wring[:, s, 0:2, :].rearrange("p a (b n) -> p (a b) n", n=P)
                        return [(dst[:, 4 * a:4 * a + 4, :], w_in[:, 4 * a:4 * a + 4, bass.ds(hd * P + D * c, P)])
                                for a in range(2)]
                    fill(c, parts, hd, 3)
            ring.base += 3 * H
            for k in range(4):
                fill(k, cols512(A["dn_w_out"][0], 4 * (k % 2), 4, 512 * (k // 2)))
            ring.base += 4

            def expert_fills(l, e, gate_w, down_w, up_off):
                gv = gate_w.rearrange("(k p) n -> p k n", p=P)
                for j in range(6):
                    w = 256 if j < 5 else 128
                    for a in range(2):
                        def parts(s, j=j, w=w, a=a):
                            return [(wring[:, s, 0:4, w * u:w * u + w],
                                     gv[:, 4 * a:4 * a + 4, bass.ds(up_off[u] + 256 * j, w)]) for u in range(2)]
                        fill(2 * j + a, parts, e, 18, l)
                for n in range(2):
                    for a in range(3):
                        nk = 4 if a < 2 else 3
                        fill(12 + 3 * n + a, cols512(down_w, 4 * a, nk, 512 * n), e, 18, l)

            wd = A["ffn_w_down"][0].rearrange("(e f) d -> e f d", f=FE)
            gu0, gu1 = A["ffn_w_gu"][0], A["moe_w_gu"][0]

            def read_ahead(l, w):
                for k in range(2):
                    sp.wait_ge(slot_split[l], 2 * (k + 1) + 36 * (8 if l else 2))
                    for dst, src in cols512(w, 4 * k, 4, 0)(ring.slot(k)):
                        sp.dma_start(dst, src).then_inc(slot_loaded[ring.slot(k)], 16)
                ring.base += 2

            def park(l):
                sp.wait_ge(S["slot_free"], 2 * UNSPLIT[l] + 2 * RING)
                sp.wait_ge(S["hrow_ready"], 2 * T * (1 + 2 * l))
                if l == 0:
                    sp.dma_start(h_dram.rearrange("(t p) d -> p t d", p=P), hrow[:, :, :]).then_inc(S["h_out"], 16)
                sp.dma_start(xpark.rearrange("(t p) d -> p t d", p=P), x[:, :, :]).then_inc(S["x_parked"], 16)

            def unpark(l):
                f = F[l]
                if l == 0:
                    last = 30
                else:
                    last = sp.value_load(tbl[0:1, 1, 9:10], min_val=9, max_val=SLOTS) * 2
                sp.wait_ge(f["xsT_ps"], last)
                sp.wait_ge(S["x_parked"], 16 * (l + 1))
                sp.dma_start(x[:, :, :], xpark.rearrange("(t p) d -> p t d", p=P)).then_inc(S["x_back"], 16)

            park(0)
            with sp.Fori(0, 2) as e:
                expert_fills(0, e, gu0, wd[bass.ds(e, 1)].rearrange("a f d -> (a f) d"), (e * FE, e * FE + 2 * FE))
            ring.base += 36
            read_ahead(0, gu0)
            unpark(0)
            wp = A["pool_w"][0].rearrange("g (k p) n -> p (g k) n", p=P)

            def parts(s):
                dst = wring[:, s, :, :].rearrange("p a (b n) -> p (a b) n", n=256)
                return [(dst[:, 4 * a:4 * a + 4, :], wp[:, 4 * a:4 * a + 4, :]) for a in range(2)]
            sp.wait_ge(slot_split[0], 2 * 38 + 2 * RING)
            for dst, src in parts(ring.slot(0)):
                sp.dma_start(dst, src).then_inc(slot_loaded[ring.slot(0)], 16)
            ring.base += 1
            park(1)
            with sp.Fori(0, 8) as e:
                expert_fills(1, e, gu1[bass.ds(e, 1)].rearrange("a k n -> (a k) n"),
                             A["moe_w_down"][0][bass.ds(e, 1)].rearrange("a f d -> (a f) d"), (0, FE))
            ring.base += 144
            read_ahead(1, gu1[0])
            unpark(1)
            sp.wait_ge(S["ln_step"], 4 * T * LN_STEPS)
            sp.dma_start(out_prompt[0], x[:, 0, :]).then_inc(S["final_out"], 16)
            sp.dma_start(out_sample[0].rearrange("(t p) d -> p t d", p=P), x[:, 1:T, :]).then_inc(S["final_out"], 16)
            sp.wait_ge(S["final_out"], 32)

        @block.tensor
        def _(pe):
            ring = Ring()
            pe.sem_inc(S["slot_free"], 2 * RING)

            def slot(k, i=0, per=0):
                pe.wait_ge(slot_loaded[ring.slot(k)], ring.loaded(k, i, per))
                return ring.slot(k)

            def gemm5(k, nk, lhs, c0, first, last, done, i=0, per=0, n=512, free=None):
                s = slot(k, i, per)
                for t in range(T):
                    if first and free is not None:
                        free(t)
                    for kk_ in range(nk):
                        mm = pe.matmul(bank(t)[:, 0:n], lhs(c0 + kk_, t), wring[:, s, kk_, 0:n],
                                       start=(first and kk_ == 0), stop=(last and kk_ == nk - 1))
                    if last:
                        mm.then_inc(done, 1)
                if not last:
                    mm.then_inc(S["slot_free"], 2)

            pe.wait_ge(S["consts_in"], 32)
            pe.wait_ge(S["small_in"], 48)
            pe.transpose(PP[3][:, 0:16], condr[:, :], ident[0:16, 0:16]).then_inc(S["cond_ps"], 1)
            pe.transpose(PP[3][:, 512:632], convr[:, :], ident[0:120, 0:120]).then_inc(S["conv_ps"], 1)
            pe.wait_ge(S["cond_ready"], 1)
            csv = cs[:, :].rearrange("p (r k) -> p k r", r=2)
            for layer in range(2):
                with pe.Fori(0, 4) as i:
                    for b in range(3):
                        pe.wait_ge(S["mod_row"], i * 3 + (12 * layer + b + 1))
                        for a in range(2):
                            s = slot(2 * b + a, i, 6)
                            for k in range(4):
                                mm = pe.matmul(bank(b)[0:2, :], csv[:, 4 * a + k, :], wring[:, s, k, :],
                                               start=(a == 0 and k == 0), stop=(a == 1 and k == 3))
                            mm.then_inc(S["slot_free" if a == 0 else "mod_ps"], 2 if a == 0 else 1)
                        pe.wait_ge(S["mod_ps"], i * 3 + (12 * layer + b + 1))
                        pe.sem_inc(S["slot_free"], 2)
                ring.base += 24
            for layer in range(2):
                pe.wait_ge(modcol_in_s, 16 * (layer + 1))
                if layer:
                    pe.wait_ge(S["modcol_ready"], 1)
                else:
                    pe.wait_ge(S["conv_cols"], 1)
                pe.transpose(PP[3][:, 0:96], modcol_in[:, :], ident[0:96, 0:96]).then_inc(S["modcol_ps"], 1)
            def transpose_x():
                pe.wait_ge(S["x_in"], 32)
                for t in range(T):
                    if t >= 4:
                        pe.wait_ge(S["xt_ready"], 2 * (t - 3))
                    for k in range(KD):
                        mm = pe.transpose(PP[t % 4][:, k * P:(k + 1) * P], x[:, t, k * P:(k + 1) * P], ident)
                    mm.then_inc(S["xt_ps"], 1)

            pe.wait_ge(S["modcol_ready"], 2)
            transpose_x()

            def lhs_x(k, t):
                return xT[:, k, t * P:(t + 1) * P]

            def lhs_o(k, t):
                return oT[:, k, t * P:(t + 1) * P]

            pe.wait_ge(S["xt_ready"], 2 * T)
            pe.wait_ge(S["small_in"], 16 * 8)
            for t in range(T):
                for k in range(KD):
                    mm = pe.matmul(bank(6)[:, 32 * t:32 * t + 32], lhs_x(k, t), wab[:, k, :],
                                   start=(k == 0), stop=(k == KD - 1))
            mm.then_inc(S["ab_ps"], 1)
            for n in range(2):
                for a in range(2):
                    gemm5(2 * n + a, 4, lhs_x, 4 * a, a == 0, a == 1, S["z_ps"],
                          free=(lambda t: pe.wait_ge(S["z_ready"], t + 1)) if n else None)
                pe.wait_ge(S["z_ps"], T * (n + 1))
                pe.sem_inc(S["slot_free"], 2)
            ring.base += 4
            pe.wait_ge(S["gate_step"], 8)
            gf, gb = gates5[:, G_, :, 0:8], gates5[:, G_, :, 8:16]
            cum = bank(7)[:, 0:240].rearrange("p (s t h) -> p s t h", s=3, h=16)
            for kind, (mf, mb) in enumerate(((LE, GE), (GT, LT), (ONES, ONES))):
                pe.matmul(cum[:, kind, :, 0:8], cmat(mf), gf, start=True, stop=True)
                mm = pe.matmul(cum[:, kind, :, 8:16], cmat(mb), gb, start=True, stop=True)
            mm.then_inc(S["cum_ps"], 1)

            def tiles(j):
                return slice(j * P, (j + 1) * P)

            def mm5(dst, lhs, rhs, sig, n):
                for t in range(T):
                    mm = pe.matmul(dst[:, tiles(t)], lhs(t), rhs(t), start=True, stop=True)
                mm.then_inc(S[sig], 1)

            with pe.Fori(0, H) as hd:
                pe.wait_ge(S["oT_ready"], hd + 1)
                for c in range(3):
                    s = slot(c, hd, 3)
                    w = wring[:, s, 0:2, :].rearrange("p a (b n) -> p (a b) n", n=P)
                    for lo, hi in ((0, 512), (512, NT)):
                        for k in range(KD):
                            mm = pe.matmul(PP[c][:, lo:hi], w[:, k, :], xT[:, k, lo:hi],
                                           start=(k == 0), stop=(k == KD - 1))
                    mm.then_inc(S["q_k_v_ps"], 1)
                    pe.wait_ge(S["q_k_v_ps"], hd * 3 + (c + 1))
                    pe.sem_inc(S["slot_free"], 2)
                for c in range(3):
                    pe.wait_ge(S["silu_done"], hd * 3 + (c + 1))
                    for t in range(T):
                        o = 0 if t == 0 else 132 + (t - 1) * P
                        mm = pe.transpose(PP[c][:, tiles(t)], cv[:, c, o:o + P], ident)
                    mm.then_inc(S["tok_ps"], 1)
                for c in range(2):
                    pe.wait_ge(S["qkn"], hd * 2 + (c + 1))
                    for t in range(T):
                        mm = pe.transpose(PP[c][:, tiles(t)], vn_t[:, c, tiles(t)], ident)
                    mm.then_inc(S["head_ps"], 1)
                pe.wait_ge(S["qkT_ready"], hd * 2 + 2)
                pe.wait_ge(S["v_ready"], hd + 1)
                qTv, kTv = ex[:, 0, :], ex[:, 1, :]
                qT, kT = qTk[:, 0, :], qTk[:, 1, :]
                mm5(PP[2], lambda t: kT[:, tiles(t)], lambda t: kT[:, tiles(t)], "gram_ps", 1)
                mm5(PP[3], lambda t: kT[:, tiles(t)], lambda t: qT[:, tiles(t)], "gram_ps", 1)
                for j, m in enumerate((LE, GT, GE, LT)):
                    pe.wait_ge(S["gm_ready"], hd * 4 + (j + 1))
                    if j >= 2:
                        pe.wait_ge(S["gram_sb"], hd * 2 + (j - 1))
                    pe.matmul(PP[j][:, 0:512], cmat(m), gm[:, j, 0:512], start=True, stop=True)
                    pe.matmul(PP[j][:, 512:NT], cmat(m), gm[:, j, 512:NT], start=True, stop=True)\
                        .then_inc(S["decay_ps"], 1)

                def vt_level(n):
                    d = n % 2
                    pe.wait_ge(S["off_ready"], hd * 14 + (n + 1))
                    if n < 2:
                        pe.wait_ge(S["inv_init"], hd * 4 + 4)
                        pe.wait_ge(S["ex_ready"], hd * 4 + 4)
                    else:
                        pe.wait_ge(S["inv_upd"], hd * 28 + 2 * (n - 1))
                    mm5(PP[d], lambda t: offd[:, d, tiles(t)], lambda t: invT[:, d, tiles(t)], "vt_ps", 1)

                def xy_level(n):
                    d = n % 2
                    pe.wait_ge(S["vt_sb"], hd * 14 + (n + 1))
                    mm5(PP[d], lambda t: inv[:, d, tiles(t)], lambda t: vt[:, d, tiles(t)], "upd_x_ps", 1)
                    mm5(PP[2 + d], lambda t: vt[:, d, tiles(t)], lambda t: inv[:, d, tiles(t)], "upd_y_ps", 1)

                for lv in range(LEVELS):
                    for d in range(2):
                        vt_level(2 * lv + d)
                    for d in range(2):
                        xy_level(2 * lv + d)
                for d in range(2):
                    pe.wait_ge(S["inv_upd"], hd * 28 + (26 + 2 * d))
                    pe.wait_ge(S["r_ready"], hd * 4 + 4)
                    mm5(PP[d], lambda t: invT[:, d, tiles(t)], lambda t: R[:, d, tiles(t)], "u_ps", 1)
                    mm5(PP[2 + d], lambda t: R[:, 2 + d, tiles(t)], lambda t: invT[:, d, tiles(t)], "wt_ps", 1)
                pe.wait_ge(S["u_sb"], hd * 2 + 2)
                pe.wait_ge(S["wt_sb"], hd * 2 + 2)
                pe.wait_ge(S["kdec_ready"], hd * 2 + 2)
                for k in range(T):
                    for d in range(2):
                        tt = tiles(k if d == 0 or k == 0 else T - k)
                        if k:
                            if k == 1:
                                pe.wait_ge(S["state_in"], hd * 32 + 32)
                            else:
                                pe.wait_ge(S["s_upd"], hd * 6 + (2 * (k - 2) + d + 1))
                            pe.wait_ge(S["o_upd"], hd * 19 + (1 + 2 + 4 * (k - 1)))
                            pe.matmul(bank(4 * d)[:, 0:P], wT(d)[:, tt], state[:, d, :], start=True, stop=True)
                            pe.matmul(bank(4 * d + 1)[:, 0:P], qT[:, tt], state[:, d, :], start=True, stop=True)\
                                .then_inc(S["s_read_ps"], 1)
                    for d in range(2):
                        tt = tiles(k if d == 0 or k == 0 else T - k)
                        if k:
                            pe.wait_ge(S["vn_ready"], hd * 8 + (2 * (k - 1) + d + 1))
                            if k == 1:
                                pe.wait_ge(S["sp_ready"], hd * 2 + (d + 1))
                        rhs = vnew[:, d, :] if k else u_all(d)[:, tt]
                        pe.matmul(bank(4 * d + 2)[:, 0:P], kdec(d)[:, tt], rhs, start=True, stop=True)
                        pe.matmul(bank(4 * d + 3)[:, 0:P], qkT[:, d, tt], rhs, start=True, stop=True)\
                            .then_inc(S["s_add_ps"], 1)
                pe.wait_ge(S["og_step"], hd * 3 + 3)
                mm5_t = [pe.transpose(PP[0][:, tiles(t)], og[:, tiles(t)], ident) for t in range(T)]
                mm5_t[-1].then_inc(S["ogT_ps"], 1)
            ring.base += 3 * H

            pe.wait_ge(S["oT_ready"], H + 1)
            for n in range(2):
                for a in range(2):
                    gemm5(2 * n + a, 4, lhs_o, 4 * a, a == 0, a == 1, S["res_ps"],
                          free=(lambda t: pe.wait_ge(S["res_step"], 2 * (t + 1))) if n else None)
                pe.wait_ge(S["res_ps"], T * (n + 1))
                pe.sem_inc(S["slot_free"], 2)
            ring.base += 4

            def ffn(l):
                f = F[l]

                def xs_group(i, t, g, b):
                    pe.wait_ge(f["xTl_ready"], 2 * (i + t) + (g + 1))
                    for k in range(4):
                        mm = pe.transpose(bank(b)[:, k * P:(k + 1) * P],
                                          xs_stage[:, t, (4 * g + k) * P:(4 * g + k + 1) * P], ident)
                    mm.then_inc(f["xsT_ps"], 1)

                def h_group(q, j, t):
                    pe.wait_ge(f["h_done"], q + 1)
                    pe.wait_ge(f["hTl_ready"], q + 1)
                    for c in range(2 if j < 5 else 1):
                        mm = pe.transpose(bank(7)[:, c * P:(c + 1) * P], hbuf[:, t, c * P:(c + 1) * P], ident)
                    mm.then_inc(f["hT_ps"], 1)

                def nest(n, body, t=0):
                    body(t)
                    if t + 1 < T:
                        if isinstance(n, int):
                            nest(n, body, t + 1)
                        else:
                            with pe.If(n > t + 1):
                                nest(n, body, t + 1)

                def half(e, m, n, hi, lo, c0, bk, first, last, done, width, free, after=None):
                    k, s = m // 2, m % 2
                    nk = half_rows(k, s)
                    pe.wait_ge(slot_split[l], split_count(k, s, e))
                    hs = (2 * ring0 + m) % HALVES

                    def tile(t):
                        if first:
                            free(t)
                        tt = slice(t * P, (t + 1) * P)
                        for c in range(nk):
                            wh, wl = whi[:, hs, c, 0:width], wlo[:, hs, c, 0:width]
                            out = bank(bk(t))[:, 0:width]
                            pe.matmul(out, hi[:, c0 + c, tt], wh, start=(first and c == 0), stop=False)
                            pe.matmul(out, lo[:, c0 + c, tt], wh, start=False, stop=False)
                            mm = pe.matmul(out, hi[:, c0 + c, tt], wl, start=False, stop=(last and c == nk - 1))
                        mm.then_inc(done if last else f["half_done"], 1)
                        if after is not None:
                            after(t)
                    nest(n, tile)

                ring0 = 0
                if l == 0:
                    n0 = T
                else:
                    pe.wait_ge(S["tbl_ready"], 1)
                    n0 = pe.value_load(tbl[0:1, 0, 0:1], min_val=1, max_val=T)
                pe.wait_ge(f["xs_in"], n0 * 16)
                for g in range(2):
                    xs_group(0, 0, g, 6 + g)
                for t in range(1, T):
                    if l == 0:
                        for g in range(2):
                            xs_group(0, t, g, 6 + g)
                    else:
                        with pe.If(n0 > t):
                            for g in range(2):
                                xs_group(0, t, g, 6 + g)

                with pe.Fori(0, 8 if l else 2) as e:
                    if l:
                        n = pe.value_load(tbl[0:1, 0, bass.ds(e, 1)], min_val=1, max_val=T)
                        n2 = pe.value_load(tbl[0:1, 0, bass.ds(e + 1, 1)], min_val=1, max_val=T)
                        c = pe.value_load(tbl[0:1, 1, bass.ds(e, 1)], min_val=0, max_val=SLOTS)
                    else:
                        n, n2, c = T, T, e * T
                    pe.wait_ge(f["xTl_ready"], (c + n) * 2 + 1)
                    for j in range(6):
                        bk = (lambda t, j=j: t if j % 2 == 0 or t > 1 else 5 + t)
                        if j == 0:
                            free = lambda t: pe.wait_ge(f["y_copied"], c * 2 + 1)
                        else:
                            free = lambda t, j=j: pe.wait_ge(
                                f["h_done"], c * 6 + n * (j - 1 if t > 1 else max(0, j - 2)) + (t + 1 if t > 1 or j > 1 else 1))
                        for s in range(4):
                            after = None
                            if s == 1 and j:
                                after = lambda t, j=j: h_group(c * 6 + n * (j - 1) + t, j - 1, t)
                            half(e, 4 * j + s, n, xTh, xTl, 2 * s, bk, s == 0, s == 3, f["gu_ps"],
                                 512 if j < 5 else 256, free, after)
                    pe.wait_ge(f["xs_in"], (c + n + n2) * 16)
                    for a in range(2):
                        bk = (lambda t, a=a: t if a == 0 or t > 1 else 5 + t)
                        free = (lambda t: pe.wait_ge(f["y_copied"], c * 2 + (t + 2))) if a else \
                            (lambda t: pe.wait_ge(f["h_done"], c * 6 + n * 5 + (t + 1)) if t > 1 else None)
                        for s in range(6):
                            m = 6 * a + s
                            if a == 0 and s == 0:
                                pe.wait_ge(f["hTl_ready"], c * 6 + n * 5 + 1)
                            after = (lambda t: h_group(c * 6 + n * 5 + t, 5, t)) if m == 1 else None
                            half(e, 24 + m, n, hTh, hTl, 2 * s, bk, s == 0, s == 5, f["down_ps"], 512,
                                 free if a == 0 else (lambda t: free(t) if t > 1 else None), after)
                            if m == 2:
                                pe.wait_ge(f["hTl_ready"], c * 6 + n * 6 + 1)
                            if m >= 2:
                                t2, g = (m - 2) // 2, m % 2
                                if t2 == 0 or l == 0:
                                    xs_group(c + n, t2, g, 7)
                                else:
                                    with pe.If(n2 > t2):
                                        xs_group(c + n, t2, g, 7)
                ring.base += 18 * (8 if l else 2) + 2

            ffn(0)
            s = slot(0)
            wpv = wring[:, s, :, :].rearrange("p a (b n) -> p (a b) n", n=256)
            hp = hrow
            for t in range(T):
                kind = POOL + (len(WINDOWS) if t else 0)
                pe.wait_ge(S["hrow_ready"], 2 * (T + t + 1))
                if t >= 2:
                    pe.wait_ge(S["poolT_sb"], t - 1)
                for k in range(KD):
                    mm = pe.matmul(PP[t % 2][:, k * P:(k + 1) * P], hp[:, t, k * P:(k + 1) * P],
                                   cm[:, kind + k // 2, :], start=True, stop=True)
                mm.then_inc(S["poolT_ps"], 1)
                pe.wait_ge(S["poolT_sb"], t + 1)
                if t >= 2:
                    pe.wait_ge(S["pool_step"], 5 * (t - 1))
                for g in range(4):
                    for k in range(2):
                        mm = pe.matmul(PP[2 + t % 2][:, g * 256:(g + 1) * 256],
                                       pT[:, t % 2, (2 * g + k) * P:(2 * g + k + 1) * P],
                                       wpv[:, 2 * g + k, :], start=(k == 0), stop=(k == 1))
                mm.then_inc(S["pool_ps"], 1)
            pe.wait_ge(S["pool_ps"], T)
            pe.sem_inc(S["slot_free"], 2)
            ring.base += 1
            for t in range(T):
                pe.wait_ge(S["hrow_ready"], 2 * (2 * T + t + 1))
                if t >= 2:
                    pe.wait_ge(S["hcol_ready"], t - 1)
                for k in range(KD):
                    mm = pe.transpose(PP[t % 2][:, k * P:(k + 1) * P], hrow[:, t, k * P:(k + 1) * P], ident)
                mm.then_inc(S["hcol_ps"], 1)
            pe.wait_ge(S["hcol_ready"], T)
            for t in range(T):
                for k in range(KD):
                    mm = pe.matmul(bank(4)[:, 8 * t:8 * t + 8], hcol[:, k, t * P:(t + 1) * P], rw[:, k, :],
                                   start=(k == 0), stop=(k == KD - 1))
            mm.then_inc(S["logit_ps"], 1)
            pe.wait_ge(S["route_step"], ROUTE_SEL)
            for i, m in enumerate((LT, ONES)):
                mm = pe.matmul(bank(5)[:, 40 * i:40 * i + 40], cmat(m), rt[:, 10, :, :], start=True, stop=True)
            mm.then_inc(S["rank_ps"], 1)
            ffn(1)

        @block.gpsimd
        def _(pool):
            pool.memset(mhalf[:, :], -0.5).then_inc(S["pool_const"], 1)
            pool.memset(cbuf, 0.0).then_inc(S["cbuf_zero"], 1)
            pool.memset(zeros[:, :], 0.0).then_inc(S["pool_const"], 1)
            pool.wait_ge(S["pool_const"], 1)

            def load_rows(n, layer, which, ln):
                for r in range(2):
                    pool.dma_start(rows[:, r, :], mod_dram[layer, r, which * D:(which + 1) * D].partition_broadcast(P))\
                        .then_inc(S["rows_in"], 16)
                pool.dma_start(rows[:, 2, :], A["ln_g"][layer, ln].partition_broadcast(P)).then_inc(S["rows_in"], 16)
                pool.dma_start(rows[:, 3, :], A["ln_b"][layer, ln].partition_broadcast(P)).then_inc(S["rows_in"], 16)

            def load_mod_rows(layer, sub):
                for r in range(2):
                    for i in range(2):
                        w = 3 * sub + 1 - i
                        pool.dma_start(mrows[:, 2 * i + r, :], mod_dram[layer, r, w * D:(w + 1) * D].partition_broadcast(P))\
                            .then_inc(S["mrows_in"], 16)

            def low_halves(l):
                ring_p = ring_of[l]

                def low(k, s, e=0, per=0):
                    nk = half_rows(k, s)
                    w = 256 if k in (10, 11) else 512
                    hs = (2 * k + s) % HALVES
                    pool.wait_ge(S["slot_hi"], hi_count(l, 2 * k + s, e))
                    pool.tensor_tensor(wlo[:, hs, 0:nk, 0:w], wring[:, ring_p.slot(k), 2 * s:2 * s + nk, 0:w],
                                       whi[:, hs, 0:nk, 0:w].bitcast(F32), ALU.subtract).then_inc(slot_split[l], 1)
                with pool.Fori(0, 8 if l else 2) as e:
                    for k in range(18):
                        for s in range(2):
                            low(k, s, e, 18)
                ring_p = Ring()
                ring_p.base = ring_of[l].base
                for k in range(2):
                    for s in range(2):
                        low(k, s, 8 if l else 2)

            def rstds(n):
                for t in range(T):
                    m = n * T + t
                    pool.wait_ge(S["ln_step"], (m * LN_STEPS) + 3)
                    pool.tensor_scalar(rstd[:, 0, t:t + 1], lnmv[:, t, 1:2], EPS, None, ALU.add).then_inc(S["ln_rstd"], 1)
                    pool.wait_ge(S["ln_rstd"], 2 * m + 1)
                    pool.tensor_tensor(rstd[:, 1, t:t + 1], rstd[:, 0, t:t + 1], mhalf[:, 0:1], ALU.pow).then_inc(S["ln_rstd"], 1)

            for l in range(2):
                pool.sem_inc(slot_split[l], 2 * RING)
            pool.wait_ge(S["pool_const"], 2)
            for b in range(3):
                pool.wait_ge(mod_out[b], 16 * 8 + 1)
            pool.dma_start(modcol_in[:, :], mod_dram[0].rearrange("r (a p) -> (r a) p", p=P)).then_inc(modcol_in_s, 16)
            pool.wait_ge(S["modcol_ready"], 1)
            pool.dma_start(modcol_in[:, :], mod_dram[1].rearrange("r (a p) -> (r a) p", p=P)).then_inc(modcol_in_s, 16)
            zrow = zeros[:, :].rearrange("p (o d) -> p o d", o=1)
            pool.dma_start(xs_dram.rearrange("(t p) d -> p t d", p=P), zrow.to_broadcast([P, SLOTS, D])).then_inc(S["xs_zero"], 16)
            pool.dma_start(ys_dram.rearrange("(t p) d -> p t d", p=P)[:, 2 * T:, :], zrow.to_broadcast([P, SLOTS - 2 * T, D]))\
                .then_inc(S["xs_zero"], 16)

            with pool.Fori(0, H) as hd:
                pool.wait_ge(S["oT_ready"], hd + 1)
                pool.wait_ge(S["gate_step"], 8)
                for j, (m, d) in enumerate(((GT, 0), (LE, 0), (LT, 1), (GE, 1))):
                    pool.tensor_tensor(per_tile(gm[:, j, :]), mat_bc(m), col_bc(gcol(G_, d, hd)), ALU.mult)\
                        .then_inc(S["gm_ready"], 1)
                for c in range(2):
                    pool.wait_ge(S["ss_done"], hd * 4 + 2 * (c + 1))
                    pool.tensor_tensor(ss[:, 4 + c, :], ss[:, 2 + c, :], mhalf[:, :], ALU.pow).then_inc(S["rn_step"], 1)
                for d in range(2):
                    for dst in (inv, invT):
                        pool.tensor_tensor(per_tile(dst[:, d, :]), mat_bc(IDENT), mat_bc(ONES), ALU.mult)\
                            .then_inc(S["inv_init"], 1)
                for n in range(2 * LEVELS):
                    lv, d = n // 2, n % 2
                    pool.wait_ge(S["a_step"], hd * 4 + (2 * d + 2))
                    if n < 2:
                        pool.wait_ge(S["conv_step"], hd * 15 + 15)
                    else:
                        pool.wait_ge(S["vt_ps"], hd * 14 + (n - 1))
                    pool.tensor_tensor(per_tile(offd[:, d, :]), per_tile(ex[:, 2 * d, :]),
                                       mat_bc(LEVEL + LEVELS * d + lv), ALU.mult).then_inc(S["off_ready"], 1)
                pool.wait_ge(S["decay_ps"], hd * 4 + 4)
                pool.wait_ge(S["v_ready"], hd + 1)
                for d in range(2):
                    pool.tensor_tensor(per_tile(R[:, d, :]), per_tile(vn_t[:, 2, :]), col_bc(gcol(BETA, d, hd)), ALU.mult)\
                        .then_inc(S["r_ready"], 1)
                for d in range(2):
                    pool.tensor_tensor(per_tile(R[:, 2 + d, :]), per_tile(vn_t[:, 1, :]), col_bc(gcol(BG, d, hd)), ALU.mult)\
                        .then_inc(S["r_ready"], 1)
                for d in range(2):
                    pool.wait_ge(S["off_ready"], hd * 14 + 14)
                    pool.tensor_tensor(per_tile(kdec(d)), per_tile(vn_t[:, 1, :]), col_bc(gcol(EK, d, hd)), ALU.mult)\
                        .then_inc(S["kdec_ready"], 1)
                pool.wait_ge(S["sso_done"], hd * 2 + 2)
                pool.tensor_tensor(ss[:, 7, :], ss[:, 6, :], mhalf[:, :], ALU.pow).then_inc(S["rno_step"], 1)

            pool.wait_ge(S["xs_zero"], 32)
            pool.wait_ge(S["oT_ready"], H + 1)
            pool.wait_ge(S["state_out"], 32 * H + 1)
            load_rows(0, 0, 2, 0)
            load_mod_rows(0, 1)
            rstds(0)
            pool.wait_ge(S["h_out"], 16)
            pool.wait_ge(S["x_parked"], 16)
            low_halves(0)

            def combine_loads(l):
                if l:
                    pool.wait_ge(S["tbl_ready"], 1)
                    total = pool.value_load(tbl[0:1, 1, 8:9], min_val=8, max_val=SLOTS - 1)
                    ahead = pool.value_load(tbl[0:1, 1, 9:10], min_val=9, max_val=SLOTS) * 2 + 1
                else:
                    ahead = 31
                pool.wait_ge(F[l]["xTl_ready"], ahead)
                pool.wait_ge(slot_split[l], 2 * (146 if l else 38) + 2 * RING)
                if l == 0:
                    pool.wait_ge(F[0]["y_out"], 16 * 20 + 1)
                else:
                    pool.wait_ge(F[1]["y_out"], total * 32 + 1)
                    pool.sem_inc(S["y_in"], 1)
                    pool.wait_ge(S["y_in"], 1)
                for t in range(T):
                    for i, dst in enumerate((yA, yB)):
                        if l == 0:
                            pool.dma_start(dst[:, t, :], ys_dram[(i * T + t) * P:(i * T + t + 1) * P, :])\
                                .then_inc(yg_in[t], 16)
                        else:
                            pool.indirect_dma_start(dst[:, t, :], None, ys_dram[:, :],
                                                    bass.IndirectOffsetOnAxis(ap=pos[:, i, t:t + 1].bitcast(U32), axis=0))\
                                .then_inc(yg_in[t], 16)

            combine_loads(0)
            load_rows(1, 0, 5, 1)
            load_mod_rows(1, 0)
            pool.dma_start(prow[:, 0, :], A["pool_b"][0].partition_broadcast(P)).then_inc(S["poolrows_in"], 16)
            pool.dma_start(prow[:, 1, :], A["pool_scale"][0].partition_broadcast(P)).then_inc(S["poolrows_in"], 16)
            rstds(1)
            pool.wait_ge(S["ln_step"], 2 * T * LN_STEPS)
            load_rows(2, 1, 2, 0)
            pool.wait_ge(S["hrow_ready"], 4 * T)
            load_mod_rows(1, 1)
            rstds(2)
            pool.wait_ge(S["tbl_ready"], 1)
            pool.wait_ge(S["hrow_ready"], 6 * T)
            for t in range(T):
                for i in range(2):
                    pool.indirect_dma_start(xs_dram[:, :], bass.IndirectOffsetOnAxis(ap=pos[:, i, t:t + 1].bitcast(U32), axis=0),
                                            hrow[:, t, :], None).then_inc(S["xs_scattered"], 16)
            pool.wait_ge(S["xs_scattered"], 160)
            pool.wait_ge(S["x_parked"], 32)
            low_halves(1)
            combine_loads(1)
            load_rows(3, 1, 5, 1)
            rstds(3)

        @block.scalar
        def _(act):
            act.sem_inc(S["oT_ready"], 1)
            act.sem_inc(S["state_out"], 1)
            for b in range(3):
                act.sem_inc(mod_out[b], 1)
            for l in range(2):
                for n in ("hTh_ready", "xTh_ready", "y_copied", "y_out"):
                    act.sem_inc(F[l][n], 1)
            act.wait_ge(S["cond_ps"], 1)
            act.activation(cs[:, :], PP[3][:, 0:16], ACT.Silu).then_inc(S["cond_ready"], 1)
            for layer in range(2):
                bv = A["ada_b"][layer]
                with act.Fori(0, 4) as i:
                    for b in range(3):
                        act.wait_ge(S["mod_row"], i * 3 + (12 * layer + b + 1))
                        act.dma_start(brow[:, b, :], bv[bass.ds(i * 1536 + 512 * b, 512)].partition_broadcast(2))\
                            .then_inc(bias_in[b], 16)
                    for b in range(3):
                        act.wait_ge(S["mod_row"], i * 3 + (12 * layer + b + 4))
                        act.dma_start(mod_dram[layer, :, bass.ds(i * 1536 + 512 * b, 512)], mrow[:, b, :])\
                            .then_inc(mod_out[b], 16)
            for n in range(2):
                for t in range(T):
                    act.wait_ge(S["z_ps"], T * n + t + 1)
                    act.activation(acc[:, t, 512 * n:512 * n + 512], bank(t), ACT.Silu).then_inc(S["z_ready"], 1)
            act.wait_ge(S["gate_step"], 2)
            act.activation(gates5[:, SPA, :, :], gates5[:, SPA, :, :], ACT.Exp, scale=-1.0).then_inc(S["gate_act"], 1)
            act.activation(gates5[:, TMP, :, :], gates5[:, AB0, :, :], ACT.Exp, scale=-1.0).then_inc(S["gate_act"], 1)
            act.activation(alog[:, :], alog[:, :], ACT.Exp).then_inc(S["gate_act"], 1)
            act.wait_ge(S["gate_act"], 1)
            act.activation(gates5[:, SPB, :, :], gates5[:, SPA, :, :], ACT.Ln, bias=1.0).then_inc(S["gate_act"], 1)
            act.wait_ge(S["cum_ps"], 1)
            cum = bank(7)[:, 0:240].rearrange("p (s q) -> p s q", s=3)
            act.activation(gates5[:, EG:EG + 3, :, :].rearrange("p s t h -> p s (t h)"), cum, ACT.Exp).then_inc(S["gate_act"], 1)

            with act.Fori(0, H) as hd:
                act.wait_ge(S["oT_ready"], hd + 1)
                for d in range(2):
                    act.dma_start(state[:, d, :], A["state_dn"][0, 0, d, bass.ds(hd, 1)].rearrange("a k v -> (a k) v"))\
                        .then_inc(S["state_in"], 16)
                act.wait_ge(S["cbuf_zero"], hd + 1)
                for c in range(3):
                    act.wait_ge(S["q_k_v_ps"], hd * 3 + (c + 1))
                    act.activation(cbuf[:, c, 2:130], PP[c][:, 0:P], ACT.Copy)
                    act.activation(cbuf[:, c, 134:646], PP[c][:, P:NT], ACT.Copy).then_inc(S["conv_in"], 1)
                for c in range(3):
                    act.wait_ge(S["conv_step"], hd * 15 + 5 * (c + 1))
                    act.activation(cv[:, c, :], cv[:, c, :], ACT.Silu).then_inc(S["silu_done"], 1)
                for c in range(2):
                    act.wait_ge(S["tok_ps"], hd * 3 + (c + 1))
                    act.activation(sq[:, c, :], PP[c][:, 0:NT], ACT.Square).then_inc(S["sq_done"], 1)
                act.wait_ge(S["tok_ps"], hd * 3 + 3)
                act.activation(vn_t[:, 2, :], PP[2][:, 0:NT], ACT.Copy).then_inc(S["v_ready"], 1)
                for c in range(2):
                    act.wait_ge(S["head_ps"], hd * 2 + (c + 1))
                    act.activation(qTk[:, c, :], PP[c][:, 0:NT], ACT.Copy).then_inc(S["qkT_ready"], 1)
                for c, dst in enumerate((kk, qk)):
                    act.wait_ge(S["gram_ps"], hd * 2 + (c + 1))
                    act.activation(dst, PP[2 + c][:, 0:NT], ACT.Copy).then_inc(S["gram_sb"], 1)
                for j in range(4):
                    act.wait_ge(S["decay_ps"], hd * 4 + (j + 1))
                    act.activation(ex[:, j, :], PP[j][:, 0:NT], ACT.Exp).then_inc(S["ex_ready"], 1)
                for n in range(2 * LEVELS):
                    d = n % 2
                    act.wait_ge(S["vt_ps"], hd * 14 + (n + 1))
                    act.activation(vt[:, d, :], PP[d][:, 0:NT], ACT.Copy).then_inc(S["vt_sb"], 1)
                for d in range(2):
                    act.wait_ge(S["u_ps"], hd * 2 + (d + 1))
                    act.activation(u_all(d), PP[d][:, 0:NT], ACT.Copy).then_inc(S["u_sb"], 1)
                    act.wait_ge(S["wt_ps"], hd * 2 + (d + 1))
                    act.activation(wT(d), PP[2 + d][:, 0:NT], ACT.Copy).then_inc(S["wt_sb"], 1)
                for d in range(2):
                    act.wait_ge(S["s_add_ps"], hd * 10 + (d + 1))
                    act.wait_ge(S["state_out"], hd * 32 + 1)
                    act.activation(state_new[:, d, :], bank(4 * d + 2)[:, 0:P], ACT.Copy).then_inc(S["sp_ready"], 1)
                for d in range(2):
                    act.wait_ge(S["sp_ready"], hd * 2 + (d + 1))
                    act.dma_start(out_state[0, 0, d, bass.ds(hd, 1)].rearrange("a k v -> (a k) v"), state_new[:, d, :])\
                        .then_inc(S["state_out"], 16)
                act.wait_ge(S["o_upd"], hd * 19 + 19)
                act.activation(invT[:, 0, :], oacc, ACT.Square).then_inc(S["sqo_done"], 1)
                act.wait_ge(S["ogT_ps"], hd + 1)
                act.activation(oT[:, bass.ds(hd, 1), :].rearrange("p a t -> p (a t)"), PP[0][:, 0:NT], ACT.Copy)\
                    .then_inc(S["oT_ready"], 1)
            act.wait_ge(S["state_out"], 32 * H + 1)

            def slot_row(tile):
                return tile.with_bounds(min_val=0, max_val=SLOTS - 1) * P

            def ffn(l):
                f = F[l]

                def load_tokens(n, c):
                    with act.Fori(0, n) as t:
                        src = xs_dram[bass.ds(slot_row(c + t), P), :] if l else h_dram[bass.ds(t * P, P), :]
                        act.dma_start(xs_stage[:, bass.ds(t, 1), :].rearrange("p a d -> p (a d)"), src)\
                            .then_inc(f["xs_in"], 16)

                def xs_high(i, t, g, b):
                    act.wait_ge(f["xsT_ps"], 2 * (i + t) + (g + 1))
                    act.activation(xTh[:, 4 * g:4 * g + 4, t * P:(t + 1) * P],
                                   bank(b).rearrange("p (k t) -> p k t", k=4), ACT.Copy).then_inc(f["xTh_ready"], 1)

                def h_high(q0, n, j):
                    nk = 2 if j < 5 else 1
                    with act.Fori(0, n) as t:
                        act.wait_ge(f["hT_ps"], q0 + t + 1)
                        act.activation(hTh[:, 2 * j:2 * j + nk, bass.ds(t * P, P)],
                                       bank(7)[:, 0:nk * P].rearrange("p (k t) -> p k t", k=nk), ACT.Copy)\
                            .then_inc(f["hTh_ready"], 1)

                def silus(q0, n, j):
                    w = 256 if j < 5 else 128
                    for t in range(T):
                        b = t if j % 2 == 0 or t > 1 else 5 + t

                        def one(t=t, b=b):
                            act.wait_ge(f["gu_ps"], q0 + (t + 1))
                            act.activation(hbuf[:, t, 0:w], bank(b)[:, 0:w], ACT.Silu).then_inc(f["sil_done"], 1)
                        if t == 0 or l == 0:
                            one()
                        else:
                            with act.If(n > t):
                                one()

                def y_out(c, n, a):
                    for t in range(T):
                        b = t if a == 0 or t > 1 else 5 + t

                        def one(t=t, b=b):
                            act.wait_ge(f["down_ps"], c * 2 + n * a + (t + 1))
                            act.wait_ge(f["y_out"], (c * 2 + n * a) * 16 + 1)
                            act.activation(ybuf[:, t, :], bank(b), ACT.Copy).then_inc(f["y_copied"], 1)
                            act.wait_ge(f["y_copied"], c * 2 + n * a + (t + 2))
                            act.dma_start(ys_dram[bass.ds(slot_row(c + t), P), 512 * a:512 * a + 512], ybuf[:, t, :])\
                                .then_inc(f["y_out"], 16)
                        if t == 0 or l == 0:
                            one()
                        else:
                            with act.If(n > t):
                                one()

                if l == 0:
                    n0 = T
                    act.wait_ge(S["h_out"], 16)
                else:
                    act.wait_ge(S["tbl_ready"], 1)
                    act.wait_ge(S["xs_scattered"], 160)
                    n0 = act.value_load(tbl[0:1, 0, 0:1], min_val=1, max_val=T)
                act.wait_ge(S["x_parked"], 16 * (l + 1))
                load_tokens(n0, 0)
                for t in range(T):
                    if t == 0 or l == 0:
                        for g in range(2):
                            xs_high(0, t, g, 6 + g)
                    else:
                        with act.If(n0 > t):
                            for g in range(2):
                                xs_high(0, t, g, 6 + g)
                with act.Fori(0, 8 if l else 2) as e:
                    if l:
                        n = act.value_load(tbl[0:1, 0, bass.ds(e, 1)], min_val=1, max_val=T)
                        n2 = act.value_load(tbl[0:1, 0, bass.ds(e + 1, 1)], min_val=1, max_val=T)
                        c = act.value_load(tbl[0:1, 1, bass.ds(e, 1)], min_val=0, max_val=SLOTS)
                    else:
                        n, n2, c = T, T, e * T
                    load_tokens(n2, c + n)
                    for j in range(6):
                        if j:
                            h_high(c * 6 + n * (j - 1), n, j - 1)
                        silus(c * 6 + n * j, n, j)
                    h_high(c * 6 + n * 5, n, 5)
                    for m in range(2, 12):
                        t2, g = (m - 2) // 2, m % 2
                        if t2 == 0 or l == 0:
                            xs_high(c + n, t2, g, 7)
                        else:
                            with act.If(n2 > t2):
                                xs_high(c + n, t2, g, 7)
                        if m in (5, 11):
                            y_out(c, n, m // 6)

            ffn(0)
            for t in range(T):
                act.wait_ge(S["poolT_ps"], t + 1)
                if t >= 2:
                    act.wait_ge(S["pool_ps"], t - 1)
                act.activation(pT[:, t % 2, :], PP[t % 2][:, :], ACT.Copy).then_inc(S["poolT_sb"], 1)
            for t in range(T):
                act.wait_ge(S["hcol_ps"], t + 1)
                act.activation(hcol[:, :, t * P:(t + 1) * P], PP[t % 2][:, :].rearrange("p (k t) -> p k t", k=KD), ACT.Copy)\
                    .then_inc(S["hcol_ready"], 1)
            act.wait_ge(S["route_step"], 2)
            act.activation(rt[:, 1, :, :], rt[:, 1, :, :], ACT.Exp).then_inc(S["route_act"], 1)
            ffn(1)

        @block.vector
        def _(dve):
            dve.wait_ge(S["conv_ps"], 1)
            dve.tensor_copy(convw[:, :, :].rearrange("p j c -> p (j c)"), PP[3][:, 512:632]).then_inc(S["conv_cols"], 1)
            dve.sem_inc(S["mod_row"], 3)
            for l in range(2):
                for n in ("hTl_ready", "xTl_ready"):
                    dve.sem_inc(F[l][n], 1)
            for layer in range(2):
                with dve.Fori(0, 4) as i:
                    for b in range(3):
                        dve.wait_ge(S["mod_ps"], i * 3 + (12 * layer + b + 1))
                        dve.wait_ge(bias_in[b], i * 16 + (64 * layer + 16))
                        dve.wait_ge(mod_out[b], i * 16 + (64 * layer + 1))
                        dve.tensor_tensor(mrow[:, b, :], bank(b)[0:2, :], brow[:, b, :], ALU.add).then_inc(S["mod_row"], 1)
            xt_n = [0]
            for layer in range(2):
                dve.wait_ge(S["modcol_ps"], layer + 1)
                dve.tensor_copy(modc[layer], PP[3][:, 0:96]).then_inc(S["modcol_ready"], 1)
            dve.wait_ge(S["modcol_ready"], 2)

            def transposed_mod(layer, sub):
                mc = modc[layer].rearrange("p (r w k) -> p r w k", r=2, w=6)
                n = xt_n[0]
                if n:
                    dve.wait_ge(S["xt_ready"], 2 * T * n)
                dve.tensor_scalar(scp1[:, :, :], mc[:, :, 3 * sub + 1, :], 1.0, None, ALU.add).then_inc(S["scp1_ready"], 1)
                dve.wait_ge(S["scp1_ready"], n + 1)
                for t in range(T):
                    r = 1 if t else 0
                    dve.wait_ge(S["xt_ps"], n * T + t + 1)
                    for k in range(KD):
                        last = dve.tensor_scalar(xT[:, k, t * P:(t + 1) * P], PP[t % 4][:, k * P:(k + 1) * P],
                                                 scp1[:, r, k:k + 1], mc[:, r, 3 * sub, k:k + 1], ALU.mult, ALU.add)
                        if k in (KD // 2 - 1, KD - 1):
                            last.then_inc(S["xt_ready"], 1)
                xt_n[0] += 1

            transposed_mod(0, 0)
            step = [0]

            def gstep(ins):
                step[0] += 1
                ins.then_inc(S["gate_step"], 1)
                dve.wait_ge(S["gate_step"], step[0])

            dve.wait_ge(S["ab_ps"], 1)
            abv = bank(6)[:, 0:160].rearrange("p (t w) -> p t w", t=T)
            gstep(dve.tensor_copy(gates5[:, AB0, :, :], abv[:, :, 16:32]))
            dve.wait_ge(S["small_in"], 16 * 8)
            bc16 = lambda a: a.rearrange("p (o h) -> p o h", o=1).to_broadcast([P, T, 16])
            dve.tensor_tensor(gates5[:, T2, :, :], abv[:, :, 0:16], bc16(dtb[:, :]), ALU.add).then_inc(S["gate_arg"], 1)
            dve.wait_ge(S["gate_arg"], 1)
            gstep(dve.scalar_tensor_tensor(gates5[:, SPA, :, :], gates5[:, T2, :, :], -1.0, gates5[:, T2, :, :], ALU.mult, ALU.max))
            dve.wait_ge(S["gate_act"], 4)
            gstep(dve.scalar_tensor_tensor(gates5[:, SPB, :, :], gates5[:, T2, :, :], 0.0, gates5[:, SPB, :, :], ALU.max, ALU.add))
            gstep(dve.tensor_tensor(gates5[:, SPB, :, :], gates5[:, SPB, :, :], bc16(alog[:, :]), ALU.mult))
            gstep(dve.tensor_scalar(gates5[:, G_, :, :], gates5[:, SPB, :, :], -1.0, None, ALU.mult))
            gstep(dve.tensor_scalar(gates5[:, TMP, :, :], gates5[:, TMP, :, :], 1.0, None, ALU.add))
            gstep(dve.reciprocal(gates5[:, BETA, :, :], gates5[:, TMP, :, :]))
            gstep(dve.memset(gates5[:, NA, :, :], 0.0))
            dve.wait_ge(S["gate_act"], 5)
            gstep(dve.tensor_tensor(gates5[:, BG, :, :], gates5[:, BETA, :, :], gates5[:, EG, :, :], ALU.mult))

            with dve.Fori(0, H) as hd:
                dve.wait_ge(S["oT_ready"], hd + 1)
                for c in range(3):
                    dve.wait_ge(S["conv_in"], hd * 3 + (c + 1))
                    for j in range(5):
                        wcol = convw[:, j, bass.ds(hd + 8 * c, 1)]
                        if j == 0:
                            ins = dve.tensor_scalar(cv[:, c, :], cbuf[:, c, 0:644], wcol, None, ALU.mult)
                        else:
                            dve.wait_ge(S["conv_step"], hd * 15 + (5 * c + j))
                            ins = dve.scalar_tensor_tensor(cv[:, c, :], cbuf[:, c, j:j + 644], wcol, cv[:, c, :],
                                                           ALU.mult, ALU.add)
                        ins.then_inc(S["conv_step"], 1)
                for c in range(2):
                    dve.wait_ge(S["sq_done"], hd * 2 + (c + 1))
                    dve.tensor_reduce(ss[:, c, :], per_tile(sq[:, c, :]), AX.X, ALU.add).then_inc(S["ss_done"], 1)
                    dve.wait_ge(S["ss_done"], hd * 4 + (2 * c + 1))
                    dve.tensor_scalar(ss[:, 2 + c, :], ss[:, c, :], EPS, float(P) if c == 0 else 1.0, ALU.add, ALU.mult)\
                        .then_inc(S["ss_done"], 1)
                for c in range(2):
                    dve.wait_ge(S["rn_step"], hd * 2 + (c + 1))
                    dve.tensor_tensor(per_tile(vn_t[:, c, :]), per_tile(PP[c][:, 0:NT]),
                                      col_bc(ss[:, 4 + c, :].rearrange("p (t o) -> p t o", o=1)), ALU.mult)\
                        .then_inc(S["qkn"], 1)
                dve.wait_ge(S["gram_sb"], hd * 2 + 2)
                for d in range(2):
                    dve.wait_ge(S["ex_ready"], hd * 4 + (2 * d + 1))
                    a = ex[:, 2 * d, :]
                    dve.tensor_tensor(a, a, kk, ALU.mult).then_inc(S["a_step"], 1)
                    dve.wait_ge(S["a_step"], hd * 4 + (2 * d + 1))
                    dve.tensor_tensor(per_tile(a), per_tile(a), col_bc(gcol(BETA, d, hd)), ALU.mult).then_inc(S["a_step"], 1)
                for d in range(2):
                    dve.wait_ge(S["ex_ready"], hd * 4 + (2 * d + 2))
                    w = ex[:, 2 * d + 1, :]
                    dve.tensor_tensor(w, w, qk, ALU.mult).then_inc(S["w_step"], 1)
                    dve.wait_ge(S["w_step"], hd * 4 + (2 * d + 1))
                    dve.tensor_tensor(per_tile(qkT[:, d, :]), per_tile(w), mat_bc(GE if d else LE), ALU.mult)\
                        .then_inc(S["w_step"], 1)
                dve.wait_ge(S["a_step"], hd * 4 + 4)
                dve.memset(oacc, 0.0).then_inc(S["o_upd"], 1)
                for n in range(2 * LEVELS):
                    d = n % 2
                    dve.wait_ge(S["upd_x_ps"], hd * 14 + (n + 1))
                    if n < 2:
                        dve.wait_ge(S["inv_init"], hd * 4 + 4)
                    else:
                        dve.wait_ge(S["inv_upd"], hd * 28 + 2 * (n - 1))
                    dve.tensor_tensor(invT[:, d, :], invT[:, d, :], PP[d][:, 0:NT], ALU.subtract).then_inc(S["inv_upd"], 1)
                    dve.wait_ge(S["upd_y_ps"], hd * 14 + (n + 1))
                    dve.tensor_tensor(inv[:, d, :], inv[:, d, :], PP[2 + d][:, 0:NT], ALU.subtract).then_inc(S["inv_upd"], 1)
                n_o = 1
                for k in range(T):
                    for d in range(2):
                        t = k if d == 0 or k == 0 else T - k
                        tt = slice(t * P, (t + 1) * P)
                        if k:
                            dve.wait_ge(S["s_read_ps"], hd * 8 + (2 * (k - 1) + d + 1))
                            dve.wait_ge(S["u_sb"], hd * 2 + 2)
                            dve.tensor_tensor(vnew[:, d, :], u_all(d)[:, tt], bank(4 * d)[:, 0:P], ALU.subtract)\
                                .then_inc(S["vn_ready"], 1)
                            dve.wait_ge(S["o_upd"], hd * 19 + n_o)
                            dve.scalar_tensor_tensor(oacc[:, tt], bank(4 * d + 1)[:, 0:P],
                                                     gates5[:, EG, t, bass.ds(hd + 8 * d, 1)], oacc[:, tt],
                                                     ALU.mult, ALU.add).then_inc(S["o_upd"], 1)
                            n_o += 1
                    for d in range(2):
                        t = k if d == 0 or k == 0 else T - k
                        tt = slice(t * P, (t + 1) * P)
                        dve.wait_ge(S["s_add_ps"], hd * 10 + (2 * k + d + 1))
                        if 0 < k < T - 1:
                            if k == 1:
                                dve.wait_ge(S["state_in"], hd * 32 + 32)
                            else:
                                dve.wait_ge(S["s_upd"], hd * 6 + (2 * (k - 2) + d + 1))
                            dve.scalar_tensor_tensor(state[:, d, :], state[:, d, :],
                                                     gates5[:, EL, t, bass.ds(hd + 8 * d, 1)],
                                                     bank(4 * d + 2)[:, 0:P], ALU.mult, ALU.add).then_inc(S["s_upd"], 1)
                        dve.wait_ge(S["o_upd"], hd * 19 + n_o)
                        dve.tensor_tensor(oacc[:, tt], oacc[:, tt], bank(4 * d + 3)[:, 0:P], ALU.add).then_inc(S["o_upd"], 1)
                        n_o += 1
                assert n_o == 19
                dve.wait_ge(S["sqo_done"], hd + 1)
                dve.tensor_reduce(ss[:, 6, :], per_tile(invT[:, 0, :]), AX.X, ALU.add).then_inc(S["sso_done"], 1)
                dve.wait_ge(S["sso_done"], hd * 2 + 1)
                dve.tensor_scalar(ss[:, 6, :], ss[:, 6, :], 1.0 / P, EPS, ALU.mult, ALU.add).then_inc(S["sso_done"], 1)
                dve.wait_ge(S["rno_step"], hd + 1)
                dve.tensor_tensor(per_tile(og), per_tile(oacc), col_bc(ss[:, 7, :].rearrange("p (t o) -> p t o", o=1)),
                                  ALU.mult).then_inc(S["og_step"], 1)
                dve.wait_ge(S["og_step"], hd * 3 + 1)
                dve.tensor_tensor(per_tile(og), per_tile(og),
                                  ngb[:, :].rearrange("p (o c) -> p o c", o=1).to_broadcast([P, T, P]), ALU.mult)\
                    .then_inc(S["og_step"], 1)
                dve.wait_ge(S["og_step"], hd * 3 + 2)
                dve.tensor_tensor(per_tile(og), per_tile(og), acc[:, :, bass.ds(hd * P, P)], ALU.mult)\
                    .then_inc(S["og_step"], 1)
                dve.wait_ge(S["off_ready"], hd * 14 + 14)
                dve.wait_ge(S["vt_ps"], hd * 14 + 14)
                dve.memset(cbuf, 0.0).then_inc(S["cbuf_zero"], 1)

            def layer_norm(n):
                for t in range(T):
                    base = (n * T + t) * LN_STEPS
                    xt = x[:, t, :]
                    ready(n, t)
                    for a in range(2):
                        dve.bn_stats(lnst[:, t, a, :], x[:, t, 512 * a:512 * a + 512]).then_inc(S["ln_step"], 1)
                    dve.wait_ge(S["ln_step"], base + 2)
                    dve.bn_aggr(lnmv[:, t, :], lnst[:, t, :, :].rearrange("p a b -> p (a b)")).then_inc(S["ln_step"], 1)
                    dve.wait_ge(S["ln_step"], base + 3)
                    dve.wait_ge(S["ln_rstd"], 2 * (n * T + t) + 2)
                    dve.tensor_scalar(xt, xt, lnmv[:, t, 0:1], rstd[:, 1, t:t + 1], ALU.subtract, ALU.mult)\
                        .then_inc(S["ln_step"], 1)
                    dve.wait_ge(S["ln_step"], base + 4)
                    dve.tensor_tensor(xt, xt, rows[:, 2, :], ALU.mult).then_inc(S["ln_step"], 1)
                    dve.wait_ge(S["ln_step"], base + 5)
                    dve.tensor_tensor(xt, xt, rows[:, 3, :], ALU.add).then_inc(S["ln_step"], LN_STEPS - 5)

            res_n = [0]

            def ready(n, t):
                dve.wait_ge(S["res_step"], res_after[n])

            res_after = {}

            def rstep(ins):
                res_n[0] += 1
                ins.then_inc(S["res_step"], 1)
                return res_n[0]

            dve.wait_ge(S["rows_in"], 64)
            for n in range(2):
                for t in range(T):
                    dve.wait_ge(S["res_ps"], T * n + t + 1)
                    cols = slice(512 * n, 512 * n + 512)
                    tmp = lnt[:, t, cols]
                    v = rstep(dve.tensor_tensor(tmp, bank(t), rows[:, 1 if t else 0, cols], ALU.mult))
                    dve.wait_ge(S["res_step"], v)
                    v = rstep(dve.scalar_tensor_tensor(x[:, t, cols], x[:, t, cols], ALPHA, tmp, ALU.mult, ALU.add))
            res_after[0] = v
            layer_norm(0)

            def rwait(ins):
                dve.wait_ge(S["res_step"], rstep(ins))

            mr_n = [0]

            def modulate_rows():
                i = mr_n[0]
                dve.wait_ge(S["mrows_in"], 64 * (i + 1))
                dve.tensor_scalar(mrows[:, 0:2, :], mrows[:, 0:2, :], 1.0, None, ALU.add).then_inc(S["mrow1"], 1)
                dve.wait_ge(S["mrow1"], i + 1)
                for t in range(T):
                    r = 1 if t else 0
                    m = 2 * (i * T + t)
                    dve.wait_ge(S["ln_step"], (i * T + t + 1) * LN_STEPS)
                    dve.tensor_tensor(hrow[:, t, :], x[:, t, :], mrows[:, r, :], ALU.mult).then_inc(S["hrow_ready"], 1)
                    dve.wait_ge(S["hrow_ready"], m + 1)
                    dve.tensor_tensor(hrow[:, t, :], hrow[:, t, :], mrows[:, 2 + r, :], ALU.add).then_inc(S["hrow_ready"], 1)
                mr_n[0] += 1

            def ffn(l):
                f = F[l]
                ring_v = ring_of[l]
                n_exp = 8 if l else 2

                def high(k, s, e=0, per=0):
                    nk = half_rows(k, s)
                    w = 256 if k in (10, 11) else 512
                    hs = (2 * k + s) % HALVES
                    if s == 0:
                        dve.wait_ge(slot_loaded[ring_v.slot(k)], ring_v.loaded(k, e, per))
                    dve.tensor_copy(whi[:, hs, 0:nk, 0:w], wring[:, ring_v.slot(k), 2 * s:2 * s + nk, 0:w])\
                        .then_inc(S["slot_hi"], 1)

                def high_after(m, e, c, n):
                    if m < 24:
                        j, s = m // 4, m % 4
                        if s < 3:
                            dve.wait_ge(f["half_done"], c * 28 + n * (3 * j + s + 1))
                        else:
                            dve.wait_ge(f["gu_ps"], c * 6 + n * (j + 1))
                    else:
                        a, s = (m - 24) // 6, (m - 24) % 6
                        if s < 5:
                            dve.wait_ge(f["half_done"], c * 28 + n * (18 + 5 * a + s + 1))
                        else:
                            dve.wait_ge(f["down_ps"], c * 2 + n * (a + 1))
                    k = (m + 4) // 2
                    if k < 18:
                        high(k, m % 2, e, 18)
                    else:
                        nk, w, hs = 2, 512, (m + 4) % HALVES
                        if m % 2 == 0:
                            dve.wait_ge(slot_loaded[ring_v.slot(k)], ring_v.loaded(k, e, 18))
                        dve.tensor_copy(whi[:, hs, :, :], wring[:, ring_v.slot(k), 2 * (m % 2):2 * (m % 2) + 2, :])\
                            .then_inc(S["slot_hi"], 1)

                def xs_low(i, t, g, b):
                    dve.wait_ge(f["xTh_ready"], 2 * (i + t) + (g + 2))
                    dst = (slice(None), slice(4 * g, 4 * g + 4), slice(t * P, (t + 1) * P))
                    dve.tensor_tensor(xTl[dst], bank(b).rearrange("p (k t) -> p k t", k=4), xTh[dst].bitcast(F32),
                                      ALU.subtract).then_inc(f["xTl_ready"], 1)

                def h_low(q0, n, j):
                    nk = 2 if j < 5 else 1
                    with dve.Fori(0, n) as t:
                        dve.wait_ge(f["hTh_ready"], q0 + t + 2)
                        dve.tensor_tensor(hTl[:, 2 * j:2 * j + nk, bass.ds(t * P, P)],
                                          bank(7)[:, 0:nk * P].rearrange("p (k t) -> p k t", k=nk),
                                          hTh[:, 2 * j:2 * j + nk, bass.ds(t * P, P)].bitcast(F32), ALU.subtract)\
                            .then_inc(f["hTl_ready"], 1)

                def products(q0, n, j):
                    w = 256 if j < 5 else 128
                    for t in range(T):
                        b = t if j % 2 == 0 or t > 1 else 5 + t

                        def one(t=t, b=b):
                            dve.wait_ge(f["sil_done"], q0 + (t + 1))
                            dve.tensor_tensor(hbuf[:, t, 0:w], hbuf[:, t, 0:w], bank(b)[:, w:2 * w], ALU.mult)\
                                .then_inc(f["h_done"], 1)
                        if t == 0 or l == 0:
                            one()
                        else:
                            with dve.If(n > t):
                                one()

                dve.wait_ge(S["xs_scattered" if l else "h_out"], 160 if l else 16)
                for k in range(2):
                    for s in range(2):
                        high(k, s)
                n0 = T if l == 0 else dve.value_load(tbl[0:1, 0, 0:1], min_val=1, max_val=T)
                for t in range(T):
                    if t == 0 or l == 0:
                        for g in range(2):
                            xs_low(0, t, g, 6 + g)
                    else:
                        with dve.If(n0 > t):
                            for g in range(2):
                                xs_low(0, t, g, 6 + g)
                with dve.Fori(0, n_exp) as e:
                    if l:
                        n = dve.value_load(tbl[0:1, 0, bass.ds(e, 1)], min_val=1, max_val=T)
                        n2 = dve.value_load(tbl[0:1, 0, bass.ds(e + 1, 1)], min_val=1, max_val=T)
                        c = dve.value_load(tbl[0:1, 1, bass.ds(e, 1)], min_val=0, max_val=SLOTS)
                    else:
                        n, n2, c = T, T, e * T
                    for j in range(6):
                        high_after(4 * j, e, c, n)
                        if j:
                            h_low(c * 6 + n * (j - 1), n, j - 1)
                        high_after(4 * j + 1, e, c, n)
                        high_after(4 * j + 2, e, c, n)
                        products(c * 6 + n * j, n, j)
                        high_after(4 * j + 3, e, c, n)
                    for m in range(12):
                        high_after(24 + m, e, c, n)
                        if m == 0:
                            h_low(c * 6 + n * 5, n, 5)
                        if m >= 2:
                            t2, g = (m - 2) // 2, m % 2
                            if t2 == 0 or l == 0:
                                xs_low(c + n, t2, g, 7)
                            else:
                                with dve.If(n2 > t2):
                                    xs_low(c + n, t2, g, 7)

                n_ln = 1 + 2 * l
                dve.wait_ge(S["rows_in"], 64 * (n_ln + 1))
                dve.wait_ge(S["x_back"], 16 * (l + 1))
                for t in range(T):
                    dve.wait_ge(yg_in[t], 32 * (l + 1))
                    rwait(dve.tensor_scalar(yA[:, t, :], yA[:, t, :], gates2[:, l, 0, t:t + 1], None, ALU.mult))
                    rwait(dve.scalar_tensor_tensor(yA[:, t, :], yB[:, t, :], gates2[:, l, 1, t:t + 1], yA[:, t, :],
                                                   ALU.mult, ALU.add))
                    rwait(dve.tensor_tensor(yA[:, t, :], yA[:, t, :], rows[:, 1 if t else 0, :], ALU.mult))
                    v = rstep(dve.scalar_tensor_tensor(x[:, t, :], x[:, t, :], ALPHA, yA[:, t, :], ALU.mult, ALU.add))
                    dve.wait_ge(S["res_step"], v)
                res_after[n_ln] = v

            rwait(dve.memset(gates2[:, 0, :, :], 1.0))
            modulate_rows()
            ffn(0)
            layer_norm(1)

            modulate_rows()
            dve.wait_ge(S["rows_in"], 64 * 3)
            dve.wait_ge(S["poolrows_in"], 32)
            pb, psc = prow[:, 0, :], prow[:, 1, :]
            for t in range(T):
                y = lnt[:, t, :]
                dve.wait_ge(S["pool_ps"], t + 1)
                dve.tensor_tensor(y, PP[2 + t % 2][:, :], pb, ALU.add).then_inc(S["pool_step"], 1)
                dve.wait_ge(S["pool_step"], 5 * t + 1)
                dve.tensor_tensor(y, y, psc, ALU.mult).then_inc(S["pool_step"], 1)
                dve.wait_ge(S["pool_step"], 5 * t + 2)
                dve.tensor_tensor(y, y, rows[:, 1 if t else 0, :], ALU.mult).then_inc(S["pool_step"], 1)
                dve.wait_ge(S["pool_step"], 5 * t + 3)
                v = rstep(dve.scalar_tensor_tensor(x[:, t, :], x[:, t, :], ALPHA, y, ALU.mult, ALU.add))
                dve.wait_ge(S["res_step"], v)
                dve.sem_inc(S["pool_step"], 2)
            res_after[2] = v
            layer_norm(2)
            modulate_rows()
            step = [0]

            def rts(ins):
                step[0] += 1
                ins.then_inc(S["route_step"], 1)
                dve.wait_ge(S["route_step"], step[0])

            LOG, E_, PR, MX, SUM, GTM, EQ, PRE, TA, TB, SEL, M1 = range(12)
            c8 = lambda a: a.to_broadcast([P, T, 8])
            dve.wait_ge(S["logit_ps"], 1)
            lg = bank(4)[:, 0:40].rearrange("p (t e) -> p t e", t=T)
            rts(dve.tensor_reduce(rt[:, SUM, :, 0:1], lg, AX.X, ALU.max))
            rts(dve.tensor_tensor(rt[:, E_, :, :], lg, c8(rt[:, SUM, :, 0:1]), ALU.subtract))
            dve.wait_ge(S["route_act"], 1)
            rts(dve.tensor_reduce(rt[:, SUM, :, 1:2], rt[:, E_, :, :], AX.X, ALU.add))
            rts(dve.reciprocal(rt[:, SUM, :, 2:3], rt[:, SUM, :, 1:2]))
            rts(dve.tensor_tensor(rt[:, PR, :, :], rt[:, E_, :, :], c8(rt[:, SUM, :, 2:3]), ALU.mult))
            for t in range(T):
                rts(dve.max(rt[:, MX, t, :], rt[:, PR, t, :]))
            m2 = rt[:, MX, :, 1:2]
            rts(dve.tensor_tensor(rt[:, GTM, :, :], rt[:, PR, :, :], c8(m2), ALU.is_gt))
            rts(dve.tensor_tensor(rt[:, EQ, :, :], rt[:, PR, :, :], c8(m2), ALU.is_equal))
            rts(dve.tensor_reduce(rt[:, PRE, :, 0:1], rt[:, GTM, :, :], AX.X, ALU.add))
            for e in range(7):
                rts(dve.tensor_tensor(rt[:, PRE, :, e + 1:e + 2], rt[:, PRE, :, e:e + 1], rt[:, EQ, :, e:e + 1], ALU.add))
            rts(dve.tensor_scalar(rt[:, TA, :, :], rt[:, PRE, :, :], 1.5, None, ALU.is_lt))
            rts(dve.tensor_tensor(rt[:, TA, :, :], rt[:, TA, :, :], rt[:, EQ, :, :], ALU.mult))
            rts(dve.tensor_tensor(rt[:, SEL, :, :], rt[:, TA, :, :], rt[:, GTM, :, :], ALU.add))
            assert step[0] == ROUTE_SEL, step[0]
            rts(dve.tensor_tensor(rt[:, SUM, :, 3:4], rt[:, MX, :, 0:1], m2, ALU.add))
            rts(dve.reciprocal(rt[:, SUM, :, 4:5], rt[:, SUM, :, 3:4]))
            rts(dve.tensor_tensor(rt[:, TB, :, :], rt[:, PR, :, :], c8(rt[:, SUM, :, 4:5]), ALU.mult))
            rts(dve.memset(rt[:, PRE, :, 0:1], 0.0))
            for e in range(7):
                rts(dve.tensor_tensor(rt[:, PRE, :, e + 1:e + 2], rt[:, PRE, :, e:e + 1], rt[:, SEL, :, e:e + 1], ALU.add))
            rts(dve.tensor_scalar(rt[:, M1, :, :], rt[:, PRE, :, :], 0.5, None, ALU.is_lt))
            rts(dve.tensor_tensor(rt[:, M1, :, :], rt[:, M1, :, :], rt[:, SEL, :, :], ALU.mult))
            rts(dve.tensor_tensor(rt[:, TA, :, :], rt[:, SEL, :, :], rt[:, M1, :, :], ALU.subtract))
            dve.wait_ge(S["rank_ps"], 1)
            rk = bank(5)[:, 0:80].rearrange("p (i t e) -> p i t e", i=2, t=T)
            rts(dve.memset(rt[:, EQ, 0:1, :], 0.0))
            for t in range(T - 1):
                rts(dve.tensor_tensor(rt[:, EQ, t + 1:t + 2, :], rt[:, EQ, t:t + 1, :], rk[:, 1, t:t + 1, :], ALU.add))
            rts(dve.tensor_tensor(cnt[:, 0:1, 0:8], rt[:, EQ, T - 1:T, :], rk[:, 1, T - 1:T, :], ALU.add))
            rts(dve.tensor_tensor(rt[:, EQ, :, :], rt[:, EQ, :, :], rk[:, 0, :, :], ALU.add))
            rts(dve.memset(cnt[:, 1, :], 1.0))
            for t in range(1, T):
                rts(dve.tensor_scalar(cnt[:, 2, 0:8], cnt[:, 0, 0:8], P * t + 0.5, None, ALU.is_gt))
                rts(dve.tensor_tensor(cnt[:, 1, 0:8], cnt[:, 1, 0:8], cnt[:, 2, 0:8], ALU.add))
            rts(dve.memset(cnt[:, 3, :], 0.0))
            for e in range(9):
                rts(dve.tensor_tensor(cnt[:, 3, e + 1:e + 2], cnt[:, 3, e:e + 1], cnt[:, 1, e:e + 1], ALU.add))
            rts(dve.tensor_copy(tbl[:, 0, :], cnt[:, 1, :]))
            rts(dve.tensor_copy(tbl[:, 1, :], cnt[:, 3, :]))
            rts(dve.tensor_scalar(cnt[:, 4, :], cnt[:, 3, :], float(P), None, ALU.mult))
            rts(dve.tensor_tensor(rt[:, EQ, :, :], rt[:, EQ, :, :], cnt[:, 4:5, 0:8].to_broadcast([P, T, 8]), ALU.add))
            for i, m in enumerate((M1, TA)):
                rts(dve.tensor_tensor(rt[:, GTM, :, :], rt[:, EQ, :, :], rt[:, m, :, :], ALU.mult))
                rts(dve.tensor_reduce(rt[:, SUM, :, 5:6], rt[:, GTM, :, :], AX.X, ALU.add))
                rts(dve.tensor_copy(pos[:, i, :], rt[:, SUM, :, 5]))
                rts(dve.tensor_tensor(rt[:, GTM, :, :], rt[:, TB, :, :], rt[:, m, :, :], ALU.mult))
                rts(dve.tensor_reduce(gates2[:, 1, i, :], rt[:, GTM, :, :], AX.X, ALU.add))
            dve.sem_inc(S["tbl_ready"], 1)
            ffn(1)
            layer_norm(3)


_INS = ["x_prompt", "x_sample", "state_dn", "c", "c_ctx", "ada_w", "ada_b", "ln_g", "ln_b", "dn_w_in", "dn_conv",
        "dn_a_log", "dn_dt_bias", "dn_norm_g", "dn_w_out", "pool_w", "pool_b", "pool_scale", "ffn_w_gu",
        "ffn_w_down", "moe_router", "moe_w_gu", "moe_w_down"]


def kernel(**inputs):
    import numpy as _np
    import concourse.bacc as _bacc
    from concourse.bass_utils import run_bass_kernel_spmd as _run

    nc = _bacc.Bacc("TRN2", target_bir_lowering=False, num_devices=1)
    arrays, A = {}, {}
    for name in _INS:
        arrays[f"in_{name}"] = _np.ascontiguousarray(inputs[name])
        A[name] = nc.dram_tensor(f"in_{name}", arrays[f"in_{name}"].shape, F32, kind="ExternalInput").ap()
    arrays["in_consts"] = shape_constants()
    A["consts"] = nc.dram_tensor("in_consts", arrays["in_consts"].shape, F32, kind="ExternalInput").ap()
    outs = [nc.dram_tensor(n, s, F32, kind="ExternalOutput").ap()
            for n, s in (("y_prompt", (1, P, D)), ("y_sample", (1, 4 * P, D)), ("new_state", (1, 1, 2, H, P, P)))]
    scratch = [nc.dram_tensor(n, s, F32, kind="Internal").ap()
               for n, s in (("mod_rows", (2, 2, 6 * D)), ("h_rows", (NT, D)), ("expert_in", (SLOTS * P, D)),
                            ("expert_out", (SLOTS * P, D)), ("x_parked", (NT, D)))]
    backbone(nc, A, *outs, *scratch)
    r = _run(nc, [arrays], core_ids=[0]).results[0]
    return r["y_prompt"], r["y_sample"], r["new_state"]
```

```python
from contextlib import ExitStack

import numpy as np

import concourse.bass as bass
from concourse import mybir

F32 = mybir.dt.float32
F32R = mybir.dt.float32r
I32 = mybir.dt.int32
U32 = mybir.dt.uint32
ALU = mybir.AluOpType
ACT = mybir.ActivationFunctionType
AX = mybir.AxisListType

P = 128
D = 1024
KD = D // P
T = 5
NT = T * P
H = 8
FE = 1408
KF = FE // P
GRID_W = 64
WINDOWS = (2, 4, 8, 16)
ALPHA = (2.0 * 2) ** 0.25
EPS = 1e-6
RING = 3
LEVELS = 7

SLOTS = 18
HALVES = 4
IDENT, LT, ONES = range(3)
POOL = 3
N_CONST = POOL + 2 * len(WINDOWS)
LE, GE, GT = range(N_CONST, N_CONST + 3)
LEVEL = GT + 1
N_ALL = LEVEL + 2 * LEVELS


def shape_constants():
    r = np.arange(P)[:, None]
    c = np.arange(P)[None, :]
    m = np.zeros((P, N_ALL, P), np.float32)
    m[:, IDENT] = r == c
    m[:, LE] = r <= c
    m[:, GE] = r >= c
    m[:, LT] = r < c
    m[:, GT] = r > c
    m[:, ONES] = 1.0
    for lv in range(LEVELS):
        s = 1 << lv
        off = (r // (2 * s) == c // (2 * s)) & (r % (2 * s) >= s) & (c % (2 * s) < s)
        m[:, LEVEL + lv] = off
        m[:, LEVEL + LEVELS + lv] = off.T
    for kind, seg in enumerate((P, GRID_W)):
        for g, w in enumerate(WINDOWS):
            for t in range(P):
                base = t // seg * seg
                lo, hi = max(t - w // 2, base), min(t - w // 2 + w, base + seg)
                m[lo:hi, POOL + kind * len(WINDOWS) + g, t] = 1.0 / (hi - lo)
                m[t, POOL + kind * len(WINDOWS) + g, t] -= 1.0
    return m


class Ring:

    def __init__(self):
        self.base = 0

    def slot(self, k):
        return (self.base + k) % RING

    def loaded(self, k, i=0, per=0):
        return 32 * ((self.base + k) // RING + 1) + i * (32 * (per // RING))

    def freed(self, k, i=0, per=0):
        return 2 * (self.base + k + 1) + i * (2 * per)


def split_count(k, e=0):
    return k + 1 + RING + e * 18


def half_rows(k, s):
    return 1 if k in (14, 17) and s == 1 else 2


def backbone(nc, A, out_prompt, out_sample, out_state, mod_dram, h_dram, xs_dram, ys_dram, xpark):
    with ExitStack() as ctx:
        def sb(name, shape, dt=F32):
            return ctx.enter_context(nc.sbuf_tensor(name, shape, dt))

        def sem(name):
            return ctx.enter_context(nc.semaphore(name))

        cm = sb("cm", [P, N_CONST, P])
        x = sb("x", [P, T, D])
        wring = sb("wring", [P, RING, 4, 512])
        modcol = sb("modcol", [P, 2, 96])
        scp1 = sb("scp1", [P, 2, KD])
        modcol_in = sb("modcol_in", [96, P])
        condr = sb("condr", [16, P])
        cs = sb("cs", [P, 16])
        convr = sb("convr", [120, P])
        convw = sb("convw", [P, 5, 24])
        wab = sb("wab", [P, KD, 32])
        rw = sb("rw", [P, KD, 8])
        dtb = sb("dtb", [P, 16])
        alog = sb("alog", [P, 16])
        ngb = sb("ngb", [P, P])
        gates5 = sb("gates5", [P, 12, T, 16])
        ss = sb("ss", [P, 8, T])
        mhalf = sb("mhalf", [P, T])
        lnst = sb("lnst", [P, T, 2, 6])
        lnmv = sb("lnmv", [P, T, 2])
        rstd = sb("rstd", [P, 2, T])
        rt = sb("rt", [P, 12, T, 8])
        cnt = sb("cnt", [P, 6, 16])
        tbl = sb("tbl", [P, 2, 16], I32)
        pos = sb("pos", [P, 2, T], I32)
        gates2 = sb("gates2", [P, 2, T])

        ctx_all = ctx
        ctx = ExitStack()
        cmd = sb("cmd", [P, N_ALL - N_CONST, P])
        state = sb("state", [P, 2, P])
        state_new = sb("state_new", [P, 2, P])
        vnew = sb("vnew", [P, 2, P])
        zeros = sb("zeros", [P, 256])
        xT = sb("xT", [P, KD, NT])
        acc = sb("acc", [P, T, D])
        big = sb("big", [P, KF * NT])
        cv = sb("cv", [P, 3, 644])
        scratch = sb("scratch", [P, 10904])
        dnrows = sb("dnrows", [P, 6 * NT])
        ctx.close()
        ctx = ExitStack()
        xTh = sb("xTh", [P, KD, NT], F32R)
        xTl = sb("xTl", [P, KD, NT], F32R)
        hTh = sb("hTh", [P, KF, NT], F32R)
        hTl = sb("hTl", [P, KF, NT], F32R)
        whi = sb("whi", [P, HALVES, 2, 512], F32R)
        wlo = sb("wlo", [P, HALVES, 2, 512], F32R)
        hbuf = sb("hbuf", [P, T, 256])
        ybuf = sb("ybuf", [P, T, 512])
        ctx.close()
        ctx = ExitStack()
        rows = sb("rows", [P, 4, D])
        mrows = sb("mrows", [P, 4, D])
        lnt = sb("lnt", [P, T, D])
        hrow = sb("hrow", [P, T, D])
        prow = sb("prow", [P, 2, D])
        pT = sb("pT", [P, 2, D])
        hcol = sb("hcol", [P, KD, NT])
        yA, yB = lnt, hrow
        ctx.close()
        ctx = ctx_all
        xs_stage = x

        def carve(buf, off, n, **dims):
            ap = buf[:, off:off + n]
            if not dims:
                return ap
            names = " ".join(dims)
            return ap.rearrange(f"p ({names}) -> p {names}", **dims)

        early = xT[0:2, :, :].rearrange("p k t -> p (k t)")
        brow = early[:, 0:1536].rearrange("p (b n) -> p b n", b=3)
        mrow = early[:, 1536:3072].rearrange("p (b n) -> p b n", b=3)
        oT = carve(big, 0, H * NT, h=H, t=NT)
        vn_t = carve(big, H * NT, 3 * NT, c=3, t=NT)
        cbuf = carve(scratch, 0, 3 * 648, c=3, t=648)
        offd = carve(scratch, 0, 2 * NT, d=2, t=NT)
        vt = carve(scratch, 1944, 2 * NT, d=2, t=NT)
        sq = carve(scratch, 3224, 2 * NT, d=2, t=NT)
        inv = sq
        invT = carve(scratch, 4504, 2 * NT, d=2, t=NT)
        qkT = carve(scratch, 5784, 2 * NT, d=2, t=NT)
        kk = carve(scratch, 7064, NT)
        qk = carve(scratch, 7704, NT)
        oacc, og = kk, qk
        gm = carve(scratch, 8344, 4 * NT, j=4, t=NT)
        R = gm
        rowsf = dnrows[:, :]
        ex = rowsf[:, 0:4 * NT].rearrange("p (j t) -> p j t", j=4)

        def per_tile(ap):
            return ap.rearrange("p (t c) -> p t c", t=T)

        qTk = rowsf[:, 4 * NT:6 * NT].rearrange("p (j t) -> p j t", j=2)
        modc = [modcol[:, 0, :], modcol[:, 1, :]]

        def u_all(d):
            return vt[:, d, :]

        def wT(d):
            return inv[:, d, :]

        def kdec(d):
            return ex[:, 2 * d, :]

        PP = [ctx.enter_context(nc.psum_tensor(f"pp{i}", [P, 1024], F32)) for i in range(4)]

        def bank(i):
            return PP[i // 2][:, 512 * (i % 2):512 * (i % 2) + 512]

        names = """consts_in x_in small_in cond_ps cond_ready mod_ps mod_row conv_ps conv_cols slot_free modcol_ps
            modcol_ready scp1_ready xt_ps xt_ready z_ps z_ready ab_ps gate_step gate_act cum_ps q_k_v_ps
            conv_in conv_step silu_done tok_ps sq_done v_ready ss_done rn_step qkn head_ps qkT_ready gram_ps
            gram_sb gm_ready decay_ps ex_ready a_step w_step inv_init off_ready vt_ps vt_sb upd_x_ps
            upd_y_ps inv_upd r_ready kdec_ready u_ps wt_ps u_sb wt_sb s_read_ps s_add_ps vn_ready o_upd
            s_upd sp_ready state_in state_out sqo_done sso_done rno_step og_step ogT_ps oT_ready res_ps
            res_step ln_step ln_rstd rows_in poolrows_in mrows_in poolT_ps poolT_sb pool_ps pool_step
            logit_ps route_step route_act final_out cbuf_zero pool_const gate_arg xs_zero slot_hi mrow1
            hrow_ready h_out xs_scattered x_parked x_back hcol_ps hcol_ready rank_ps tbl_ready y_in""".split()
        S = {n: sem(n) for n in names}
        slot_loaded = [sem(f"slot_loaded{i}") for i in range(RING)]
        bias_in = [sem(f"bias_in{i}") for i in range(3)]
        mod_out = [sem(f"mod_out{i}") for i in range(3)]
        modcol_in_s = sem("modcol_rows_in")
        F = [{n: sem(f"{n}{l}") for n in ("gu_ps", "sil_done", "h_done", "hT_ps", "hTh_ready", "hTl_ready",
                                          "down_ps", "half_done", "y_copied", "y_out", "xs_in", "xsT_ps",
                                          "xTh_ready", "xTl_ready")} for l in range(2)]
        slot_split = [[sem(f"slot_split_{who}{l}") for who in ("pool", "dve")] for l in range(2)]
        yg_in = [sem(f"yg_in{t}") for t in range(T)]

        def cmat(m, n=0):
            buf, m = (cm, m) if m < N_CONST else (cmd, m - N_CONST)
            return buf[:, m:m + 1, :] if n else buf[:, m, :]

        ring_of = [Ring(), Ring()]
        ring_of[0].base = 48 + 4 + 3 * H + 4
        ring_of[1].base = ring_of[0].base + 36 + 2 + 1

        UNSPLIT = (ring_of[0].base, ring_of[0].base + 1)

        def hi_count(l, m, e=0):
            return (76 if l else 0) + m + 1 + e * 36

        ident = cm[:, IDENT, :]
        block = ctx.enter_context(nc.Block())

        def col_bc(ap):
            return ap.to_broadcast([P, T, P])

        def mat_bc(m):
            return cmat(m, 1).to_broadcast([P, T, P])

        AB0, SPA, SPB, G_, BETA, EG, EK, EL, BG, TMP, NA, T2 = range(12)

        def gcol(which, d, hd):
            return gates5[:, which, :, bass.ds(hd + 8 * d, 1)]

        def upd_count(n):
            return max(1, 2 * n) if n < 12 else n + 11

        LN_STEPS = 8
        ROUTE_SEL = 23

        @block.sync
        def _(sp):
            ring = Ring()
            sp.dma_start(cm[:, :, :], A["consts"][:, 0:N_CONST, :]).then_inc(S["consts_in"], 16)
            sp.dma_start(cmd[:, :, :], A["consts"][:, N_CONST:, :]).then_inc(S["consts_in"], 16)
            sp.dma_start(condr[0:8, :], A["c_ctx"].rearrange("(k p) -> k p", p=P)).then_inc(S["small_in"], 16)
            sp.dma_start(condr[8:16, :], A["c"][0].rearrange("(k p) -> k p", p=P)).then_inc(S["small_in"], 16)
            sp.dma_start(convr[:, :], A["dn_conv"][0].rearrange("j (c p) -> (j c) p", p=P)).then_inc(S["small_in"], 16)

            def fill(k, parts, i=0, per=0, l=None):
                if l is None:
                    sp.wait_ge(S["slot_free"], ring.freed(k, i, per))
                else:
                    for split in slot_split[l]:
                        sp.wait_ge(split, k + 1 + i * per)
                for dst, src in parts(ring.slot(k)):
                    sp.dma_start(dst, src).then_inc(slot_loaded[ring.slot(k)], 16)

            def cols512(w, k0, nk, c0):
                wv = w.rearrange("(k p) n -> p k n", p=P)
                a = (nk + 1) // 2

                def parts(s):
                    return [(wring[:, s, 0:a, :], wv[:, k0:k0 + a, bass.ds(c0, 512)]),
                            (wring[:, s, a:nk, :], wv[:, k0 + a:k0 + nk, bass.ds(c0, 512)])]
                return parts

            for layer in range(2):
                with sp.Fori(0, 4) as i:
                    for k in range(6):
                        fill(k, cols512(A["ada_w"][layer], 4 * (k % 2), 4, i * 1536 + 512 * (k // 2)), i, 6)
                ring.base += 24
                if layer == 0:
                    sp.dma_start(x[:, 0, :], A["x_prompt"][0]).then_inc(S["x_in"], 16)
                    sp.dma_start(x[:, 1:T, :], A["x_sample"][0].rearrange("(t p) d -> p t d", p=P)).then_inc(S["x_in"], 16)
                    sp.dma_start(wab[:, :, :], A["dn_w_in"][0].rearrange("(k p) n -> p k n", p=P)[:, :, 4096:4128]).then_inc(S["small_in"], 16)
                    sp.dma_start(rw[:, :, :], A["moe_router"][0].rearrange("(k p) n -> p k n", p=P)).then_inc(S["small_in"], 16)
                    sp.dma_start(dtb[:, :], A["dn_dt_bias"][0].rearrange("d h -> (d h)").partition_broadcast(P)).then_inc(S["small_in"], 16)
                    sp.dma_start(alog[:, :], A["dn_a_log"][0].rearrange("d h -> (d h)").partition_broadcast(P)).then_inc(S["small_in"], 16)
                    sp.dma_start(ngb[:, :], A["dn_norm_g"][0].partition_broadcast(P)).then_inc(S["small_in"], 16)
            for k in range(4):
                fill(k, cols512(A["dn_w_in"][0], 4 * (k % 2), 4, 3072 + 512 * (k // 2)))
            ring.base += 4
            w_in = A["dn_w_in"][0].rearrange("(k p) n -> p k n", p=P)
            with sp.Fori(0, H) as hd:
                for c in range(3):
                    def parts(s, c=c):
                        dst = wring[:, s, 0:2, :].rearrange("p a (b n) -> p (a b) n", n=P)
                        return [(dst[:, 4 * a:4 * a + 4, :], w_in[:, 4 * a:4 * a + 4, bass.ds(hd * P + D * c, P)])
                                for a in range(2)]
                    fill(c, parts, hd, 3)
            ring.base += 3 * H
            for k in range(4):
                fill(k, cols512(A["dn_w_out"][0], 4 * (k % 2), 4, 512 * (k // 2)))
            ring.base += 4

            def expert_fills(l, e, gate_w, down_w, up_off):
                gv = gate_w.rearrange("(k p) n -> p k n", p=P)
                for j in range(6):
                    w = 256 if j < 5 else 128
                    for a in range(2):
                        def parts(s, j=j, w=w, a=a):
                            return [(wring[:, s, 0:4, w * u:w * u + w],
                                     gv[:, 4 * a:4 * a + 4, bass.ds(up_off[u] + 256 * j, w)]) for u in range(2)]
                        fill(2 * j + a, parts, e, 18, l)
                for n in range(2):
                    for a in range(3):
                        nk = 4 if a < 2 else 3
                        fill(12 + 3 * n + a, cols512(down_w, 4 * a, nk, 512 * n), e, 18, l)

            wd = A["ffn_w_down"][0].rearrange("(e f) d -> e f d", f=FE)
            gu0, gu1 = A["ffn_w_gu"][0], A["moe_w_gu"][0]

            def read_ahead(l, w):
                for k in range(2):
                    for split in slot_split[l]:
                        sp.wait_ge(split, k + 1 + 18 * (8 if l else 2))
                    for dst, src in cols512(w, 4 * k, 4, 0)(ring.slot(k)):
                        sp.dma_start(dst, src).then_inc(slot_loaded[ring.slot(k)], 16)
                ring.base += 2

            def all_slots_free(l):
                sp.wait_ge(S["slot_free"], 2 * UNSPLIT[l] + 2 * RING)

            def unpark(l):
                f = F[l]
                if l == 0:
                    last = 30
                else:
                    last = sp.value_load(tbl[0:1, 1, 9:10], min_val=9, max_val=SLOTS) * 2
                sp.wait_ge(f["xsT_ps"], last)
                sp.wait_ge(S["x_parked"], 16 * (l + 1))
                sp.dma_start(x[:, :, :], xpark.rearrange("(t p) d -> p t d", p=P)).then_inc(S["x_back"], 16)

            all_slots_free(0)
            with sp.Fori(0, 2) as e:
                expert_fills(0, e, gu0, wd[bass.ds(e, 1)].rearrange("a f d -> (a f) d"), (e * FE, e * FE + 2 * FE))
            ring.base += 36
            read_ahead(0, gu0)
            unpark(0)
            wp = A["pool_w"][0].rearrange("g (k p) n -> p (g k) n", p=P)

            def parts(s):
                dst = wring[:, s, :, :].rearrange("p a (b n) -> p (a b) n", n=256)
                return [(dst[:, 4 * a:4 * a + 4, :], wp[:, 4 * a:4 * a + 4, :]) for a in range(2)]
            for split in slot_split[0]:
                sp.wait_ge(split, 38 + RING)
            for dst, src in parts(ring.slot(0)):
                sp.dma_start(dst, src).then_inc(slot_loaded[ring.slot(0)], 16)
            ring.base += 1
            all_slots_free(1)
            with sp.Fori(0, 8) as e:
                expert_fills(1, e, gu1[bass.ds(e, 1)].rearrange("a k n -> (a k) n"),
                             A["moe_w_down"][0][bass.ds(e, 1)].rearrange("a f d -> (a f) d"), (0, FE))
            ring.base += 144
            read_ahead(1, gu1[0])
            unpark(1)
            sp.wait_ge(S["ln_step"], 4 * T * LN_STEPS)
            sp.dma_start(out_prompt[0], x[:, 0, :]).then_inc(S["final_out"], 16)
            sp.dma_start(out_sample[0].rearrange("(t p) d -> p t d", p=P), x[:, 1:T, :]).then_inc(S["final_out"], 16)
            sp.wait_ge(S["final_out"], 32)

        @block.tensor
        def _(pe):
            ring = Ring()
            pe.sem_inc(S["slot_free"], 2 * RING)

            def slot(k, i=0, per=0):
                pe.wait_ge(slot_loaded[ring.slot(k)], ring.loaded(k, i, per))
                return ring.slot(k)

            def gemm5(k, nk, lhs, c0, first, last, done, i=0, per=0, n=512, free=None):
                s = slot(k, i, per)
                for t in range(T):
                    if first and free is not None:
                        free(t)
                    for kk_ in range(nk):
                        mm = pe.matmul(bank(t)[:, 0:n], lhs(c0 + kk_, t), wring[:, s, kk_, 0:n],
                                       start=(first and kk_ == 0), stop=(last and kk_ == nk - 1))
                    if last:
                        mm.then_inc(done, 1)
                if not last:
                    mm.then_inc(S["slot_free"], 2)

            pe.wait_ge(S["consts_in"], 32)
            pe.wait_ge(S["small_in"], 48)
            pe.transpose(PP[3][:, 0:16], condr[:, :], ident[0:16, 0:16]).then_inc(S["cond_ps"], 1)
            pe.transpose(PP[3][:, 512:632], convr[:, :], ident[0:120, 0:120]).then_inc(S["conv_ps"], 1)
            pe.wait_ge(S["cond_ready"], 1)
            csv = cs[:, :].rearrange("p (r k) -> p k r", r=2)
            for layer in range(2):
                with pe.Fori(0, 4) as i:
                    for b in range(3):
                        pe.wait_ge(S["mod_row"], i * 3 + (12 * layer + b + 1))
                        for a in range(2):
                            s = slot(2 * b + a, i, 6)
                            for k in range(4):
                                mm = pe.matmul(bank(b)[0:2, :], csv[:, 4 * a + k, :], wring[:, s, k, :],
                                               start=(a == 0 and k == 0), stop=(a == 1 and k == 3))
                            mm.then_inc(S["slot_free" if a == 0 else "mod_ps"], 2 if a == 0 else 1)
                        pe.wait_ge(S["mod_ps"], i * 3 + (12 * layer + b + 1))
                        pe.sem_inc(S["slot_free"], 2)
                ring.base += 24
            for layer in range(2):
                pe.wait_ge(modcol_in_s, 16 * (layer + 1))
                if layer:
                    pe.wait_ge(S["modcol_ready"], 1)
                else:
                    pe.wait_ge(S["conv_cols"], 1)
                pe.transpose(PP[3][:, 0:96], modcol_in[:, :], ident[0:96, 0:96]).then_inc(S["modcol_ps"], 1)
            def transpose_x():
                pe.wait_ge(S["x_in"], 32)
                for t in range(T):
                    if t >= 4:
                        pe.wait_ge(S["xt_ready"], 2 * (t - 3))
                    for k in range(KD):
                        mm = pe.transpose(PP[t % 4][:, k * P:(k + 1) * P], x[:, t, k * P:(k + 1) * P], ident)
                    mm.then_inc(S["xt_ps"], 1)

            pe.wait_ge(S["modcol_ready"], 2)
            transpose_x()

            def lhs_x(k, t):
                return xT[:, k, t * P:(t + 1) * P]

            def lhs_o(k, t):
                return oT[:, k, t * P:(t + 1) * P]

            pe.wait_ge(S["xt_ready"], 2 * T)
            pe.wait_ge(S["small_in"], 16 * 8)
            for t in range(T):
                for k in range(KD):
                    mm = pe.matmul(bank(6)[:, 32 * t:32 * t + 32], lhs_x(k, t), wab[:, k, :],
                                   start=(k == 0), stop=(k == KD - 1))
            mm.then_inc(S["ab_ps"], 1)
            for n in range(2):
                for a in range(2):
                    gemm5(2 * n + a, 4, lhs_x, 4 * a, a == 0, a == 1, S["z_ps"],
                          free=(lambda t: pe.wait_ge(S["z_ready"], t + 1)) if n else None)
                pe.wait_ge(S["z_ps"], T * (n + 1))
                pe.sem_inc(S["slot_free"], 2)
            ring.base += 4
            pe.wait_ge(S["gate_step"], 8)
            gf, gb = gates5[:, G_, :, 0:8], gates5[:, G_, :, 8:16]
            cum = bank(7)[:, 0:240].rearrange("p (s t h) -> p s t h", s=3, h=16)
            for kind, (mf, mb) in enumerate(((LE, GE), (GT, LT), (ONES, ONES))):
                pe.matmul(cum[:, kind, :, 0:8], cmat(mf), gf, start=True, stop=True)
                mm = pe.matmul(cum[:, kind, :, 8:16], cmat(mb), gb, start=True, stop=True)
            mm.then_inc(S["cum_ps"], 1)

            def tiles(j):
                return slice(j * P, (j + 1) * P)

            def mm5(dst, lhs, rhs, sig, n):
                for t in range(T):
                    mm = pe.matmul(dst[:, tiles(t)], lhs(t), rhs(t), start=True, stop=True)
                mm.then_inc(S[sig], 1)

            def project(h, lo, hi, release=True):
                for i in range(lo, hi):
                    c, part, k = i // 16, i // 8 % 2, i % 8
                    if i % 16 == 0:
                        slot(c, h, 3)
                        if c == 2:
                            pe.wait_ge(S["conv_in"], h * 3 + 1)
                    w = wring[:, ring.slot(c), 0:2, :].rearrange("p a (b n) -> p (a b) n", n=P)
                    cols = slice(0, 512) if part == 0 else slice(512, NT)
                    mm = pe.matmul(PP[3 if c == 1 else 2][:, cols], w[:, k, :], xT[:, k, cols],
                                   start=(k == 0), stop=(k == KD - 1))
                    if i % 16 == 15:
                        mm.then_inc(S["q_k_v_ps"], 1)
                    elif i % 16 == 0 and c:
                        mm.then_inc(S["slot_free"], 2)

            def head(hd, more):
                pe.wait_ge(S["oT_ready"], hd + 1)
                for c in range(3):
                    pe.wait_ge(S["silu_done"], hd * 3 + (c + 1))
                    for t in range(T):
                        o = 0 if t == 0 else 132 + (t - 1) * P
                        mm = pe.transpose(PP[c][:, tiles(t)], cv[:, c, o:o + P], ident)
                    mm.then_inc(S["tok_ps"], 1)
                for c in range(2):
                    pe.wait_ge(S["qkn"], hd * 2 + (c + 1))
                    for t in range(T):
                        mm = pe.transpose(PP[c][:, tiles(t)], vn_t[:, c, tiles(t)], ident)
                    mm.then_inc(S["head_ps"], 1)
                pe.wait_ge(S["qkT_ready"], hd * 2 + 2)
                pe.wait_ge(S["v_ready"], hd + 1)
                qTv, kTv = ex[:, 0, :], ex[:, 1, :]
                qT, kT = qTk[:, 0, :], qTk[:, 1, :]
                mm5(PP[2], lambda t: kT[:, tiles(t)], lambda t: kT[:, tiles(t)], "gram_ps", 1)
                mm5(PP[3], lambda t: kT[:, tiles(t)], lambda t: qT[:, tiles(t)], "gram_ps", 1)
                for j, m in enumerate((LE, GT, GE, LT)):
                    pe.wait_ge(S["gm_ready"], hd * 4 + (j + 1))
                    if j >= 2:
                        pe.wait_ge(S["gram_sb"], hd * 2 + (j - 1))
                    pe.matmul(PP[j][:, 0:512], cmat(m), gm[:, j, 0:512], start=True, stop=True)
                    pe.matmul(PP[j][:, 512:NT], cmat(m), gm[:, j, 512:NT], start=True, stop=True)\
                        .then_inc(S["decay_ps"], 1)

                def vt_level(n):
                    d = n % 2
                    pe.wait_ge(S["off_ready"], hd * 14 + (n + 1))
                    if n < 2:
                        pe.wait_ge(S["inv_init"], hd * 4 + 2)
                        pe.wait_ge(S["ex_ready"], hd * 4 + 4)
                    else:
                        pe.wait_ge(S["inv_upd"], hd * 24 + upd_count(n - 2))
                    mm5(PP[d], lambda t: offd[:, d, tiles(t)], lambda t: invT[:, d, tiles(t)], "vt_ps", 1)

                def xy_level(n):
                    d = n % 2
                    if n < 4:
                        pe.wait_ge(S["inv_init"], hd * 4 + 4)
                    pe.wait_ge(S["vt_sb"], hd * 12 + (n - 1))
                    mm5(PP[d], lambda t: inv[:, d, tiles(t)], lambda t: vt[:, d, tiles(t)], "upd_x_ps", 1)
                    if n < 12:
                        mm5(PP[2 + d], lambda t: vt[:, d, tiles(t)], lambda t: inv[:, d, tiles(t)], "upd_y_ps", 1)

                for lv in range(LEVELS):
                    for d in range(2):
                        vt_level(2 * lv + d)
                    for d in range(2):
                        if lv:
                            xy_level(2 * lv + d)
                for d in range(2):
                    pe.wait_ge(S["inv_upd"], hd * 24 + upd_count(12 + d))
                    pe.wait_ge(S["r_ready"], hd * 4 + 4)
                    mm5(PP[d], lambda t: invT[:, d, tiles(t)], lambda t: R[:, d, tiles(t)], "u_ps", 1)
                    mm5(PP[2 + d], lambda t: R[:, 2 + d, tiles(t)], lambda t: invT[:, d, tiles(t)], "wt_ps", 1)
                pe.wait_ge(S["u_sb"], hd * 2 + 2)
                pe.wait_ge(S["wt_sb"], hd * 2 + 2)
                pe.wait_ge(S["kdec_ready"], hd * 2 + 2)
                gap = 0
                for k in range(T):
                    if k:
                        for d in range(2):
                            tt = tiles(k if d == 0 else T - k)
                            if k == 1:
                                pe.wait_ge(S["state_in"], hd * 32 + 32)
                            else:
                                pe.wait_ge(S["s_upd"], hd * 6 + (2 * (k - 2) + d + 1))
                            pe.wait_ge(S["o_upd"], hd * 19 + (1 + 2 + 4 * (k - 1)))
                            pe.matmul(bank(2 * d)[:, 0:P], wT(d)[:, tt], state[:, d, :], start=True, stop=True)
                            pe.matmul(bank(2 * d)[:, P:2 * P], qT[:, tt], state[:, d, :], start=True, stop=True)\
                                .then_inc(S["s_read_ps"], 1)
                        if more:
                            project(hd + 1, 16 * gap // 3, 16 * (gap + 1) // 3)
                        gap += 1
                    for d in range(2):
                        tt = tiles(k if d == 0 or k == 0 else T - k)
                        if k:
                            pe.wait_ge(S["vn_ready"], hd * 8 + (2 * (k - 1) + d + 1))
                            if k == 1:
                                pe.wait_ge(S["sp_ready"], hd * 2 + (d + 1))
                        rhs = vnew[:, d, :] if k else u_all(d)[:, tt]
                        pe.matmul(bank(2 * d + 1)[:, 0:P], kdec(d)[:, tt], rhs, start=True, stop=True)
                        pe.matmul(bank(2 * d + 1)[:, P:2 * P], qkT[:, d, tt], rhs, start=True, stop=True)\
                            .then_inc(S["s_add_ps"], 1)
                    if more:
                        project(hd + 1, 16 * gap // 3, 16 * (gap + 1) // 3)
                    gap += 1
                pe.wait_ge(S["og_step"], hd * 3 + 3)
                for t in range(T):
                    mm = pe.transpose(PP[0][:, tiles(t)], og[:, tiles(t)], ident)
                    if t == 0 and more:
                        mm.then_inc(S["slot_free"], 2)
                mm.then_inc(S["ogT_ps"], 1)

            pe.wait_ge(S["z_ready"], 2 * T)
            pe.wait_ge(S["gate_act"], 5)
            project(0, 0, 48)
            pe.wait_ge(S["q_k_v_ps"], 3)
            pe.sem_inc(S["slot_free"], 2)
            with pe.Fori(0, H - 1) as hd:
                head(hd, True)
            head(H - 1, False)
            ring.base += 3 * H

            pe.wait_ge(S["oT_ready"], H + 1)
            for n in range(2):
                for a in range(2):
                    gemm5(2 * n + a, 4, lhs_o, 4 * a, a == 0, a == 1, S["res_ps"],
                          free=(lambda t: pe.wait_ge(S["res_step"], 2 * (t + 1))) if n else None)
                pe.wait_ge(S["res_ps"], T * (n + 1))
                pe.sem_inc(S["slot_free"], 2)
            ring.base += 4

            def ffn(l):
                f = F[l]

                def xs_group(i, t, g, b):
                    pe.wait_ge(f["xTl_ready"], 2 * (i + t) + (g + 1))
                    for k in range(4):
                        mm = pe.transpose(bank(b)[:, k * P:(k + 1) * P],
                                          xs_stage[:, t, (4 * g + k) * P:(4 * g + k + 1) * P], ident)
                    mm.then_inc(f["xsT_ps"], 1)

                def h_group(q, j, t):
                    pe.wait_ge(f["h_done"], q + 1)
                    pe.wait_ge(f["hTl_ready"], q + 1)
                    for c in range(2 if j < 5 else 1):
                        mm = pe.transpose(bank(7)[:, c * P:(c + 1) * P], hbuf[:, t, c * P:(c + 1) * P], ident)
                    mm.then_inc(f["hT_ps"], 1)

                def nest(n, body, t=0):
                    body(t)
                    if t + 1 < T:
                        if isinstance(n, int):
                            nest(n, body, t + 1)
                        else:
                            with pe.If(n > t + 1):
                                nest(n, body, t + 1)

                def half(e, m, n, hi, lo, c0, bk, first, last, done, width, free, after=None):
                    k, s = m // 2, m % 2
                    nk = half_rows(k, s)
                    pe.wait_ge(slot_split[l][s], split_count(k, e))
                    hs = (2 * ring0 + m) % HALVES

                    def tile(t):
                        if first:
                            free(t)
                        tt = slice(t * P, (t + 1) * P)
                        for c in range(nk):
                            wh, wl = whi[:, hs, c, 0:width], wlo[:, hs, c, 0:width]
                            out = bank(bk(t))[:, 0:width]
                            pe.matmul(out, hi[:, c0 + c, tt], wh, start=(first and c == 0), stop=False)
                            pe.matmul(out, lo[:, c0 + c, tt], wh, start=False, stop=False)
                            mm = pe.matmul(out, hi[:, c0 + c, tt], wl, start=False, stop=(last and c == nk - 1))
                        mm.then_inc(done if last else f["half_done"], 1)
                        if after is not None:
                            after(t)
                    nest(n, tile)

                ring0 = 0
                if l == 0:
                    n0 = T
                else:
                    pe.wait_ge(S["tbl_ready"], 1)
                    n0 = pe.value_load(tbl[0:1, 0, 0:1], min_val=1, max_val=T)
                pe.wait_ge(f["xs_in"], n0 * 16)
                for g in range(2):
                    xs_group(0, 0, g, 6 + g)
                for t in range(1, T):
                    if l == 0:
                        for g in range(2):
                            xs_group(0, t, g, 6 + g)
                    else:
                        with pe.If(n0 > t):
                            for g in range(2):
                                xs_group(0, t, g, 6 + g)

                with pe.Fori(0, 8 if l else 2) as e:
                    if l:
                        n = pe.value_load(tbl[0:1, 0, bass.ds(e, 1)], min_val=1, max_val=T)
                        n2 = pe.value_load(tbl[0:1, 0, bass.ds(e + 1, 1)], min_val=1, max_val=T)
                        c = pe.value_load(tbl[0:1, 1, bass.ds(e, 1)], min_val=0, max_val=SLOTS)
                    else:
                        n, n2, c = T, T, e * T
                    pe.wait_ge(f["xTl_ready"], (c + n) * 2 + 1)
                    for j in range(6):
                        bk = (lambda t, j=j: t if j % 2 == 0 or t > 1 else 5 + t)
                        def free(t, j=j):
                            if t < 2 and j < 2:
                                if j:
                                    pe.wait_ge(f["y_copied"], c * 2 + 1)
                            elif j == 0:
                                pe.wait_ge(f["y_copied"], c * 2 + 1)
                            else:
                                pe.wait_ge(f["h_done"], c * 6 + n * (j - 1 if t > 1 else j - 2) + (t + 1))
                        for s in range(4):
                            after = None
                            if s == 1 and j:
                                after = lambda t, j=j: h_group(c * 6 + n * (j - 1) + t, j - 1, t)
                            half(e, 4 * j + s, n, xTh, xTl, 2 * s, bk, s == 0, s == 3, f["gu_ps"],
                                 512 if j < 5 else 256, free, after)
                    pe.wait_ge(f["xs_in"], (c + n + n2) * 16)
                    for a in range(2):
                        bk = (lambda t, a=a: t if a == 0 or t > 1 else 5 + t)
                        free = (lambda t: pe.wait_ge(f["y_copied"], c * 2 + (t + 2))) if a else \
                            (lambda t: pe.wait_ge(f["h_done"], c * 6 + n * 5 + (t + 1)) if t > 1 else None)
                        for s in range(6):
                            m = 6 * a + s
                            if a == 0 and s == 0:
                                pe.wait_ge(f["hTl_ready"], c * 6 + n * 5 + 1)
                            after = (lambda t: h_group(c * 6 + n * 5 + t, 5, t)) if m == 1 else None
                            half(e, 24 + m, n, hTh, hTl, 2 * s, bk, s == 0, s == 5, f["down_ps"], 512,
                                 free if a == 0 else (lambda t: free(t) if t > 1 else None), after)
                            if m == 2:
                                pe.wait_ge(f["hTl_ready"], c * 6 + n * 6 + 1)
                            if m == 11:
                                pe.wait_ge(f["y_copied"], c * 2 + n + 1)
                            if m >= 2:
                                t2, g = (m - 2) // 2, m % 2
                                if t2 == 0 or l == 0:
                                    xs_group(c + n, t2, g, 7)
                                else:
                                    with pe.If(n2 > t2):
                                        xs_group(c + n, t2, g, 7)
                ring.base += 18 * (8 if l else 2) + 2

            ffn(0)
            s = slot(0)
            wpv = wring[:, s, :, :].rearrange("p a (b n) -> p (a b) n", n=256)
            hp = hrow
            for t in range(T):
                kind = POOL + (len(WINDOWS) if t else 0)
                pe.wait_ge(S["hrow_ready"], 2 * (T + t + 1))
                if t >= 2:
                    pe.wait_ge(S["poolT_sb"], t - 1)
                for k in range(KD):
                    mm = pe.matmul(PP[t % 2][:, k * P:(k + 1) * P], hp[:, t, k * P:(k + 1) * P],
                                   cm[:, kind + k // 2, :], start=True, stop=True)
                mm.then_inc(S["poolT_ps"], 1)
                pe.wait_ge(S["poolT_sb"], t + 1)
                if t >= 2:
                    pe.wait_ge(S["pool_step"], 5 * (t - 1))
                for g in range(4):
                    for k in range(2):
                        mm = pe.matmul(PP[2 + t % 2][:, g * 256:(g + 1) * 256],
                                       pT[:, t % 2, (2 * g + k) * P:(2 * g + k + 1) * P],
                                       wpv[:, 2 * g + k, :], start=(k == 0), stop=(k == 1))
                mm.then_inc(S["pool_ps"], 1)
            pe.wait_ge(S["pool_ps"], T)
            pe.sem_inc(S["slot_free"], 2)
            ring.base += 1
            for t in range(T):
                pe.wait_ge(S["hrow_ready"], 2 * (2 * T + t + 1))
                if t >= 2:
                    pe.wait_ge(S["hcol_ready"], t - 1)
                for k in range(KD):
                    mm = pe.transpose(PP[t % 2][:, k * P:(k + 1) * P], hrow[:, t, k * P:(k + 1) * P], ident)
                mm.then_inc(S["hcol_ps"], 1)
            pe.wait_ge(S["hcol_ready"], T)
            for t in range(T):
                for k in range(KD):
                    mm = pe.matmul(bank(4)[:, 8 * t:8 * t + 8], hcol[:, k, t * P:(t + 1) * P], rw[:, k, :],
                                   start=(k == 0), stop=(k == KD - 1))
            mm.then_inc(S["logit_ps"], 1)
            pe.wait_ge(S["route_step"], ROUTE_SEL)
            for i, m in enumerate((LT, ONES)):
                mm = pe.matmul(bank(5)[:, 40 * i:40 * i + 40], cmat(m), rt[:, 10, :, :], start=True, stop=True)
            mm.then_inc(S["rank_ps"], 1)
            ffn(1)

        @block.gpsimd
        def _(pool):
            pool.memset(mhalf[:, :], -0.5).then_inc(S["pool_const"], 1)
            pool.memset(cbuf, 0.0).then_inc(S["cbuf_zero"], 1)
            pool.memset(zeros[:, :], 0.0).then_inc(S["pool_const"], 1)
            pool.wait_ge(S["pool_const"], 1)

            def load_rows(n, layer, which, ln):
                for r in range(2):
                    pool.dma_start(rows[:, r, :], mod_dram[layer, r, which * D:(which + 1) * D].partition_broadcast(P))\
                        .then_inc(S["rows_in"], 16)
                pool.dma_start(rows[:, 2, :], A["ln_g"][layer, ln].partition_broadcast(P)).then_inc(S["rows_in"], 16)
                pool.dma_start(rows[:, 3, :], A["ln_b"][layer, ln].partition_broadcast(P)).then_inc(S["rows_in"], 16)

            def load_mod_rows(layer, sub):
                for r in range(2):
                    for i in range(2):
                        w = 3 * sub + 1 - i
                        pool.dma_start(mrows[:, 2 * i + r, :], mod_dram[layer, r, w * D:(w + 1) * D].partition_broadcast(P))\
                            .then_inc(S["mrows_in"], 16)

            def low_halves(l):
                ring_p = ring_of[l]

                def low(k, e):
                    w = 256 if k in (10, 11) else 512
                    hs = 2 * k % HALVES
                    pool.wait_ge(S["slot_hi"], hi_count(l, 2 * k, e))
                    pool.tensor_tensor(wlo[:, hs, :, 0:w], wring[:, ring_p.slot(k), 0:2, 0:w],
                                       whi[:, hs, :, 0:w].bitcast(F32), ALU.subtract).then_inc(slot_split[l][0], 1)
                with pool.Fori(0, 8 if l else 2) as e:
                    for k in range(18):
                        low(k, e)
                for k in range(2):
                    low(k, 8 if l else 2)

            def after_ln(n, mod=True):
                for t in range(T + 1):
                    m = n * T + t
                    if t < T:
                        pool.wait_ge(S["ln_step"], m * LN_STEPS + 3)
                        pool.tensor_scalar(rstd[:, 0, t:t + 1], lnmv[:, t, 1:2], EPS, None, ALU.add).then_inc(S["ln_rstd"], 1)
                        pool.wait_ge(S["ln_rstd"], 2 * m + 1)
                        pool.tensor_tensor(rstd[:, 1, t:t + 1], rstd[:, 0, t:t + 1], mhalf[:, 0:1], ALU.pow)\
                            .then_inc(S["ln_rstd"], 1)
                    if t and mod:
                        r = 1 if t > 1 else 0
                        pool.wait_ge(S["ln_step"], m * LN_STEPS)
                        if t == 1:
                            pool.wait_ge(S["mrow1"], n + 1)
                        pool.tensor_tensor(hrow[:, t - 1, :], x[:, t - 1, :], mrows[:, r, :], ALU.mult)\
                            .then_inc(S["hrow_ready"], 1)
                        pool.wait_ge(S["hrow_ready"], 2 * m - 1)
                        pool.tensor_tensor(hrow[:, t - 1, :], hrow[:, t - 1, :], mrows[:, 2 + r, :], ALU.add)\
                            .then_inc(S["hrow_ready"], 1)

            for l in range(2):
                pool.sem_inc(slot_split[l][0], RING)
            pool.wait_ge(S["pool_const"], 2)
            for b in range(3):
                pool.wait_ge(mod_out[b], 16 * 8 + 1)
            pool.dma_start(modcol_in[:, :], mod_dram[0].rearrange("r (a p) -> (r a) p", p=P)).then_inc(modcol_in_s, 16)
            pool.wait_ge(S["modcol_ready"], 1)
            pool.dma_start(modcol_in[:, :], mod_dram[1].rearrange("r (a p) -> (r a) p", p=P)).then_inc(modcol_in_s, 16)
            for dst in (xs_dram, ys_dram[2 * T * P:, :]):
                rows_in_tile = dst.rearrange("(p r) (c d) -> p (r c) d", p=P, d=256)
                pool.dma_start(rows_in_tile, zeros[:, :].rearrange("p (o d) -> p o d", o=1)
                               .to_broadcast([P, rows_in_tile.shape[1], 256])).then_inc(S["xs_zero"], 16)

            with pool.Fori(0, H) as hd:
                pool.wait_ge(S["oT_ready"], hd + 1)
                pool.wait_ge(S["gate_step"], 8)
                for j, (m, d) in enumerate(((GT, 0), (LE, 0), (LT, 1), (GE, 1))):
                    pool.tensor_tensor(per_tile(gm[:, j, :]), mat_bc(m), col_bc(gcol(G_, d, hd)), ALU.mult)\
                        .then_inc(S["gm_ready"], 1)
                for c in range(2):
                    pool.wait_ge(S["ss_done"], hd * 4 + 2 * (c + 1))
                    pool.tensor_tensor(ss[:, 4 + c, :], ss[:, 2 + c, :], mhalf[:, :], ALU.pow).then_inc(S["rn_step"], 1)
                for d in range(2):
                    pool.tensor_tensor(per_tile(invT[:, d, :]), mat_bc(IDENT), mat_bc(ONES), ALU.mult)\
                        .then_inc(S["inv_init"], 1)
                for n in range(2 * LEVELS):
                    lv, d = n // 2, n % 2
                    pool.wait_ge(S["a_step"], hd * 4 + (2 * d + 2))
                    if n >= 2:
                        pool.wait_ge(S["vt_ps"], hd * 14 + (n - 1))
                        if n < 4:
                            pool.wait_ge(S["inv_init"], hd * 4 + (n + 1))
                    else:
                        pool.wait_ge(S["conv_step"], hd * 15 + 15)
                    pool.tensor_tensor(per_tile(offd[:, d, :]), per_tile(ex[:, 2 * d, :]),
                                       mat_bc(LEVEL + LEVELS * d + lv), ALU.mult).then_inc(S["off_ready"], 1)
                    if n < 2:
                        pool.wait_ge(S["off_ready"], hd * 14 + (n + 1))
                        pool.tensor_tensor(per_tile(inv[:, d, :]), mat_bc(IDENT), per_tile(offd[:, d, :]), ALU.subtract)\
                            .then_inc(S["inv_init"], 1)
                pool.wait_ge(S["decay_ps"], hd * 4 + 4)
                pool.wait_ge(S["v_ready"], hd + 1)
                for d in range(2):
                    pool.tensor_tensor(per_tile(R[:, d, :]), per_tile(vn_t[:, 2, :]), col_bc(gcol(BETA, d, hd)), ALU.mult)\
                        .then_inc(S["r_ready"], 1)
                for d in range(2):
                    pool.tensor_tensor(per_tile(R[:, 2 + d, :]), per_tile(vn_t[:, 1, :]), col_bc(gcol(BG, d, hd)), ALU.mult)\
                        .then_inc(S["r_ready"], 1)
                for d in range(2):
                    pool.wait_ge(S["off_ready"], hd * 14 + 14)
                    pool.tensor_tensor(per_tile(kdec(d)), per_tile(vn_t[:, 1, :]), col_bc(gcol(EK, d, hd)), ALU.mult)\
                        .then_inc(S["kdec_ready"], 1)
                pool.wait_ge(S["sso_done"], hd * 2 + 2)
                pool.tensor_tensor(ss[:, 7, :], ss[:, 6, :], mhalf[:, :], ALU.pow).then_inc(S["rno_step"], 1)

            pool.wait_ge(S["xs_zero"], 32)
            pool.wait_ge(S["oT_ready"], H + 1)
            pool.wait_ge(S["state_out"], 32 * H + 1)
            load_rows(0, 0, 2, 0)
            load_mod_rows(0, 1)
            after_ln(0)
            pool.wait_ge(S["h_out"], 16)
            pool.wait_ge(S["x_parked"], 16)
            low_halves(0)

            def combine_loads(l):
                if l:
                    pool.wait_ge(S["tbl_ready"], 1)
                    total = pool.value_load(tbl[0:1, 1, 8:9], min_val=8, max_val=SLOTS - 1)
                    ahead = pool.value_load(tbl[0:1, 1, 9:10], min_val=9, max_val=SLOTS) * 2 + 1
                else:
                    ahead = 31
                pool.wait_ge(F[l]["xTl_ready"], ahead)
                for split in slot_split[l]:
                    pool.wait_ge(split, (146 if l else 38) + RING)
                if l:
                    pool.sem_inc(S["y_in"], 1)
                    pool.wait_ge(S["y_in"], 1)
                load_rows(1 + 2 * l, l, 5, 1)
                if l == 0:
                    load_mod_rows(1, 0)
                    pool.dma_start(prow[:, 0, :], A["pool_b"][0].partition_broadcast(P)).then_inc(S["poolrows_in"], 16)
                    pool.dma_start(prow[:, 1, :], A["pool_scale"][0].partition_broadcast(P)).then_inc(S["poolrows_in"], 16)
                if l == 0:
                    pool.wait_ge(F[0]["y_out"], 16 * 20 + 1)
                else:
                    pool.wait_ge(F[1]["y_out"], total * 32 + 1)
                    pool.sem_inc(S["y_in"], 1)
                    pool.wait_ge(S["y_in"], 2)
                for t in range(T):
                    for i, dst in enumerate((yA, yB)):
                        if l == 0:
                            pool.dma_start(dst[:, t, :], ys_dram[(i * T + t) * P:(i * T + t + 1) * P, :])\
                                .then_inc(yg_in[t], 16)
                        else:
                            pool.indirect_dma_start(dst[:, t, :], None, ys_dram[:, :],
                                                    bass.IndirectOffsetOnAxis(ap=pos[:, i, t:t + 1].bitcast(U32), axis=0))\
                                .then_inc(yg_in[t], 16)

            combine_loads(0)
            after_ln(1)
            pool.wait_ge(S["ln_step"], 2 * T * LN_STEPS)
            load_rows(2, 1, 2, 0)
            pool.wait_ge(S["hrow_ready"], 4 * T)
            load_mod_rows(1, 1)
            after_ln(2)
            pool.wait_ge(S["tbl_ready"], 1)
            pool.wait_ge(S["hrow_ready"], 6 * T)
            for t in range(T):
                for i in range(2):
                    pool.indirect_dma_start(xs_dram[:, :], bass.IndirectOffsetOnAxis(ap=pos[:, i, t:t + 1].bitcast(U32), axis=0),
                                            hrow[:, t, :], None).then_inc(S["xs_scattered"], 16)
            pool.wait_ge(S["xs_scattered"], 160)
            pool.wait_ge(S["x_parked"], 32)
            low_halves(1)
            combine_loads(1)
            after_ln(3, mod=False)

        @block.scalar
        def _(act):
            act.sem_inc(S["oT_ready"], 1)
            act.sem_inc(S["state_out"], 1)
            for b in range(3):
                act.sem_inc(mod_out[b], 1)
            for l in range(2):
                for n in ("hTh_ready", "xTh_ready", "y_copied", "y_out"):
                    act.sem_inc(F[l][n], 1)
            act.wait_ge(S["cond_ps"], 1)
            act.activation(cs[:, :], PP[3][:, 0:16], ACT.Silu).then_inc(S["cond_ready"], 1)
            for layer in range(2):
                bv = A["ada_b"][layer]
                with act.Fori(0, 4) as i:
                    for b in range(3):
                        act.wait_ge(S["mod_row"], i * 3 + (12 * layer + b + 1))
                        act.dma_start(brow[:, b, :], bv[bass.ds(i * 1536 + 512 * b, 512)].partition_broadcast(2))\
                            .then_inc(bias_in[b], 16)
                    for b in range(3):
                        act.wait_ge(S["mod_row"], i * 3 + (12 * layer + b + 4))
                        act.dma_start(mod_dram[layer, :, bass.ds(i * 1536 + 512 * b, 512)], mrow[:, b, :])\
                            .then_inc(mod_out[b], 16)
            for n in range(2):
                for t in range(T):
                    act.wait_ge(S["z_ps"], T * n + t + 1)
                    act.activation(acc[:, t, 512 * n:512 * n + 512], bank(t), ACT.Silu).then_inc(S["z_ready"], 1)
            act.wait_ge(S["gate_step"], 2)
            act.activation(gates5[:, SPA, :, :], gates5[:, SPA, :, :], ACT.Exp, scale=-1.0).then_inc(S["gate_act"], 1)
            act.activation(gates5[:, TMP, :, :], gates5[:, AB0, :, :], ACT.Exp, scale=-1.0).then_inc(S["gate_act"], 1)
            act.activation(alog[:, :], alog[:, :], ACT.Exp).then_inc(S["gate_act"], 1)
            act.wait_ge(S["gate_act"], 1)
            act.activation(gates5[:, SPB, :, :], gates5[:, SPA, :, :], ACT.Ln, bias=1.0).then_inc(S["gate_act"], 1)
            act.wait_ge(S["cum_ps"], 1)
            cum = bank(7)[:, 0:240].rearrange("p (s q) -> p s q", s=3)
            act.activation(gates5[:, EG:EG + 3, :, :].rearrange("p s t h -> p s (t h)"), cum, ACT.Exp).then_inc(S["gate_act"], 1)

            def conv_input(h, c):
                act.wait_ge(S["q_k_v_ps"], h * 3 + (c + 1))
                act.wait_ge(S["cbuf_zero"], h + 1)
                ps = PP[3 if c == 1 else 2]
                act.activation(cbuf[:, c, 2:130], ps[:, 0:P], ACT.Copy)
                act.activation(cbuf[:, c, 134:646], ps[:, P:NT], ACT.Copy).then_inc(S["conv_in"], 1)

            def conv_silu(h, c):
                act.wait_ge(S["conv_step"], h * 15 + 5 * (c + 1))
                act.activation(cv[:, c, :], cv[:, c, :], ACT.Silu).then_inc(S["silu_done"], 1)

            def head(hd, more):
                act.wait_ge(S["oT_ready"], hd + 1)
                for d in range(2):
                    act.dma_start(state[:, d, :], A["state_dn"][0, 0, d, bass.ds(hd, 1)].rearrange("a k v -> (a k) v"))\
                        .then_inc(S["state_in"], 16)
                for c in range(2):
                    act.wait_ge(S["tok_ps"], hd * 3 + (c + 1))
                    act.activation(sq[:, c, :], PP[c][:, 0:NT], ACT.Square).then_inc(S["sq_done"], 1)
                act.wait_ge(S["tok_ps"], hd * 3 + 3)
                act.activation(vn_t[:, 2, :], PP[2][:, 0:NT], ACT.Copy).then_inc(S["v_ready"], 1)
                for c in range(2):
                    act.wait_ge(S["head_ps"], hd * 2 + (c + 1))
                    act.activation(qTk[:, c, :], PP[c][:, 0:NT], ACT.Copy).then_inc(S["qkT_ready"], 1)
                for c, dst in enumerate((kk, qk)):
                    act.wait_ge(S["gram_ps"], hd * 2 + (c + 1))
                    act.activation(dst, PP[2 + c][:, 0:NT], ACT.Copy).then_inc(S["gram_sb"], 1)
                for j in range(4):
                    act.wait_ge(S["decay_ps"], hd * 4 + (j + 1))
                    act.activation(ex[:, j, :], PP[j][:, 0:NT], ACT.Exp).then_inc(S["ex_ready"], 1)
                for n in range(2, 2 * LEVELS):
                    d = n % 2
                    act.wait_ge(S["vt_ps"], hd * 14 + (n + 1))
                    act.activation(vt[:, d, :], PP[d][:, 0:NT], ACT.Copy).then_inc(S["vt_sb"], 1)
                for d in range(2):
                    act.wait_ge(S["u_ps"], hd * 2 + (d + 1))
                    act.activation(u_all(d), PP[d][:, 0:NT], ACT.Copy).then_inc(S["u_sb"], 1)
                    act.wait_ge(S["wt_ps"], hd * 2 + (d + 1))
                    act.activation(wT(d), PP[2 + d][:, 0:NT], ACT.Copy).then_inc(S["wt_sb"], 1)
                for d in range(2):
                    act.wait_ge(S["s_add_ps"], hd * 10 + (d + 1))
                    act.wait_ge(S["state_out"], hd * 32 + 1)
                    act.activation(state_new[:, d, :], bank(2 * d + 1)[:, 0:P], ACT.Copy).then_inc(S["sp_ready"], 1)
                for d in range(2):
                    act.wait_ge(S["sp_ready"], hd * 2 + (d + 1))
                    act.dma_start(out_state[0, 0, d, bass.ds(hd, 1)].rearrange("a k v -> (a k) v"), state_new[:, d, :])\
                        .then_inc(S["state_out"], 16)
                if more:
                    conv_input(hd + 1, 0)
                    conv_input(hd + 1, 1)
                    conv_silu(hd + 1, 0)
                    conv_input(hd + 1, 2)
                act.wait_ge(S["o_upd"], hd * 19 + 19)
                act.activation(invT[:, 0, :], oacc, ACT.Square).then_inc(S["sqo_done"], 1)
                if more:
                    conv_silu(hd + 1, 1)
                act.wait_ge(S["ogT_ps"], hd + 1)
                act.activation(oT[:, bass.ds(hd, 1), :].rearrange("p a t -> p (a t)"), PP[0][:, 0:NT], ACT.Copy)\
                    .then_inc(S["oT_ready"], 1)
                if more:
                    conv_silu(hd + 1, 2)

            for c in range(3):
                conv_input(0, c)
            for c in range(3):
                conv_silu(0, c)
            with act.Fori(0, H - 1) as hd:
                head(hd, True)
            head(H - 1, False)
            act.wait_ge(S["state_out"], 32 * H + 1)

            def slot_row(tile):
                return tile.with_bounds(min_val=0, max_val=SLOTS - 1) * P

            def ffn(l):
                f = F[l]

                ring_v = ring_of[l]

                def high(k, s, e=0, per=0):
                    nk = half_rows(k, s)
                    w = 256 if k in (10, 11) else 512
                    hs = (2 * k + s) % HALVES
                    if s == 0:
                        act.wait_ge(slot_loaded[ring_v.slot(k)], ring_v.loaded(k, e, per))
                    act.activation(whi[:, hs, 0:nk, 0:w], wring[:, ring_v.slot(k), 2 * s:2 * s + nk, 0:w], ACT.Copy)\
                        .then_inc(S["slot_hi"], 1)

                def high_after(m, e, c, n):
                    if m < 24:
                        j, s = m // 4, m % 4
                        if s < 3:
                            act.wait_ge(f["half_done"], c * 28 + n * (3 * j + s + 1))
                        else:
                            act.wait_ge(f["gu_ps"], c * 6 + n * (j + 1))
                    else:
                        a, s = (m - 24) // 6, (m - 24) % 6
                        if s < 5:
                            act.wait_ge(f["half_done"], c * 28 + n * (18 + 5 * a + s + 1))
                        else:
                            act.wait_ge(f["down_ps"], c * 2 + n * (a + 1))
                    k = (m + 4) // 2
                    if k < 18:
                        high(k, m % 2, e, 18)
                    else:
                        nk, w, hs = 2, 512, (m + 4) % HALVES
                        if m % 2 == 0:
                            act.wait_ge(slot_loaded[ring_v.slot(k)], ring_v.loaded(k, e, 18))
                        act.activation(whi[:, hs, :, :], wring[:, ring_v.slot(k), 2 * (m % 2):2 * (m % 2) + 2, :], ACT.Copy)\
                            .then_inc(S["slot_hi"], 1)

                def load_tokens(n, c):
                    with act.Fori(0, n) as t:
                        src = xs_dram[bass.ds(slot_row(c + t), P), :] if l else h_dram[bass.ds(t * P, P), :]
                        act.dma_start(xs_stage[:, bass.ds(t, 1), :].rearrange("p a d -> p (a d)"), src)\
                            .then_inc(f["xs_in"], 16)

                def xs_high(i, t, g, b):
                    act.wait_ge(f["xsT_ps"], 2 * (i + t) + (g + 1))
                    act.activation(xTh[:, 4 * g:4 * g + 4, t * P:(t + 1) * P],
                                   bank(b).rearrange("p (k t) -> p k t", k=4), ACT.Copy).then_inc(f["xTh_ready"], 1)

                def h_high(q0, n, j):
                    nk = 2 if j < 5 else 1
                    with act.Fori(0, n) as t:
                        act.wait_ge(f["hT_ps"], q0 + t + 1)
                        act.activation(hTh[:, 2 * j:2 * j + nk, bass.ds(t * P, P)],
                                       bank(7)[:, 0:nk * P].rearrange("p (k t) -> p k t", k=nk), ACT.Copy)\
                            .then_inc(f["hTh_ready"], 1)

                def silus(q0, n, j):
                    w = 256 if j < 5 else 128
                    for t in range(T):
                        b = t if j % 2 == 0 or t > 1 else 5 + t

                        def one(t=t, b=b):
                            act.wait_ge(f["gu_ps"], q0 + (t + 1))
                            act.activation(hbuf[:, t, 0:w], bank(b)[:, 0:w], ACT.Silu).then_inc(f["sil_done"], 1)
                        if t == 0 or l == 0:
                            one()
                        else:
                            with act.If(n > t):
                                one()

                def y_out(c, n, a):
                    for t in range(T):
                        b = t if a == 0 or t > 1 else 5 + t

                        def one(t=t, b=b):
                            act.wait_ge(f["down_ps"], c * 2 + n * a + (t + 1))
                            act.wait_ge(f["y_out"], (c * 2 + n * a) * 16 + 1)
                            act.activation(ybuf[:, t, :], bank(b), ACT.Copy).then_inc(f["y_copied"], 1)
                            act.wait_ge(f["y_copied"], c * 2 + n * a + (t + 2))
                            act.dma_start(ys_dram[bass.ds(slot_row(c + t), P), 512 * a:512 * a + 512], ybuf[:, t, :])\
                                .then_inc(f["y_out"], 16)
                        if t == 0 or l == 0:
                            one()
                        else:
                            with act.If(n > t):
                                one()

                act.wait_ge(S["hrow_ready"], 2 * T * (1 + 2 * l))
                if l == 0:
                    act.dma_start(h_dram.rearrange("(t p) d -> p t d", p=P), hrow[:, :, :]).then_inc(S["h_out"], 16)
                act.dma_start(xpark.rearrange("(t p) d -> p t d", p=P), x[:, :, :]).then_inc(S["x_parked"], 16)
                if l == 0:
                    n0 = T
                    act.wait_ge(S["h_out"], 16)
                else:
                    act.wait_ge(S["tbl_ready"], 1)
                    act.wait_ge(S["xs_scattered"], 160)
                    n0 = act.value_load(tbl[0:1, 0, 0:1], min_val=1, max_val=T)
                act.wait_ge(S["x_parked"], 16 * (l + 1))
                load_tokens(n0, 0)
                for k in range(2):
                    for s in range(2):
                        high(k, s)
                for t in range(T):
                    if t == 0 or l == 0:
                        for g in range(2):
                            xs_high(0, t, g, 6 + g)
                    else:
                        with act.If(n0 > t):
                            for g in range(2):
                                xs_high(0, t, g, 6 + g)
                with act.Fori(0, 8 if l else 2) as e:
                    if l:
                        n = act.value_load(tbl[0:1, 0, bass.ds(e, 1)], min_val=1, max_val=T)
                        n2 = act.value_load(tbl[0:1, 0, bass.ds(e + 1, 1)], min_val=1, max_val=T)
                        c = act.value_load(tbl[0:1, 1, bass.ds(e, 1)], min_val=0, max_val=SLOTS)
                    else:
                        n, n2, c = T, T, e * T
                    load_tokens(n2, c + n)
                    for j in range(6):
                        high_after(4 * j, e, c, n)
                        if j:
                            h_high(c * 6 + n * (j - 1), n, j - 1)
                        high_after(4 * j + 1, e, c, n)
                        high_after(4 * j + 2, e, c, n)
                        silus(c * 6 + n * j, n, j)
                        high_after(4 * j + 3, e, c, n)
                    for m in range(12):
                        high_after(24 + m, e, c, n)
                        if m == 0:
                            h_high(c * 6 + n * 5, n, 5)
                        if m < 2:
                            continue
                        t2, g = (m - 2) // 2, m % 2
                        if t2 == 0 or l == 0:
                            xs_high(c + n, t2, g, 7)
                        else:
                            with act.If(n2 > t2):
                                xs_high(c + n, t2, g, 7)
                        if m in (5, 11):
                            y_out(c, n, m // 6)

            ffn(0)
            for t in range(T):
                act.wait_ge(S["poolT_ps"], t + 1)
                if t >= 2:
                    act.wait_ge(S["pool_ps"], t - 1)
                act.activation(pT[:, t % 2, :], PP[t % 2][:, :], ACT.Copy).then_inc(S["poolT_sb"], 1)
            for t in range(T):
                act.wait_ge(S["hcol_ps"], t + 1)
                act.activation(hcol[:, :, t * P:(t + 1) * P], PP[t % 2][:, :].rearrange("p (k t) -> p k t", k=KD), ACT.Copy)\
                    .then_inc(S["hcol_ready"], 1)
            act.wait_ge(S["route_step"], 2)
            act.activation(rt[:, 1, :, :], rt[:, 1, :, :], ACT.Exp).then_inc(S["route_act"], 1)
            ffn(1)

        @block.vector
        def _(dve):
            dve.wait_ge(S["conv_ps"], 1)
            dve.tensor_copy(convw[:, :, :].rearrange("p j c -> p (j c)"), PP[3][:, 512:632]).then_inc(S["conv_cols"], 1)
            dve.sem_inc(S["mod_row"], 3)
            for l in range(2):
                for n in ("hTl_ready", "xTl_ready"):
                    dve.sem_inc(F[l][n], 1)
                dve.sem_inc(slot_split[l][1], RING)
            for layer in range(2):
                with dve.Fori(0, 4) as i:
                    for b in range(3):
                        dve.wait_ge(S["mod_ps"], i * 3 + (12 * layer + b + 1))
                        dve.wait_ge(bias_in[b], i * 16 + (64 * layer + 16))
                        dve.wait_ge(mod_out[b], i * 16 + (64 * layer + 1))
                        dve.tensor_tensor(mrow[:, b, :], bank(b)[0:2, :], brow[:, b, :], ALU.add).then_inc(S["mod_row"], 1)
            xt_n = [0]
            for layer in range(2):
                dve.wait_ge(S["modcol_ps"], layer + 1)
                dve.tensor_copy(modc[layer], PP[3][:, 0:96]).then_inc(S["modcol_ready"], 1)
            dve.wait_ge(S["modcol_ready"], 2)

            def transposed_mod(layer, sub):
                mc = modc[layer].rearrange("p (r w k) -> p r w k", r=2, w=6)
                n = xt_n[0]
                if n:
                    dve.wait_ge(S["xt_ready"], 2 * T * n)
                dve.tensor_scalar(scp1[:, :, :], mc[:, :, 3 * sub + 1, :], 1.0, None, ALU.add).then_inc(S["scp1_ready"], 1)
                dve.wait_ge(S["scp1_ready"], n + 1)
                for t in range(T):
                    r = 1 if t else 0
                    dve.wait_ge(S["xt_ps"], n * T + t + 1)
                    for k in range(KD):
                        last = dve.tensor_scalar(xT[:, k, t * P:(t + 1) * P], PP[t % 4][:, k * P:(k + 1) * P],
                                                 scp1[:, r, k:k + 1], mc[:, r, 3 * sub, k:k + 1], ALU.mult, ALU.add)
                        if k in (KD // 2 - 1, KD - 1):
                            last.then_inc(S["xt_ready"], 1)
                xt_n[0] += 1

            transposed_mod(0, 0)
            step = [0]

            def gstep(ins):
                step[0] += 1
                ins.then_inc(S["gate_step"], 1)
                dve.wait_ge(S["gate_step"], step[0])

            dve.wait_ge(S["ab_ps"], 1)
            abv = bank(6)[:, 0:160].rearrange("p (t w) -> p t w", t=T)
            gstep(dve.tensor_copy(gates5[:, AB0, :, :], abv[:, :, 16:32]))
            dve.wait_ge(S["small_in"], 16 * 8)
            bc16 = lambda a: a.rearrange("p (o h) -> p o h", o=1).to_broadcast([P, T, 16])
            dve.tensor_tensor(gates5[:, T2, :, :], abv[:, :, 0:16], bc16(dtb[:, :]), ALU.add).then_inc(S["gate_arg"], 1)
            dve.wait_ge(S["gate_arg"], 1)
            gstep(dve.scalar_tensor_tensor(gates5[:, SPA, :, :], gates5[:, T2, :, :], -1.0, gates5[:, T2, :, :], ALU.mult, ALU.max))
            dve.wait_ge(S["gate_act"], 4)
            gstep(dve.scalar_tensor_tensor(gates5[:, SPB, :, :], gates5[:, T2, :, :], 0.0, gates5[:, SPB, :, :], ALU.max, ALU.add))
            gstep(dve.tensor_tensor(gates5[:, SPB, :, :], gates5[:, SPB, :, :], bc16(alog[:, :]), ALU.mult))
            gstep(dve.tensor_scalar(gates5[:, G_, :, :], gates5[:, SPB, :, :], -1.0, None, ALU.mult))
            gstep(dve.tensor_scalar(gates5[:, TMP, :, :], gates5[:, TMP, :, :], 1.0, None, ALU.add))
            gstep(dve.reciprocal(gates5[:, BETA, :, :], gates5[:, TMP, :, :]))
            gstep(dve.memset(gates5[:, NA, :, :], 0.0))
            dve.wait_ge(S["gate_act"], 5)
            gstep(dve.tensor_tensor(gates5[:, BG, :, :], gates5[:, BETA, :, :], gates5[:, EG, :, :], ALU.mult))

            def conv(h, c, lo, hi):
                for j in range(lo, hi):
                    wcol = convw[:, j, bass.ds(h + 8 * c, 1)]
                    if j == 0:
                        dve.wait_ge(S["conv_in"], h * 3 + (c + 1))
                        if not isinstance(h, int):
                            dve.wait_ge(S["tok_ps"], h * 3 + (c - 2))
                        ins = dve.tensor_scalar(cv[:, c, :], cbuf[:, c, 0:644], wcol, None, ALU.mult)
                    else:
                        dve.wait_ge(S["conv_step"], h * 15 + (5 * c + j))
                        ins = dve.scalar_tensor_tensor(cv[:, c, :], cbuf[:, c, j:j + 644], wcol, cv[:, c, :],
                                                       ALU.mult, ALU.add)
                    ins.then_inc(S["conv_step"], 1)

            def head(hd, more):
                dve.wait_ge(S["oT_ready"], hd + 1)
                for c in range(2):
                    dve.wait_ge(S["sq_done"], hd * 2 + (c + 1))
                    dve.tensor_reduce(ss[:, c, :], per_tile(sq[:, c, :]), AX.X, ALU.add).then_inc(S["ss_done"], 1)
                    dve.wait_ge(S["ss_done"], hd * 4 + (2 * c + 1))
                    dve.tensor_scalar(ss[:, 2 + c, :], ss[:, c, :], EPS, float(P) if c == 0 else 1.0, ALU.add, ALU.mult)\
                        .then_inc(S["ss_done"], 1)
                for c in range(2):
                    dve.wait_ge(S["rn_step"], hd * 2 + (c + 1))
                    dve.tensor_tensor(per_tile(vn_t[:, c, :]), per_tile(PP[c][:, 0:NT]),
                                      col_bc(ss[:, 4 + c, :].rearrange("p (t o) -> p t o", o=1)), ALU.mult)\
                        .then_inc(S["qkn"], 1)
                dve.wait_ge(S["gram_sb"], hd * 2 + 2)
                for d in range(2):
                    dve.wait_ge(S["ex_ready"], hd * 4 + (2 * d + 1))
                    a = ex[:, 2 * d, :]
                    dve.tensor_tensor(a, a, kk, ALU.mult).then_inc(S["a_step"], 1)
                    dve.wait_ge(S["a_step"], hd * 4 + (2 * d + 1))
                    dve.tensor_tensor(per_tile(a), per_tile(a), col_bc(gcol(BETA, d, hd)), ALU.mult).then_inc(S["a_step"], 1)
                for d in range(2):
                    dve.wait_ge(S["ex_ready"], hd * 4 + (2 * d + 2))
                    w = ex[:, 2 * d + 1, :]
                    dve.tensor_tensor(w, w, qk, ALU.mult).then_inc(S["w_step"], 1)
                    dve.wait_ge(S["w_step"], hd * 4 + (2 * d + 1))
                    dve.tensor_tensor(per_tile(qkT[:, d, :]), per_tile(w), mat_bc(GE if d else LE), ALU.mult)\
                        .then_inc(S["w_step"], 1)
                dve.wait_ge(S["a_step"], hd * 4 + 4)
                dve.memset(oacc, 0.0).then_inc(S["o_upd"], 1)
                for n in range(2 * LEVELS):
                    d = n % 2
                    if n < 2:
                        dve.wait_ge(S["inv_init"], hd * 4 + 2)
                        dve.wait_ge(S["vt_ps"], hd * 14 + (n + 1))
                    else:
                        dve.wait_ge(S["upd_x_ps"], hd * 12 + (n - 1))
                        dve.wait_ge(S["inv_upd"], hd * 24 + upd_count(n - 2))
                    dve.tensor_tensor(invT[:, d, :], invT[:, d, :], PP[d][:, 0:NT], ALU.subtract).then_inc(S["inv_upd"], 1)
                    if 2 <= n < 12:
                        dve.wait_ge(S["upd_y_ps"], hd * 10 + (n - 1))
                        dve.tensor_tensor(inv[:, d, :], inv[:, d, :], PP[2 + d][:, 0:NT], ALU.subtract).then_inc(S["inv_upd"], 1)
                if more:
                    dve.wait_ge(S["vt_ps"], hd * 14 + 14)
                    dve.memset(cbuf[:, :, 0:2], 0.0)
                    dve.memset(cbuf[:, :, 130:134], 0.0)
                    dve.memset(cbuf[:, :, 646:648], 0.0).then_inc(S["cbuf_zero"], 1)
                n_o = 1
                for k in range(T):
                    for d in range(2):
                        t = k if d == 0 or k == 0 else T - k
                        tt = slice(t * P, (t + 1) * P)
                        if k:
                            dve.wait_ge(S["s_read_ps"], hd * 8 + (2 * (k - 1) + d + 1))
                            dve.wait_ge(S["u_sb"], hd * 2 + 2)
                            dve.tensor_tensor(vnew[:, d, :], u_all(d)[:, tt], bank(2 * d)[:, 0:P], ALU.subtract)\
                                .then_inc(S["vn_ready"], 1)
                            dve.wait_ge(S["o_upd"], hd * 19 + n_o)
                            dve.scalar_tensor_tensor(oacc[:, tt], bank(2 * d)[:, P:2 * P],
                                                     gates5[:, EG, t, bass.ds(hd + 8 * d, 1)], oacc[:, tt],
                                                     ALU.mult, ALU.add).then_inc(S["o_upd"], 1)
                            n_o += 1
                    if more and k in (3, 4):
                        conv(hd + 1, k - 3, *((2, 5) if k == 3 else (0, 2)))
                    for d in range(2):
                        t = k if d == 0 or k == 0 else T - k
                        tt = slice(t * P, (t + 1) * P)
                        dve.wait_ge(S["s_add_ps"], hd * 10 + (2 * k + d + 1))
                        if k == 0:
                            dve.wait_ge(S["sp_ready"], hd * 2 + (d + 1))
                        if 0 < k < T - 1:
                            if k == 1:
                                dve.wait_ge(S["state_in"], hd * 32 + 32)
                            else:
                                dve.wait_ge(S["s_upd"], hd * 6 + (2 * (k - 2) + d + 1))
                            dve.scalar_tensor_tensor(state[:, d, :], state[:, d, :],
                                                     gates5[:, EL, t, bass.ds(hd + 8 * d, 1)],
                                                     bank(2 * d + 1)[:, 0:P], ALU.mult, ALU.add).then_inc(S["s_upd"], 1)
                        dve.wait_ge(S["o_upd"], hd * 19 + n_o)
                        dve.tensor_tensor(oacc[:, tt], oacc[:, tt], bank(2 * d + 1)[:, P:2 * P], ALU.add).then_inc(S["o_upd"], 1)
                        n_o += 1
                    if more and k in (2, 4):
                        conv(hd + 1, (k - 2) // 2, *((0, 2) if k == 2 else (2, 5)))
                assert n_o == 19
                dve.wait_ge(S["sqo_done"], hd + 1)
                dve.tensor_reduce(ss[:, 6, :], per_tile(invT[:, 0, :]), AX.X, ALU.add).then_inc(S["sso_done"], 1)
                dve.wait_ge(S["sso_done"], hd * 2 + 1)
                dve.tensor_scalar(ss[:, 6, :], ss[:, 6, :], 1.0 / P, EPS, ALU.mult, ALU.add).then_inc(S["sso_done"], 1)
                if more:
                    conv(hd + 1, 2, 0, 1)
                dve.wait_ge(S["rno_step"], hd + 1)
                dve.tensor_tensor(per_tile(og), per_tile(oacc), col_bc(ss[:, 7, :].rearrange("p (t o) -> p t o", o=1)),
                                  ALU.mult).then_inc(S["og_step"], 1)
                dve.wait_ge(S["og_step"], hd * 3 + 1)
                dve.tensor_tensor(per_tile(og), per_tile(og),
                                  ngb[:, :].rearrange("p (o c) -> p o c", o=1).to_broadcast([P, T, P]), ALU.mult)\
                    .then_inc(S["og_step"], 1)
                dve.wait_ge(S["og_step"], hd * 3 + 2)
                dve.tensor_tensor(per_tile(og), per_tile(og), acc[:, :, bass.ds(hd * P, P)], ALU.mult)\
                    .then_inc(S["og_step"], 1)
                if more:
                    conv(hd + 1, 2, 1, 5)

            for c in range(3):
                conv(0, c, 0, 5)
            with dve.Fori(0, H - 1) as hd:
                head(hd, True)
            head(H - 1, False)

            def layer_norm(n, t):
                base = (n * T + t) * LN_STEPS
                xt = x[:, t, :]
                for a in range(2):
                    dve.bn_stats(lnst[:, t, a, :], x[:, t, 512 * a:512 * a + 512]).then_inc(S["ln_step"], 1)
                dve.wait_ge(S["ln_step"], base + 2)
                dve.bn_aggr(lnmv[:, t, :], lnst[:, t, :, :].rearrange("p a b -> p (a b)")).then_inc(S["ln_step"], 1)
                dve.wait_ge(S["ln_step"], base + 3)
                if t == 0 and n < 3:
                    dve.wait_ge(S["mrows_in"], 64 * (n + 1))
                    dve.tensor_scalar(mrows[:, 0:2, :], mrows[:, 0:2, :], 1.0, None, ALU.add).then_inc(S["mrow1"], 1)
                dve.wait_ge(S["ln_rstd"], 2 * (n * T + t) + 2)
                dve.tensor_scalar(xt, xt, lnmv[:, t, 0:1], rstd[:, 1, t:t + 1], ALU.subtract, ALU.mult)\
                    .then_inc(S["ln_step"], 1)
                dve.wait_ge(S["ln_step"], base + 4)
                dve.tensor_tensor(xt, xt, rows[:, 2, :], ALU.mult).then_inc(S["ln_step"], 1)
                dve.wait_ge(S["ln_step"], base + 5)
                dve.tensor_tensor(xt, xt, rows[:, 3, :], ALU.add).then_inc(S["ln_step"], LN_STEPS - 5)

            res_n = [0]

            def rstep(ins):
                res_n[0] += 1
                ins.then_inc(S["res_step"], 1)
                return res_n[0]

            dve.wait_ge(S["rows_in"], 64)
            for n in range(2):
                for t in range(T):
                    dve.wait_ge(S["res_ps"], T * n + t + 1)
                    cols = slice(512 * n, 512 * n + 512)
                    tmp = lnt[:, t, cols]
                    v = rstep(dve.tensor_tensor(tmp, bank(t), rows[:, 1 if t else 0, cols], ALU.mult))
                    dve.wait_ge(S["res_step"], v)
                    v = rstep(dve.scalar_tensor_tensor(x[:, t, cols], x[:, t, cols], ALPHA, tmp, ALU.mult, ALU.add))
                    if n:
                        dve.wait_ge(S["res_step"], v)
                        layer_norm(0, t)

            def rwait(ins):
                dve.wait_ge(S["res_step"], rstep(ins))

            def ffn(l):
                f = F[l]
                ring_v = ring_of[l]
                n_exp = 8 if l else 2

                def low(m, e):
                    k = m // 2
                    nk = half_rows(k, 1)
                    w = 256 if k in (10, 11) else 512
                    hs = m % HALVES
                    dve.wait_ge(S["slot_hi"], hi_count(l, m, e))
                    dve.tensor_tensor(wlo[:, hs, 0:nk, 0:w], wring[:, ring_v.slot(k), 2:2 + nk, 0:w],
                                      whi[:, hs, 0:nk, 0:w].bitcast(F32), ALU.subtract).then_inc(slot_split[l][1], 1)

                def xs_low(i, t, g, b):
                    dve.wait_ge(f["xTh_ready"], 2 * (i + t) + (g + 2))
                    dst = (slice(None), slice(4 * g, 4 * g + 4), slice(t * P, (t + 1) * P))
                    dve.tensor_tensor(xTl[dst], bank(b).rearrange("p (k t) -> p k t", k=4), xTh[dst].bitcast(F32),
                                      ALU.subtract).then_inc(f["xTl_ready"], 1)

                def h_low(q0, n, j):
                    nk = 2 if j < 5 else 1
                    with dve.Fori(0, n) as t:
                        dve.wait_ge(f["hTh_ready"], q0 + t + 2)
                        dve.tensor_tensor(hTl[:, 2 * j:2 * j + nk, bass.ds(t * P, P)],
                                          bank(7)[:, 0:nk * P].rearrange("p (k t) -> p k t", k=nk),
                                          hTh[:, 2 * j:2 * j + nk, bass.ds(t * P, P)].bitcast(F32), ALU.subtract)\
                            .then_inc(f["hTl_ready"], 1)

                def products(q0, n, j):
                    w = 256 if j < 5 else 128
                    for t in range(T):
                        b = t if j % 2 == 0 or t > 1 else 5 + t

                        def one(t=t, b=b):
                            dve.wait_ge(f["sil_done"], q0 + (t + 1))
                            dve.tensor_tensor(hbuf[:, t, 0:w], hbuf[:, t, 0:w], bank(b)[:, w:2 * w], ALU.mult)\
                                .then_inc(f["h_done"], 1)
                        if t == 0 or l == 0:
                            one()
                        else:
                            with dve.If(n > t):
                                one()

                for k in range(2):
                    low(2 * k + 1, 0)
                n0 = T if l == 0 else dve.value_load(tbl[0:1, 0, 0:1], min_val=1, max_val=T)
                for t in range(T):
                    if t == 0 or l == 0:
                        for g in range(2):
                            xs_low(0, t, g, 6 + g)
                    else:
                        with dve.If(n0 > t):
                            for g in range(2):
                                xs_low(0, t, g, 6 + g)
                with dve.Fori(0, n_exp) as e:
                    if l:
                        n = dve.value_load(tbl[0:1, 0, bass.ds(e, 1)], min_val=1, max_val=T)
                        n2 = dve.value_load(tbl[0:1, 0, bass.ds(e + 1, 1)], min_val=1, max_val=T)
                        c = dve.value_load(tbl[0:1, 1, bass.ds(e, 1)], min_val=0, max_val=SLOTS)
                    else:
                        n, n2, c = T, T, e * T
                    for j in range(6):
                        if j:
                            h_low(c * 6 + n * (j - 1), n, j - 1)
                        low(4 * j + 5, e)
                        products(c * 6 + n * j, n, j)
                        low(4 * j + 7, e)
                    for m in range(12):
                        if m % 2:
                            low(28 + m, e)
                        if m == 0:
                            h_low(c * 6 + n * 5, n, 5)
                        if m >= 2:
                            t2, g = (m - 2) // 2, m % 2
                            if t2 == 0 or l == 0:
                                xs_low(c + n, t2, g, 7)
                            else:
                                with dve.If(n2 > t2):
                                    xs_low(c + n, t2, g, 7)

                n_ln = 1 + 2 * l
                dve.wait_ge(S["x_back"], 16 * (l + 1))
                for t in range(T):
                    dve.wait_ge(yg_in[t], 32 * (l + 1))
                    if l == 0:
                        rwait(dve.tensor_tensor(yA[:, t, :], yA[:, t, :], yB[:, t, :], ALU.add))
                    else:
                        rwait(dve.tensor_scalar(yA[:, t, :], yA[:, t, :], gates2[:, 0, t:t + 1], None, ALU.mult))
                        rwait(dve.scalar_tensor_tensor(yA[:, t, :], yB[:, t, :], gates2[:, 1, t:t + 1], yA[:, t, :],
                                                       ALU.mult, ALU.add))
                    dve.wait_ge(S["rows_in"], 64 * (n_ln + 1))
                    rwait(dve.tensor_tensor(yA[:, t, :], yA[:, t, :], rows[:, 1 if t else 0, :], ALU.mult))
                    rwait(dve.scalar_tensor_tensor(x[:, t, :], x[:, t, :], ALPHA, yA[:, t, :], ALU.mult, ALU.add))
                    layer_norm(n_ln, t)

            ffn(0)

            dve.wait_ge(S["rows_in"], 64 * 3)
            dve.wait_ge(S["poolrows_in"], 32)
            pb, psc = prow[:, 0, :], prow[:, 1, :]
            for t in range(T):
                y = lnt[:, t, :]
                dve.wait_ge(S["pool_ps"], t + 1)
                dve.tensor_tensor(y, PP[2 + t % 2][:, :], pb, ALU.add).then_inc(S["pool_step"], 1)
                dve.wait_ge(S["pool_step"], 5 * t + 1)
                dve.tensor_tensor(y, y, psc, ALU.mult).then_inc(S["pool_step"], 1)
                dve.wait_ge(S["pool_step"], 5 * t + 2)
                dve.tensor_tensor(y, y, rows[:, 1 if t else 0, :], ALU.mult).then_inc(S["pool_step"], 1)
                dve.wait_ge(S["pool_step"], 5 * t + 3)
                v = rstep(dve.scalar_tensor_tensor(x[:, t, :], x[:, t, :], ALPHA, y, ALU.mult, ALU.add))
                dve.wait_ge(S["res_step"], v)
                dve.sem_inc(S["pool_step"], 2)
                layer_norm(2, t)
            step = [0]

            def rts(ins):
                step[0] += 1
                ins.then_inc(S["route_step"], 1)
                dve.wait_ge(S["route_step"], step[0])

            LOG, E_, PR, MX, SUM, GTM, EQ, PRE, TA, TB, SEL, M1 = range(12)
            c8 = lambda a: a.to_broadcast([P, T, 8])
            dve.wait_ge(S["logit_ps"], 1)
            lg = bank(4)[:, 0:40].rearrange("p (t e) -> p t e", t=T)
            rts(dve.tensor_reduce(rt[:, SUM, :, 0:1], lg, AX.X, ALU.max))
            rts(dve.tensor_tensor(rt[:, E_, :, :], lg, c8(rt[:, SUM, :, 0:1]), ALU.subtract))
            dve.wait_ge(S["route_act"], 1)
            rts(dve.tensor_reduce(rt[:, SUM, :, 1:2], rt[:, E_, :, :], AX.X, ALU.add))
            rts(dve.reciprocal(rt[:, SUM, :, 2:3], rt[:, SUM, :, 1:2]))
            rts(dve.tensor_tensor(rt[:, PR, :, :], rt[:, E_, :, :], c8(rt[:, SUM, :, 2:3]), ALU.mult))
            for t in range(T):
                rts(dve.max(rt[:, MX, t, :], rt[:, PR, t, :]))
            m2 = rt[:, MX, :, 1:2]
            rts(dve.tensor_tensor(rt[:, GTM, :, :], rt[:, PR, :, :], c8(m2), ALU.is_gt))
            rts(dve.tensor_tensor(rt[:, EQ, :, :], rt[:, PR, :, :], c8(m2), ALU.is_equal))
            rts(dve.tensor_reduce(rt[:, PRE, :, 0:1], rt[:, GTM, :, :], AX.X, ALU.add))
            for e in range(7):
                rts(dve.tensor_tensor(rt[:, PRE, :, e + 1:e + 2], rt[:, PRE, :, e:e + 1], rt[:, EQ, :, e:e + 1], ALU.add))
            rts(dve.tensor_scalar(rt[:, TA, :, :], rt[:, PRE, :, :], 1.5, None, ALU.is_lt))
            rts(dve.tensor_tensor(rt[:, TA, :, :], rt[:, TA, :, :], rt[:, EQ, :, :], ALU.mult))
            rts(dve.tensor_tensor(rt[:, SEL, :, :], rt[:, TA, :, :], rt[:, GTM, :, :], ALU.add))
            assert step[0] == ROUTE_SEL, step[0]
            rts(dve.tensor_tensor(rt[:, SUM, :, 3:4], rt[:, MX, :, 0:1], m2, ALU.add))
            rts(dve.reciprocal(rt[:, SUM, :, 4:5], rt[:, SUM, :, 3:4]))
            rts(dve.tensor_tensor(rt[:, TB, :, :], rt[:, PR, :, :], c8(rt[:, SUM, :, 4:5]), ALU.mult))
            rts(dve.memset(rt[:, PRE, :, 0:1], 0.0))
            for e in range(7):
                rts(dve.tensor_tensor(rt[:, PRE, :, e + 1:e + 2], rt[:, PRE, :, e:e + 1], rt[:, SEL, :, e:e + 1], ALU.add))
            rts(dve.tensor_scalar(rt[:, M1, :, :], rt[:, PRE, :, :], 0.5, None, ALU.is_lt))
            rts(dve.tensor_tensor(rt[:, M1, :, :], rt[:, M1, :, :], rt[:, SEL, :, :], ALU.mult))
            rts(dve.tensor_tensor(rt[:, TA, :, :], rt[:, SEL, :, :], rt[:, M1, :, :], ALU.subtract))
            dve.wait_ge(S["rank_ps"], 1)
            rk = bank(5)[:, 0:80].rearrange("p (i t e) -> p i t e", i=2, t=T)
            rts(dve.memset(rt[:, EQ, 0:1, :], 0.0))
            for t in range(T - 1):
                rts(dve.tensor_tensor(rt[:, EQ, t + 1:t + 2, :], rt[:, EQ, t:t + 1, :], rk[:, 1, t:t + 1, :], ALU.add))
            rts(dve.tensor_tensor(cnt[:, 0:1, 0:8], rt[:, EQ, T - 1:T, :], rk[:, 1, T - 1:T, :], ALU.add))
            rts(dve.tensor_tensor(rt[:, EQ, :, :], rt[:, EQ, :, :], rk[:, 0, :, :], ALU.add))
            rts(dve.memset(cnt[:, 1, :], 1.0))
            for t in range(1, T):
                rts(dve.tensor_scalar(cnt[:, 2, 0:8], cnt[:, 0, 0:8], P * t + 0.5, None, ALU.is_gt))
                rts(dve.tensor_tensor(cnt[:, 1, 0:8], cnt[:, 1, 0:8], cnt[:, 2, 0:8], ALU.add))
            rts(dve.memset(cnt[:, 3, :], 0.0))
            for e in range(9):
                rts(dve.tensor_tensor(cnt[:, 3, e + 1:e + 2], cnt[:, 3, e:e + 1], cnt[:, 1, e:e + 1], ALU.add))
            rts(dve.tensor_copy(tbl[:, 0, :], cnt[:, 1, :]))
            rts(dve.tensor_copy(tbl[:, 1, :], cnt[:, 3, :]))
            rts(dve.tensor_scalar(cnt[:, 4, :], cnt[:, 3, :], float(P), None, ALU.mult))
            rts(dve.tensor_tensor(rt[:, EQ, :, :], rt[:, EQ, :, :], cnt[:, 4:5, 0:8].to_broadcast([P, T, 8]), ALU.add))
            for i, m in enumerate((M1, TA)):
                rts(dve.tensor_tensor(rt[:, GTM, :, :], rt[:, EQ, :, :], rt[:, m, :, :], ALU.mult))
                rts(dve.tensor_reduce(rt[:, SUM, :, 5:6], rt[:, GTM, :, :], AX.X, ALU.add))
                rts(dve.tensor_copy(pos[:, i, :], rt[:, SUM, :, 5]))
                rts(dve.tensor_tensor(rt[:, GTM, :, :], rt[:, TB, :, :], rt[:, m, :, :], ALU.mult))
                rts(dve.tensor_reduce(gates2[:, i, :], rt[:, GTM, :, :], AX.X, ALU.add))
            dve.sem_inc(S["tbl_ready"], 1)
            ffn(1)


_INS = ["x_prompt", "x_sample", "state_dn", "c", "c_ctx", "ada_w", "ada_b", "ln_g", "ln_b", "dn_w_in", "dn_conv",
        "dn_a_log", "dn_dt_bias", "dn_norm_g", "dn_w_out", "pool_w", "pool_b", "pool_scale", "ffn_w_gu",
        "ffn_w_down", "moe_router", "moe_w_gu", "moe_w_down"]


def kernel(**inputs):
    import numpy as _np
    import concourse.bacc as _bacc
    from concourse.bass_utils import run_bass_kernel_spmd as _run

    nc = _bacc.Bacc("TRN2", target_bir_lowering=False, num_devices=1)
    arrays, A = {}, {}
    for name in _INS:
        arrays[f"in_{name}"] = _np.ascontiguousarray(inputs[name])
        A[name] = nc.dram_tensor(f"in_{name}", arrays[f"in_{name}"].shape, F32, kind="ExternalInput").ap()
    arrays["in_consts"] = shape_constants()
    A["consts"] = nc.dram_tensor("in_consts", arrays["in_consts"].shape, F32, kind="ExternalInput").ap()
    outs = [nc.dram_tensor(n, s, F32, kind="ExternalOutput").ap()
            for n, s in (("y_prompt", (1, P, D)), ("y_sample", (1, 4 * P, D)), ("new_state", (1, 1, 2, H, P, P)))]
    scratch = [nc.dram_tensor(n, s, F32, kind="Internal").ap()
               for n, s in (("mod_rows", (2, 2, 6 * D)), ("h_rows", (NT, D)), ("expert_in", (SLOTS * P, D)),
                            ("expert_out", (SLOTS * P, D)), ("x_parked", (NT, D)))]
    backbone(nc, A, *outs, *scratch)
    r = _run(nc, [arrays], core_ids=[0]).results[0]
    return r["y_prompt"], r["y_sample"], r["new_state"]
```
